# Optimizing a Trainium2 kernel written in Bass

```python
import math
import jax
import jax.numpy as jnp
from jax import lax
import numpy as np
import jax, jax.numpy as jnp

D_MODEL = 1024
BATCH = 1
SEQ = 256
DEPTH = 2

CTX_LEN = 256
GRID_W = 64

FOURIER_WIDTH = D_MODEL // 4
FOURIER_GROUPS = 4
FOURIER_GROUP_DIM = FOURIER_WIDTH // FOURIER_GROUPS
POOL_WINDOWS = (2, 4, 8, 16)
POOL_WIDTH = D_MODEL // 4
POOL_GROUP_DIM = POOL_WIDTH // len(POOL_WINDOWS)
HEAD_DIM = 64
Q_WIDTH = D_MODEL // 2
N_HEADS = Q_WIDTH // HEAD_DIM
N_KV_HEADS = N_HEADS // 4
GQA_GROUP = N_HEADS // N_KV_HEADS
KV_WIDTH = N_KV_HEADS * HEAD_DIM
ROPE_THETA = 10000.0
ROPE_AX_FREQS = HEAD_DIM // 4
Q_BLOCK = 128
N_BRANCHES = 3
OFF_P = FOURIER_WIDTH
OFF_Q = OFF_P + POOL_WIDTH
OFF_K = OFF_Q + Q_WIDTH
OFF_V = OFF_K + KV_WIDTH
OFF_G = OFF_V + KV_WIDTH
IN_COLS = OFF_G + N_BRANCHES * D_MODEL
PEER_HEADS = 8
PEER_KEYS = 128
PEER_EXPERTS = PEER_KEYS * PEER_KEYS
PEER_TOPK = 16
PEER_KEY_DIM = 128
PEER_QDIM = 2 * PEER_KEY_DIM
PEER_CHUNK = 128
EPS = 1e-6


def rmsnorm(x, g):
    x32 = x.astype(jnp.float32)
    y = x32 * lax.rsqrt(jnp.mean(x32 * x32, axis=-1, keepdims=True) + EPS)
    return (y * g.astype(jnp.float32)).astype(x.dtype)

def modulate(h, shift, scale):
    return h * (1 + scale) + shift

def axial_rope_angles(L):
    rows = L // GRID_W
    row = jnp.repeat(jnp.arange(rows), GRID_W).astype(jnp.float32)
    col = jnp.tile(jnp.arange(GRID_W), rows).astype(jnp.float32)
    inv = ROPE_THETA ** (-jnp.arange(ROPE_AX_FREQS, dtype=jnp.float32) / ROPE_AX_FREQS)
    return row[:, None] * inv, col[:, None] * inv

def rope_rotate(x, ang):
    F = ang.shape[-1]
    cos = jnp.cos(ang)[None, :, None, :].astype(x.dtype)
    sin = jnp.sin(ang)[None, :, None, :].astype(x.dtype)
    x1, x2 = x[..., :F], x[..., F:]
    return jnp.concatenate([x1 * cos - x2 * sin, x2 * cos + x1 * sin], axis=-1)

def apply_axial_rope(x, ang_row, ang_col):
    half = HEAD_DIM // 2
    return jnp.concatenate([rope_rotate(x[..., :half], ang_row),
                            rope_rotate(x[..., half:], ang_col)], axis=-1)

def split_proj(P):
    B, L, _ = P.shape
    f = P[..., :OFF_P]
    p = P[..., OFF_P:OFF_Q]
    q = P[..., OFF_Q:OFF_K].reshape(B, L, N_HEADS, HEAD_DIM)
    k = P[..., OFF_K:OFF_V].reshape(B, L, N_KV_HEADS, HEAD_DIM)
    v = P[..., OFF_V:OFF_G].reshape(B, L, N_KV_HEADS, HEAD_DIM)
    gates = jax.nn.sigmoid(P[..., OFF_G:]).reshape(B, L, N_BRANCHES, D_MODEL)
    return f, p, q, k, v, gates

def fourier_branch(f, w):
    B, L, _ = f.shape
    fg = f.reshape(B, L, FOURIER_GROUPS, FOURIER_GROUP_DIM).astype(jnp.float32)
    re = jnp.fft.fftn(fg, axes=(1, 3), norm='ortho').real
    return re.reshape(B, L, FOURIER_WIDTH).astype(f.dtype) @ w

def pool_branch(p, w_grp, scale, w_proj):
    B, L, _ = p.shape
    n_g = len(POOL_WINDOWS)
    pg = p.reshape(B, L, n_g, POOL_GROUP_DIM)
    cs = jnp.concatenate([jnp.zeros((B, 1, n_g, POOL_GROUP_DIM), jnp.float32),
                          jnp.cumsum(pg.astype(jnp.float32), axis=1)], axis=1)
    t = jnp.arange(L)
    means = []
    for gi, win in enumerate(POOL_WINDOWS):
        lo = jnp.maximum(t - win // 2, 0)
        hi = jnp.minimum(t + win - win // 2, L)
        s = cs[:, hi, gi] - cs[:, lo, gi]
        means.append(s / (hi - lo).astype(jnp.float32)[None, :, None])
    pooled = jnp.stack(means, axis=2).astype(p.dtype) - pg
    mixed = jnp.einsum('blgc,gce->blge', pooled, w_grp).reshape(B, L, POOL_WIDTH) * scale
    return mixed @ w_proj

def attend(q, k, v):
    s = jnp.einsum('bqhgd,bkhd->bhgqk', q, k).astype(jnp.float32) * (HEAD_DIM ** -0.5)
    p = jax.nn.softmax(s, axis=-1).astype(v.dtype)
    return jnp.einsum('bhgqk,bkhd->bqhgd', p, v)

def latent_attention(q, k_all, v_all):
    B, L = q.shape[0], q.shape[1]
    nb = L // Q_BLOCK
    qb = q.reshape(B, nb, Q_BLOCK, N_KV_HEADS, GQA_GROUP, HEAD_DIM).swapaxes(0, 1)
    ob = lax.map(lambda qq: attend(qq, k_all, v_all), qb)
    return ob.swapaxes(0, 1).reshape(B, L, Q_WIDTH)

def merge(yf, yp, ya, gates, w_out):
    return (gates[:, :, 0] * yf + gates[:, :, 1] * yp + gates[:, :, 2] * ya) @ w_out

def peer(h, wq, sub_keys, u_tab, v_tab):
    B, L, D = h.shape
    xs = h.reshape(-1, PEER_CHUNK, D)

    def block(xc):
        C = xc.shape[0]
        q = (xc @ wq).reshape(C, PEER_HEADS, 2, PEER_KEY_DIM)
        s = jnp.einsum('chpd,hpnd->chpn', q, sub_keys).astype(jnp.float32)
        s1, i1 = lax.top_k(s[:, :, 0], PEER_TOPK)
        s2, i2 = lax.top_k(s[:, :, 1], PEER_TOPK)
        cand = (s1[..., :, None] + s2[..., None, :]).reshape(C, PEER_HEADS, PEER_TOPK * PEER_TOPK)
        cidx = (i1[..., :, None] * PEER_KEYS + i2[..., None, :]).reshape(C, PEER_HEADS, PEER_TOPK * PEER_TOPK)
        top, pos = lax.top_k(cand, PEER_TOPK)
        eidx = jnp.take_along_axis(cidx, pos, axis=-1)
        g = jax.nn.softmax(top, axis=-1).astype(xc.dtype)
        a = jax.nn.gelu(jnp.einsum('chkd,cd->chk', u_tab[eidx], xc))
        return jnp.einsum('chk,chkd->cd', g * a, v_tab[eidx])

    return lax.map(block, xs).reshape(B, L, D)

def first_inputs(seed: int = 0) -> dict:
    key = jax.random.key(seed)
    ks = jax.random.split(key, 24)
    f32 = jnp.float32

    def nrm(k, shape, scale):
        return jax.random.normal(k, shape, f32) * scale

    def gain(k, shape):
        return 1.0 + 0.02 * jax.random.normal(k, shape, f32)

    return {
        'x': nrm(ks[0], (BATCH, SEQ, D_MODEL), 1.0),
        'c': nrm(ks[1], (BATCH, D_MODEL), 1.0),
        'ctx': nrm(ks[2], (BATCH, CTX_LEN, D_MODEL), 1.0),
        'c_ctx': nrm(ks[3], (D_MODEL,), 1.0),
        'ada_w': nrm(ks[4], (DEPTH, D_MODEL, 6 * D_MODEL), 0.5 * D_MODEL ** -0.5),
        'ada_b': nrm(ks[5], (DEPTH, 6 * D_MODEL), 0.02),
        'norm_mix': gain(ks[6], (DEPTH, D_MODEL)),
        'w_in': nrm(ks[7], (DEPTH, D_MODEL, IN_COLS), D_MODEL ** -0.5),
        'fourier_w': nrm(ks[8], (DEPTH, FOURIER_WIDTH, D_MODEL), FOURIER_WIDTH ** -0.5),
        'pool_w': nrm(ks[9], (DEPTH, len(POOL_WINDOWS), POOL_GROUP_DIM, POOL_GROUP_DIM), POOL_GROUP_DIM ** -0.5),
        'pool_scale': gain(ks[10], (DEPTH, POOL_WIDTH)),
        'pool_proj': nrm(ks[11], (DEPTH, POOL_WIDTH, D_MODEL), POOL_WIDTH ** -0.5),
        'q_norm': gain(ks[12], (DEPTH, HEAD_DIM)),
        'k_norm': gain(ks[13], (DEPTH, HEAD_DIM)),
        'attn_proj': nrm(ks[14], (DEPTH, Q_WIDTH, D_MODEL), Q_WIDTH ** -0.5),
        'w_out': nrm(ks[15], (DEPTH, D_MODEL, D_MODEL), D_MODEL ** -0.5),
        'norm_ffn': gain(ks[16], (DEPTH, D_MODEL)),
        'peer_wq': nrm(ks[17], (DEPTH, D_MODEL, PEER_HEADS * PEER_QDIM), D_MODEL ** -0.5),
        'peer_keys': nrm(ks[18], (DEPTH, PEER_HEADS, 2, PEER_KEYS, PEER_KEY_DIM), PEER_KEY_DIM ** -0.5),
        'peer_u': nrm(ks[19], (DEPTH, PEER_EXPERTS, D_MODEL), D_MODEL ** -0.5),
        'peer_v': nrm(ks[20], (DEPTH, PEER_EXPERTS, D_MODEL), PEER_HEADS ** -0.5),
    }

def first_block(x, c, ctx, c_ctx, ada_w, ada_b, norm_mix, w_in, fourier_w, pool_w, pool_scale,
              pool_proj, q_norm, k_norm, attn_proj, w_out, norm_ffn, peer_wq, peer_keys, peer_u, peer_v):
    B, L, _ = x.shape
    ang_row, ang_col = axial_rope_angles(L)
    for l in range(DEPTH):
        last = l == DEPTH - 1
        m_lat = jnp.split((jax.nn.silu(c) @ ada_w[l] + ada_b[l])[:, None, :], 6, axis=-1)
        m_ctx = jnp.split(jax.nn.silu(c_ctx) @ ada_w[l] + ada_b[l], 6, axis=-1)

        h = modulate(rmsnorm(x, norm_mix[l]), m_lat[0], m_lat[1])
        hc = modulate(rmsnorm(ctx, norm_mix[l]), m_ctx[0], m_ctx[1])
        f, p, q, k, v, gates = split_proj(h @ w_in[l])
        fc, pc, qc, kc, vc, gates_c = split_proj(hc @ w_in[l])

        q = apply_axial_rope(rmsnorm(q, q_norm[l]), ang_row, ang_col)
        k = apply_axial_rope(rmsnorm(k, k_norm[l]), ang_row, ang_col)
        kc = rmsnorm(kc, k_norm[l])
        k_all = jnp.concatenate([k, kc], axis=1)
        v_all = jnp.concatenate([v, vc], axis=1)
        q = q.reshape(B, L, N_KV_HEADS, GQA_GROUP, HEAD_DIM)
        ya = latent_attention(q, k_all, v_all) @ attn_proj[l]
        yf = fourier_branch(f, fourier_w[l])
        yp = pool_branch(p, pool_w[l], pool_scale[l], pool_proj[l])
        x = x + m_lat[2] * merge(yf, yp, ya, gates, w_out[l])

        if not last:
            Lc = ctx.shape[1]
            qc = rmsnorm(qc, q_norm[l]).reshape(B, Lc, N_KV_HEADS, GQA_GROUP, HEAD_DIM)
            yac = attend(qc, kc, vc).reshape(B, Lc, Q_WIDTH) @ attn_proj[l]
            yfc = fourier_branch(fc, fourier_w[l])
            ypc = pool_branch(pc, pool_w[l], pool_scale[l], pool_proj[l])
            ctx = ctx + m_ctx[2] * merge(yfc, ypc, yac, gates_c, w_out[l])

        h2 = modulate(rmsnorm(x, norm_ffn[l]), m_lat[3], m_lat[4])
        x = x + m_lat[5] * peer(h2, peer_wq[l], peer_keys[l], peer_u[l], peer_v[l])
        if not last:
            hc2 = modulate(rmsnorm(ctx, norm_ffn[l]), m_ctx[3], m_ctx[4])
            ctx = ctx + m_ctx[5] * peer(hc2, peer_wq[l], peer_keys[l], peer_u[l], peer_v[l])
    return x


MIX_WIDTH = 2 * D_MODEL
BLOCK = 128
SWA_HEADS = (MIX_WIDTH // 4) // HEAD_DIM
SWA_KV_HEADS = SWA_HEADS // 4
SWA_WINDOW = 128
FOX_HEADS = (MIX_WIDTH // 4) // HEAD_DIM
SSM_HEAD_DIM = 64
SSM_HEADS = (MIX_WIDTH // 2) // SSM_HEAD_DIM
SSM_GROUPS = 2
SSM_STATE = 128
SSM_CONV = 4
SSM_CHUNK = 128
MEM_TOKENS = 256
MEM_HEADS = 4
MEM_HEAD_DIM = D_MODEL // MEM_HEADS
NEG_INF = -1e30

SWA_W = SWA_HEADS * HEAD_DIM
SWA_KV_W = SWA_KV_HEADS * HEAD_DIM
FOX_W = FOX_HEADS * HEAD_DIM
SSM_W = SSM_HEADS * SSM_HEAD_DIM
SSM_BC_W = SSM_GROUPS * SSM_STATE
SSM_CONV_W = SSM_W + 2 * SSM_BC_W
IN_SPLITS = (SWA_W, SWA_KV_W, SWA_KV_W, SWA_W,
             FOX_W, FOX_W, FOX_W, FOX_HEADS, FOX_W,
             SSM_W, SSM_CONV_W, SSM_HEADS)
IN_W = SWA_W + 2 * SWA_KV_W + SWA_W + 4 * FOX_W + FOX_HEADS + SSM_W + SSM_CONV_W + SSM_HEADS


def _offsets(sizes):
    out, acc = [], 0
    for s in sizes[:-1]:
        acc += s
        out.append(acc)
    return out

def rms_norm(x, w):
    xf = x.astype(jnp.float32)
    y = xf * lax.rsqrt(jnp.mean(xf * xf, axis=-1, keepdims=True) + EPS)
    return (y * w.astype(jnp.float32)).astype(x.dtype)

def rope_tables(seq):
    pos = jnp.arange(seq, dtype=jnp.float32)
    inv = 1.0 / (ROPE_THETA ** (jnp.arange(0, HEAD_DIM, 2, dtype=jnp.float32) / HEAD_DIM))
    ang = pos[:, None] * inv[None, :]
    return jnp.cos(ang), jnp.sin(ang)

def apply_rope(x, cos, sin):
    xf = x.astype(jnp.float32)
    x1, x2 = jnp.split(xf, 2, axis=-1)
    c = cos[None, :, None, :]
    s = sin[None, :, None, :]
    return jnp.concatenate([x1 * c - x2 * s, x2 * c + x1 * s], axis=-1).astype(x.dtype)

def sliding_window_attention(q, k, v, sinks):
    b, s, hq, hd = q.shape
    hkv = k.shape[2]
    g = hq // hkv
    n = s // BLOCK
    qb = q.reshape(b, n, BLOCK, hkv, g, hd)
    kb = k.reshape(b, n, BLOCK, hkv, hd)
    vb = v.reshape(b, n, BLOCK, hkv, hd)
    pad = ((0, 0), (1, 0), (0, 0), (0, 0), (0, 0))
    kcat = jnp.concatenate([jnp.pad(kb, pad)[:, :-1], kb], axis=2)
    vcat = jnp.concatenate([jnp.pad(vb, pad)[:, :-1], vb], axis=2)
    scores = jnp.einsum('bnqkgd,bnskd->bnkgqs', qb, kcat).astype(jnp.float32) * (hd ** -0.5)
    qi = jnp.arange(BLOCK)[:, None]
    si = jnp.arange(2 * BLOCK)[None, :] - BLOCK
    rel = qi - si
    band = (rel >= 0) & (rel < SWA_WINDOW)
    valid = (jnp.arange(n)[:, None, None] * BLOCK + si[None]) >= 0
    mask = band[None] & valid
    scores = jnp.where(mask[None, :, None, None], scores, NEG_INF)
    sink = sinks.astype(jnp.float32).reshape(hkv, g)[None, None, :, :, None, None]
    m = jnp.maximum(jnp.max(scores, axis=-1, keepdims=True), sink)
    p = jnp.exp(scores - m)
    probs = (p / (jnp.sum(p, axis=-1, keepdims=True) + jnp.exp(sink - m))).astype(v.dtype)
    out = jnp.einsum('bnkgqs,bnskd->bnqkgd', probs, vcat)
    return out.reshape(b, s, hq, hd)

def forgetting_attention(q, k, v, log_f):
    b, s, h, hd = q.shape
    n = s // BLOCK
    c = jnp.cumsum(log_f, axis=1).transpose(0, 2, 1)
    qb = q.reshape(b, n, BLOCK, h, hd).swapaxes(0, 1)
    cq = c.reshape(b, h, n, BLOCK).transpose(2, 0, 1, 3)
    kpos = jnp.arange(s)
    scale = hd ** -0.5

    def one_block(args):
        qi, ci, i = args
        logits = jnp.einsum('bqhd,bkhd->bhqk', qi, k).astype(jnp.float32) * scale
        logits = logits + ci[..., :, None] - c[:, :, None, :]
        qpos = i * BLOCK + jnp.arange(BLOCK)
        mask = kpos[None, :] <= qpos[:, None]
        logits = jnp.where(mask, logits, NEG_INF)
        probs = jax.nn.softmax(logits, axis=-1).astype(v.dtype)
        return jnp.einsum('bhqk,bkhd->bqhd', probs, v)

    out = lax.map(one_block, (qb, cq, jnp.arange(n)))
    return out.swapaxes(0, 1).reshape(b, s, h, hd)

def causal_depthwise_conv(u, w, bias):
    kw = w.astype(u.dtype)[:, None, :]
    out = lax.conv_general_dilated(u, kw, window_strides=(1,), padding=[(SSM_CONV - 1, 0)],
                                   dimension_numbers=('NWC', 'WIO', 'NWC'),
                                   feature_group_count=u.shape[-1])
    return out + bias.astype(u.dtype)

def ssd_chunked(x, dt, a, bmat, cmat):
    b, s, h, p = x.shape
    g, nst = bmat.shape[2], bmat.shape[3]
    hg = h // g
    L = SSM_CHUNK
    nc = s // L
    xs = (x.astype(jnp.float32) * dt[..., None]).reshape(b, nc, L, g, hg, p)
    acs = jnp.cumsum((dt * a.astype(jnp.float32)).reshape(b, nc, L, g, hg), axis=2)
    bm = bmat.astype(jnp.float32).reshape(b, nc, L, g, nst)
    cm = cmat.astype(jnp.float32).reshape(b, nc, L, g, nst)
    diff = acs[:, :, :, None] - acs[:, :, None, :]
    causal = jnp.tril(jnp.ones((L, L), dtype=bool))
    decay = jnp.exp(jnp.where(causal[:, :, None, None], diff, NEG_INF))
    cb = jnp.einsum('bclgn,bcsgn->bclsg', cm, bm)
    y_diag = jnp.einsum('bclsg,bclsgh,bcsghp->bclghp', cb, decay, xs)
    decay_st = jnp.exp(acs[:, :, -1:] - acs)
    states = jnp.einsum('bclgn,bclgh,bclghp->bcghpn', bm, decay_st, xs)
    chunk_decay = jnp.exp(acs[:, :, -1])

    def step(carry, inp):
        st, dec = inp
        return carry * dec[..., None, None] + st, carry

    init = jnp.zeros((b, g, hg, p, nst), jnp.float32)
    _, prev = lax.scan(step, init, (states.swapaxes(0, 1), chunk_decay.swapaxes(0, 1)))
    prev = prev.swapaxes(0, 1)
    y_off = jnp.einsum('bclgn,bcghpn,bclgh->bclghp', cm, prev, jnp.exp(acs))
    return (y_diag + y_off).reshape(b, s, h, p)

def hybrid_mixer(h, w_in, b_forget, sinks, conv_w, conv_b, dt_bias, a_log, d_skip,
                 ssm_norm_w, w_out, cos, sin):
    b, s, _ = h.shape
    proj = h @ w_in.astype(h.dtype)
    (q_a, k_a, v_a, g_a, q_b, k_b, v_b, f_b, g_b, z_c, xbc_c, dt_c) = jnp.split(
        proj, _offsets(IN_SPLITS), axis=-1)
    qa = apply_rope(q_a.reshape(b, s, SWA_HEADS, HEAD_DIM), cos, sin)
    ka = apply_rope(k_a.reshape(b, s, SWA_KV_HEADS, HEAD_DIM), cos, sin)
    va = v_a.reshape(b, s, SWA_KV_HEADS, HEAD_DIM)
    ya = sliding_window_attention(qa, ka, va, sinks).reshape(b, s, SWA_W)
    ya = ya * jax.nn.silu(g_a)
    log_f = jax.nn.log_sigmoid(f_b.astype(jnp.float32) + b_forget.astype(jnp.float32))
    yb = forgetting_attention(q_b.reshape(b, s, FOX_HEADS, HEAD_DIM),
                              k_b.reshape(b, s, FOX_HEADS, HEAD_DIM),
                              v_b.reshape(b, s, FOX_HEADS, HEAD_DIM), log_f).reshape(b, s, FOX_W)
    yb = yb * jax.nn.silu(g_b)
    xbc = jax.nn.silu(causal_depthwise_conv(xbc_c, conv_w, conv_b))
    xs, bm, cm = jnp.split(xbc, [SSM_W, SSM_W + SSM_BC_W], axis=-1)
    xs = xs.reshape(b, s, SSM_HEADS, SSM_HEAD_DIM)
    bm = bm.reshape(b, s, SSM_GROUPS, SSM_STATE)
    cm = cm.reshape(b, s, SSM_GROUPS, SSM_STATE)
    dt = jax.nn.softplus(dt_c.astype(jnp.float32) + dt_bias.astype(jnp.float32))
    a = -jnp.exp(a_log.astype(jnp.float32))
    yc = ssd_chunked(xs, dt, a, bm, cm) + d_skip.astype(jnp.float32)[:, None] * xs.astype(jnp.float32)
    yc = yc.reshape(b, s, SSM_W).astype(h.dtype)
    yc = rms_norm(yc * jax.nn.silu(z_c), ssm_norm_w)
    y = jnp.concatenate([ya, yb, yc], axis=-1)
    return y @ w_out.astype(h.dtype)

def memory_cross_attention(h, mem_n, wq, wk, wv, wo):
    b, s, _ = h.shape
    m = mem_n.shape[1]
    q = (h @ wq.astype(h.dtype)).reshape(b, s, MEM_HEADS, MEM_HEAD_DIM)
    k = (mem_n @ wk.astype(h.dtype)).reshape(b, m, MEM_HEADS, MEM_HEAD_DIM)
    v = (mem_n @ wv.astype(h.dtype)).reshape(b, m, MEM_HEADS, MEM_HEAD_DIM)
    logits = jnp.einsum('bqhd,bkhd->bhqk', q, k).astype(jnp.float32) * (MEM_HEAD_DIM ** -0.5)
    probs = jax.nn.softmax(logits, axis=-1).astype(v.dtype)
    out = jnp.einsum('bhqk,bkhd->bqhd', probs, v).reshape(b, s, D_MODEL)
    return out @ wo.astype(h.dtype)

def second_inputs(seed: int = 0) -> dict:
    key = jax.random.key(seed)
    ks = jax.random.split(key, 20)
    f32 = jnp.float32

    def nrm(k, shape, scale):
        return jax.random.normal(k, shape, f32) * scale

    dt0 = jnp.exp(jax.random.uniform(ks[7], (DEPTH, SSM_HEADS), f32, np.log(1e-3), np.log(1e-1)))
    return {
        "x": nrm(ks[0], (BATCH, SEQ, D_MODEL), 1.0),
        "mem": nrm(ks[1], (BATCH, MEM_TOKENS, D_MODEL), 1.0),
        "norm_mix_w": 1.0 + nrm(ks[2], (DEPTH, D_MODEL), 0.02),
        "w_in": nrm(ks[3], (DEPTH, D_MODEL, IN_W), D_MODEL ** -0.5),
        "b_forget": jax.random.uniform(ks[4], (DEPTH, FOX_HEADS), f32, 1.0, 6.0),
        "swa_sinks": nrm(ks[5], (DEPTH, SWA_HEADS), 0.5),
        "conv_w": nrm(ks[6], (DEPTH, SSM_CONV, SSM_CONV_W), SSM_CONV ** -0.5),
        "conv_b": nrm(ks[8], (DEPTH, SSM_CONV_W), 0.02),
        "dt_bias": dt0 + jnp.log(-jnp.expm1(-dt0)),
        "a_log": jnp.log(jax.random.uniform(ks[9], (DEPTH, SSM_HEADS), f32, 1.0, 16.0)),
        "d_skip": 1.0 + nrm(ks[10], (DEPTH, SSM_HEADS), 0.1),
        "ssm_norm_w": 1.0 + nrm(ks[11], (DEPTH, SSM_W), 0.02),
        "w_out": nrm(ks[12], (DEPTH, MIX_WIDTH, D_MODEL), MIX_WIDTH ** -0.5),
        "norm_xq_w": 1.0 + nrm(ks[13], (DEPTH, D_MODEL), 0.02),
        "norm_mem_w": 1.0 + nrm(ks[14], (DEPTH, D_MODEL), 0.02),
        "w_mq": nrm(ks[15], (DEPTH, D_MODEL, D_MODEL), D_MODEL ** -0.5),
        "w_mk": nrm(ks[16], (DEPTH, D_MODEL, D_MODEL), D_MODEL ** -0.5),
        "w_mv": nrm(ks[17], (DEPTH, D_MODEL, D_MODEL), D_MODEL ** -0.5),
        "w_mo": nrm(ks[18], (DEPTH, D_MODEL, D_MODEL), D_MODEL ** -0.5),
        "final_norm_w": 1.0 + nrm(ks[19], (D_MODEL,), 0.02),
    }

def second_block(x, mem, norm_mix_w, w_in, b_forget, swa_sinks, conv_w, conv_b, dt_bias, a_log,
              d_skip, ssm_norm_w, w_out, norm_xq_w, norm_mem_w, w_mq, w_mk, w_mv, w_mo,
              final_norm_w):
    cos, sin = rope_tables(x.shape[1])
    for l in range(DEPTH):
        h = rms_norm(x, norm_mix_w[l])
        x = x + hybrid_mixer(h, w_in[l], b_forget[l], swa_sinks[l], conv_w[l], conv_b[l],
                             dt_bias[l], a_log[l], d_skip[l], ssm_norm_w[l], w_out[l], cos, sin)
        hq = rms_norm(x, norm_xq_w[l])
        mem_n = rms_norm(mem, norm_mem_w[l])
        x = x + memory_cross_attention(hq, mem_n, w_mq[l], w_mk[l], w_mv[l], w_mo[l])
    return rms_norm(x, final_norm_w)


def setup_inputs(seed=0):
    out = dict(first_inputs(seed))
    for name, value in second_inputs(seed + 1).items():
        if name != "x":
            out[name + "_2"] = value
    return out


def reference(
    x, c, ctx, c_ctx, ada_w, ada_b, norm_mix, w_in, fourier_w, pool_w, pool_scale, pool_proj,
    q_norm, k_norm, attn_proj, w_out, norm_ffn, peer_wq, peer_keys, peer_u, peer_v, mem_2,
    norm_mix_w_2, w_in_2, b_forget_2, swa_sinks_2, conv_w_2, conv_b_2, dt_bias_2, a_log_2,
    d_skip_2, ssm_norm_w_2, w_out_2, norm_xq_w_2, norm_mem_w_2, w_mq_2, w_mk_2, w_mv_2, w_mo_2,
    final_norm_w_2,
):
    x = first_block(
        x, c, ctx, c_ctx, ada_w, ada_b, norm_mix, w_in, fourier_w, pool_w, pool_scale,
        pool_proj, q_norm, k_norm, attn_proj, w_out, norm_ffn, peer_wq, peer_keys, peer_u,
        peer_v,
    )
    return second_block(
        x, mem_2, norm_mix_w_2, w_in_2, b_forget_2, swa_sinks_2, conv_w_2, conv_b_2, dt_bias_2,
        a_log_2, d_skip_2, ssm_norm_w_2, w_out_2, norm_xq_w_2, norm_mem_w_2, w_mq_2, w_mk_2,
        w_mv_2, w_mo_2, final_norm_w_2,
    )


_drawn_inputs = setup_inputs


def setup_inputs(seed=0):
    import zlib

    import numpy as np

    out = dict(_drawn_inputs(seed))
    spreads = {}
    factors = {'ctx': 2.732,
     'norm_mix': 4.743,
     'pool_scale': 6.209,
     'q_norm': 8.0,
     'k_norm': 8.0,
     'norm_ffn': 3.415,
     'swa_sinks_2': 8.0,
     'ssm_norm_w_2': 3.658,
     'norm_xq_w_2': 8.0,
     'norm_mem_w_2': 8.0}
    for name, (base, spread) in spreads.items():
        noise = np.random.default_rng([zlib.crc32(name.encode()), seed]).standard_normal(out[name].shape)
        drawn = base * np.exp(spread * noise) if base else spread * noise
        out[name] = jnp.asarray(drawn.astype(out[name].dtype))
    for name, factor in factors.items():
        out[name] = (out[name] * factor).astype(out[name].dtype)
    return out
```

```python
from contextlib import ExitStack

import numpy as np

import concourse.bass as bass
from concourse import mybir
from concourse.alu_op_type import AluOpType as ALU

ACT = mybir.ActivationFunctionType
F32 = mybir.dt.float32
U32 = mybir.dt.uint32
AX = mybir.AxisListType.X

P = 128
DM = 1024
KD = DM // P
SEQ = 256
DEPTH = 2
HD = 64
NORM_EPS = 1e-6
MASKED = -1e30
RING = 3
SLOT = 4096
TOPK = 16
PEER_HEADS = 8
PICKS = PEER_HEADS * TOPK
EXPERTS = 128 * 128
ROWS = 8
IN_COLS = 4352
OFF_G = 1280
HALVED = 0.5
W2_TOKEN_COLS = 4360
W2_COLS = 5912


class Signal:

    def __init__(self, nc, name):
        self.sem = nc.alloc_semaphore(name)
        self.total = 0
        self.base = 0

    def one(self, by=1):
        self.total += by
        return self.sem, by

    def at(self, n):
        return self.sem, self.base + n

    def now(self):
        return self.sem, self.total


def window_mean(win):
    m = np.zeros((SEQ, SEQ), np.float64)
    for t in range(SEQ):
        lo, hi = max(t - win // 2, 0), min(t + win - win // 2, SEQ)
        m[lo:hi, t] = 1.0 / (hi - lo)
    return m - np.eye(SEQ)


def tiled(m):
    return m.reshape(2, P, -1).transpose(1, 0, 2).reshape(P, -1)


def rotary(angles, axes):
    cos, sin = np.cos(angles), np.sin(angles)
    c = np.concatenate([cos, cos], -1).reshape(SEQ, -1)
    s = np.concatenate([-sin, sin], -1).reshape(SEQ, -1)
    return c, s


def shape_constants():
    tok = np.arange(SEQ)
    common = np.concatenate([np.eye(P), np.ones((P, P)), np.tile(np.arange(16), (P, 1))], 1)
    ang = 2 * np.pi * (np.outer(tok, tok) % SEQ) / SEQ
    c_len, s_len = np.cos(ang) / np.sqrt(SEQ), np.sin(ang) / np.sqrt(SEQ)
    ch = np.arange(64)
    ang = 2 * np.pi * (np.outer(ch, ch) % 64) / 64
    two = np.eye(2)
    c_ch, s_ch = np.kron(two, np.cos(ang) / 8), np.kron(two, -np.sin(ang) / 8)
    pools = np.concatenate([tiled(window_mean(w)) for w in (2, 4, 8, 16)], 1)
    inv = (10000.0 ** (-np.arange(16, dtype=np.float32) / 16)).astype(np.float32)
    row = (tok // 64).astype(np.float32)[:, None] * inv
    col = (tok % 64).astype(np.float32)[:, None] * inv
    c1, s1 = rotary(np.stack([row, col], 1), 2)
    first = np.concatenate([tiled(c_len), tiled(s_len), c_ch, s_ch, pools, tiled(c1), tiled(s1)], 1)
    upper = (tok[:, None] <= tok[None, :]).astype(np.float64)
    rel = tok[:, None] - tok[None, :]
    band = np.where((rel >= 0) & (rel < 128), 0.0, MASKED)
    causal = np.where(rel >= 0, 0.0, MASKED)
    inv = (1.0 / (10000.0 ** (np.arange(0, 64, 2, dtype=np.float32) / 64))).astype(np.float32)
    c2, s2 = rotary((tok.astype(np.float32)[:, None] * inv)[:, None, :], 1)
    second = np.concatenate([tiled(upper), tiled(band), tiled(causal), tiled(causal.T), tiled(c2), tiled(s2)], 1)
    return [np.ascontiguousarray(a, np.float32) for a in (common, first, second)]


def build_kernel(nc, io, out, stop=None):
    ctx = ExitStack()

    def area(name, cols, dt=F32):
        return nc.alloc_sbuf_tensor(name, [P, cols], dt)[:, :]

    ring = area("ring", RING * SLOT)
    stream = area("stream", 4 * DM).rearrange("p (t d) -> p t d", t=4)
    turned = area("turned", KD * 512)
    turned_v = turned.rearrange("p (k t) -> p k t", k=KD)
    proj = area("proj", 9216)
    mixed = area("mixed", 4 * DM)
    mixed_v = mixed.rearrange("p (t d) -> p t d", t=4)
    lifted = area("lifted", 4096)
    gate_rows = area("gate_rows", 4 * DM)
    heads = area("heads", 4096)
    tables = area("tables", 3584)
    common = area("common", 272)
    columns = area("columns", 352)
    row_packs = mixed[:, 0:384].rearrange("p (a b) -> p a b", a=3)
    head_gain = area("head_gain", 256)
    small_rows = area("small_rows", 160)
    pool_blocks = area("pool_blocks", 512)
    stats = area("stats", 64)
    silu_c = area("silu_c", 32)
    mods = area("mods", 96)
    norm_cols = area("norm_cols", 64)
    soft = area("soft", 512)
    psum = nc.alloc_psum_tensor("psum", [P, 8, 512], F32)

    ident, ones, iota16 = common[:, 0:128], common[:, 128:256], common[:, 256:272]

    def signal(name):
        return Signal(nc, name)

    products = signal("products")
    read_v, read_a = signal("read_v"), signal("read_a")
    step_v, step_a, step_g = signal("step_v"), signal("step_a"), signal("step_g")
    ready_v, ready_a, ready_g = signal("ready_v"), signal("ready_a"), signal("ready_g")
    loaded = signal("loaded")
    stored = signal("stored")
    landed = [signal(f"landed{i}") for i in range(RING)]
    gathered = [signal(f"gathered{i}") for i in range(ROWS)]
    rows_used = signal("rows_used")
    staged = signal("staged")
    admitted = signal("admitted")
    every = [products, read_v, read_a, step_v, step_a, step_g, ready_v, ready_a, ready_g, loaded, stored]

    def open_stage():
        for s in every:
            s.base = s.total

    def chain(eng, step, ins):
        ins.then_inc(*step.one())
        eng.wait_ge(*step.now())

    plan = []

    def plan_block(key, w, c0, c1):
        plan.append((key, (c1 - c0), [(0, P, w[:, c0:c1].rearrange("(k p) n -> p k n", p=P))]))

    def plan_first(l):
        for b in range(12):
            plan_block(("ada", l, b), io["ada_w"][l], 512 * b, 512 * b + 512)
        for b, (c0, c1) in enumerate(((0, 512), (512, 1024), (1024, 1280))):
            plan_block(("w_in", l, b), io["w_in"][l], c0, c1)
        for cb in range(2):
            c0 = 512 * cb
            for br in range(3):
                g0 = OFF_G + br * DM + c0
                plan_block(("gate", l, cb, br), io["w_in"][l], g0, g0 + 512)
                if br < 2:
                    plan_block(("branch", l, cb, br), io["fourier_w" if br == 0 else "pool_proj"][l], c0, c0 + 512)
                else:
                    w = io["attn_proj"][l]
                    plan.append((("branch", l, cb, br), 512,
                                 [(64 * h, 64, w[256 * h:256 * h + 256, c0:c0 + 512].rearrange("(c d) n -> d c n", d=64))
                                  for h in range(2)]))
        for b in range(2):
            plan_block(("w_out", l, b), io["w_out"][l], 512 * b, 512 * b + 512)
        plan.append((("keys", l), 128, [(0, P, io["peer_keys"][l].rearrange("h s n k -> n (h s) k"))]))
        for b in range(4):
            plan_block(("wq", l, b), io["peer_wq"][l], 512 * b, 512 * b + 512)

    def plan_second(l):
        w = io["w_in_2"][l]
        for b in range(9):
            plan_block(("w_in2", l, b), w, 512 * b, min(512 * b + 512, W2_TOKEN_COLS))
        for b in range(3):
            plan_block(("conv", l, b), w, W2_TOKEN_COLS + 512 * b, W2_TOKEN_COLS + 512 * b + 512)
        plan_block(("dt", l), w, W2_COLS - 16, W2_COLS)
        for b in range(2):
            for half in range(2):
                plan_block(("w_out2", l, b, half), io["w_out_2"][l][1024 * half:1024 * half + 1024, :],
                           512 * b, 512 * b + 512)
        for name in ("w_mq_2", "w_mk_2", "w_mv_2", "w_mo_2"):
            for b in range(2):
                plan_block((name, l, b), io[name][l], 512 * b, 512 * b + 512)

    plan_first(0)
    plan_first(1)
    plan_second(0)
    plan_second(1)
    used = []
    landing = []
    for n_load, (_, _, load_parts) in enumerate(plan):
        landed[n_load % RING].one(16 * len(load_parts))
        landing.append(landed[n_load % RING].now())
    issued = [0]

    def slot_view(n):
        key, cols, parts = plan[n]
        k = parts[0][2].shape[1]
        s = n % RING
        return ring[:, s * SLOT:s * SLOT + k * cols].rearrange("p (k n) -> p k n", k=k)

    def issue_loads(sp):
        while issued[0] < min(len(plan), len(used) + RING):
            n = issued[0]
            if n >= RING:
                sp.wait_ge(products.sem, used[n - RING])
            for p0, np_, src in plan[n][2]:
                sp.dma_start(slot_view(n)[p0:p0 + np_, :, :], src).then_inc(landed[n % RING].sem, 16)
            issued[0] += 1

    def take(pe, key):
        n = len(used)
        assert plan[n][0] == key, (plan[n][0], key)
        pe.wait_ge(*landing[n])
        return slot_view(n)

    def release():
        used.append(products.total)

    def run_stage(tensor=None, vector=None, scalar=None, gpsimd=None, sync=None, drain=False):
        with nc.Block(no_gpsimd_drain=not drain) as block:
            if tensor:
                block.tensor(tensor)
            if vector:
                block.vector(vector)
            if scalar:
                block.scalar(scalar)
            if gpsimd:
                block.gpsimd(gpsimd)

            @block.sync
            def _(sp):
                if sync:
                    sync(sp)
                issue_loads(sp)

    def setup_stage():
        open_stage()
        packs = [
            [("norm_mix", 16), ("norm_ffn", 16), ("ada_b", 96)],
            [("c", 8), ("c_ctx", 8), ("norm_mix_w_2", 16), ("norm_xq_w_2", 16), ("norm_mem_w_2", 16),
             ("ssm_norm_w_2", 16), ("conv_b_2", 24), ("pool_scale", 4)],
            [("conv_w_2", 96)],
        ]
        heights = [sum(n for _, n in pack) for pack in packs]
        where = {}
        for a, pack in enumerate(packs):
            r = 0
            for name, n in pack:
                where[name] = (a * P + r, n)
                r += n

        def sync(sp):
            sp.dma_start(common, io["common"]).then_inc(*loaded.one(16))
            for a, pack in enumerate(packs):
                r = 0
                for name, n in pack:
                    src = io[name]
                    if len(src.shape) == 3:
                        src = src.rearrange("a b c -> (a b c)")
                    elif len(src.shape) == 2:
                        src = src.rearrange("a b -> (a b)")
                    sp.dma_start(row_packs[r:r + n, a, :], src.rearrange("(r q) -> r q", q=P)).then_inc(*loaded.one(16))
                    r += n
            for t in range(2):
                sp.dma_start(stream[:, t, :], io["x"][0, t * P:t * P + P, :]).then_inc(*loaded.one(16))
                sp.dma_start(stream[:, 2 + t, :], io["ctx"][0, t * P:t * P + P, :]).then_inc(*loaded.one(16))
            sp.dma_start(tables[:, 0:3584], io["first"]).then_inc(*loaded.one(16))
            for l in range(DEPTH):
                for j, name in enumerate(("q_norm", "k_norm")):
                    sp.dma_start(head_gain[:, (2 * l + j) * HD:(2 * l + j + 1) * HD],
                                 io[name][l:l + 1, :].broadcast_to([P, HD])).then_inc(*loaded.one(16))
            r = 0
            for name in ("swa_sinks_2", "b_forget_2", "dt_bias_2", "a_log_2", "d_skip_2"):
                w = io[name].shape[1]
                for l in range(DEPTH):
                    sp.dma_start(small_rows[:, r:r + w], io[name][l:l + 1, :].broadcast_to([P, w])).then_inc(*loaded.one(16))
                    r += w
            sp.wait_ge(*ready_g.at(1))
            for l in range(DEPTH):
                for g in range(4):
                    c0 = (2 * l + g // 2) * P + 64 * (g % 2)
                    sp.dma_start(pool_blocks[64 * (g % 2):64 * (g % 2) + 64, c0:c0 + 64],
                                 io["pool_w"][l, g]).then_inc(*loaded.one(16))
            sp.wait_ge(*loaded.now())

        def gpsimd(pool):
            pool.memset(pool_blocks, 0.0).then_inc(*ready_g.one())
            pool.memset(stats[:, 32:64], -0.5).then_inc(*ready_g.one())

        def vector(dve):
            dve.memset(columns, 0.0).then_inc(*step_v.one())
            dve.wait_ge(*step_v.now())
            for a, rows in enumerate(heights):
                dve.wait_ge(*products.at(a + 1))
                c0 = a * P if a < 2 else 2 * P
                chain(dve, step_v, dve.tensor_copy(columns[:, c0:c0 + rows], psum[:, a, 0:rows]))
            for name in ("conv_w_2", "conv_b_2"):
                c0, n = where[name]
                chain(dve, step_v, dve.tensor_scalar(columns[:, c0:c0 + n], columns[:, c0:c0 + n], HALVED, None, ALU.mult))

        with nc.Block() as block:
            block.sync(sync)
            loads = loaded.total

            @block.gpsimd
            def _(pool):
                gpsimd(pool)

            @block.tensor
            def _(pe):
                pe.wait_ge(loaded.sem, loads)
                for a, rows in enumerate(heights):
                    pe.transpose(psum[:, a, 0:rows], row_packs[0:rows, a, :], ident[0:rows, 0:rows]).then_inc(*products.one())

            @block.vector
            def _(dve):
                dve.memset(soft, 0.0).then_inc(rows_used.sem, ROWS)
                rows_used.total += ROWS
                vector(dve)
                dve.wait_ge(*step_a.at(1))
                c0 = where["c"][0]
                th = silu_c[:, 0:16]
                chain(dve, step_v, dve.scalar_tensor_tensor(out=th, in0=th, scalar=1.0, in1=columns[:, c0:c0 + 16],
                                                            op0=ALU.add, op1=ALU.mult))
                chain(dve, step_v, dve.tensor_scalar(
                    silu_c[:, 16:32].rearrange("p (k s) -> p s k", s=2),
                    th.rearrange("p (s k) -> p s k", s=2), HALVED, None, ALU.mult))

            @block.scalar
            def _(act):
                act.wait_ge(*step_v.at(6))
                c0 = where["c"][0]
                act.activation(silu_c[:, 0:16], columns[:, c0:c0 + 16], ACT.Tanh, scale=0.5).then_inc(*step_a.one())
        return where

    where = setup_stage()

    def column(name, j):
        return columns[:, where[name][0] + j:where[name][0] + j + 1]

    def ada_stage(l):
        open_stage()
        mods_v = mods.rearrange("p (j s) -> p j s", s=2)
        cond = silu_c[:, 16:32].rearrange("p (k s) -> p k s", s=2)
        gain1, gain2 = (norm_cols[:, 16 * i:16 * i + 16].rearrange("p (k s) -> p k s", s=2) for i in range(2))
        diag = [soft[:, 128 * i:128 * i + 128] for i in range(4)]
        gate_list = [(m, s, k) for m in (2, 5) for s in range(2) for k in range(KD)]

        def tensor(pe):
            for b in range(12):
                w = take(pe, ("ada", l, b))
                for c in range(4):
                    j = 4 * b + c
                    for k in range(KD):
                        mm = pe.matmul(psum[:, 0, 2 * j:2 * j + 2], w[:, k, c * P:c * P + P], cond[:, k, :],
                                       start=k == 0, stop=k == KD - 1)
                mm.then_inc(*products.one())
                release()
            for i, (m, s, k) in enumerate(gate_list):
                pe.wait_ge(*ready_v.at(i + 1))
                bank = 1 + (i // 4) % 7
                if i // 4 >= 7 and i % 4 == 0:
                    pe.wait_ge(*read_a.at(i // 4 - 6))
                pe.matmul(psum[:, bank, 128 * (i % 4):128 * (i % 4) + 128], ones, diag[i % 4],
                          start=True, stop=True).then_inc(*products.one())

        def vector(dve):
            dve.wait_ge(*products.at(12))
            bias = columns[:, where["ada_b"][0] + 48 * l:where["ada_b"][0] + 48 * l + 48]
            chain(dve, step_v, dve.tensor_tensor(out=mods_v, in0=psum[:, 0, 0:96].rearrange("p (j s) -> p j s", s=2),
                                                 in1=bias.unsqueeze(2).broadcast_to([P, 48, 2]), op=ALU.add))
            for gain, m, name in ((gain1, 1, "norm_mix"), (gain2, 4, "norm_ffn")):
                g = columns[:, where[name][0] + 8 * l:where[name][0] + 8 * l + 8]
                chain(dve, step_v, dve.scalar_tensor_tensor(
                    out=gain, in0=mods_v[:, 8 * m:8 * m + 8, :], scalar=1.0,
                    in1=g.unsqueeze(2).broadcast_to([P, 8, 2]), op0=ALU.add, op1=ALU.mult))
            for i, (m, s, k) in enumerate(gate_list):
                if i >= 4:
                    dve.wait_ge(*products.at(12 + i - 3))
                dve.tensor_scalar(diag[i % 4], ident, mods_v[:, 8 * m + k, s:s + 1], None, ALU.mult).then_inc(*ready_v.one())

        def scalar(act):
            for q in range(8):
                act.wait_ge(*products.at(12 + 4 * q + 4))
                act.copy(gate_rows[:, 512 * q:512 * q + 512], psum[:, 1 + q % 7, :]).then_inc(*read_a.one())

        run_stage(tensor, vector, scalar)

    def first_gain(which, k, s):
        return norm_cols[:, 16 * which + 2 * k + s:16 * which + 2 * k + s + 1]

    def first_shift(which, k, s):
        j = (0 if which == 0 else 3) * 8 + k
        return mods[:, 2 * j + s:2 * j + s + 1]

    def gate_row(which, s):
        return gate_rows[:, (2 * which + s) * DM:(2 * which + s + 1) * DM]

    def inverse_root(pool, dst, src, n):
        return pool.tensor_tensor(out=dst, in0=src, in1=stats[:, 32:32 + n], op=ALU.pow)

    def norm_stage(tiles, gain, shift):
        open_stage()
        n = len(tiles)

        def scalar(act):
            for i, t in enumerate(tiles):
                act.activation(mixed_v[:, t, :], stream[:, t, :], ACT.Square,
                               accum_out=stats[:, t:t + 1]).then_inc(*ready_a.one())
            for g in range(1, 2 * n, 2):
                act.wait_ge(*products.at(g + 1))
                for q in range(4):
                    k, t = 4 * (g % 2) + q, tiles[g // 2]
                    ins = act.activation(turned_v[:, k, t * P:t * P + P], psum[:, g % 8, q * P:q * P + P], ACT.Identity,
                                         scale=gain(k, t), bias=shift(k, t) if shift else 0.0)
                ins.then_inc(*read_a.one())

        def vector(dve):
            for i, t in enumerate(tiles):
                dve.wait_ge(*ready_a.at(i + 1))
                dve.tensor_scalar(stats[:, 8 + t:9 + t], stats[:, t:t + 1], 1.0 / DM, NORM_EPS,
                                  ALU.mult, ALU.add).then_inc(*ready_v.one())
            for i, t in enumerate(tiles):
                dve.wait_ge(*ready_g.at(i + 1))
                dve.tensor_scalar(mixed_v[:, t, :], stream[:, t, :], stats[:, 16 + t:17 + t], None,
                                  ALU.mult).then_inc(*step_v.one())
            for g in range(0, 2 * n, 2):
                dve.wait_ge(*products.at(g + 1))
                for q in range(4):
                    k, t = 4 * (g % 2) + q, tiles[g // 2]
                    ins = dve.tensor_scalar(turned_v[:, k, t * P:t * P + P], psum[:, g % 8, q * P:q * P + P],
                                            gain(k, t), shift(k, t) if shift else 0.0, ALU.mult, ALU.add)
                ins.then_inc(*read_v.one())

        def gpsimd(pool):
            for i, t in enumerate(tiles):
                pool.wait_ge(*ready_v.at(i + 1))
                inverse_root(pool, stats[:, 16 + t:17 + t], stats[:, 8 + t:9 + t], 1).then_inc(*ready_g.one())

        def tensor(pe):
            for g in range(2 * n):
                t = tiles[g // 2]
                pe.wait_ge(*step_v.at(g // 2 + 1))
                for q in range(4):
                    k = 4 * (g % 2) + q
                    mm = pe.transpose(psum[:, g % 8, q * P:q * P + P], mixed_v[:, t, k * P:k * P + P], ident)
                mm.then_inc(*products.one())

        run_stage(tensor, vector, scalar, gpsimd)

    def turn_stage(groups):
        open_stage()

        def tensor(pe):
            for g, (sources, _) in enumerate(groups):
                if g >= 8:
                    pe.wait_ge(*(read_v if g % 2 == 0 else read_a).at((g - 8) // 2 + 1))
                for q, src in enumerate(sources):
                    mm = pe.transpose(psum[:, g % 8, q * P:q * P + P], src, ident)
                mm.then_inc(*products.one())

        def vector(dve):
            for g in range(0, len(groups), 2):
                dve.wait_ge(*products.at(g + 1))
                for c0, w, dst, scale in groups[g][1]:
                    src = psum[:, g % 8, c0:c0 + w]
                    if len(dst.shape) == 3:
                        src = src.rearrange("p (a b) -> p a b", a=dst.shape[1])
                    if isinstance(scale, float):
                        ins = dve.tensor_scalar(dst, src, scale, None, ALU.mult) if scale != 1.0 else dve.tensor_copy(dst, src)
                    else:
                        ins = dve.tensor_scalar(dst, src, scale, None, ALU.mult)
                ins.then_inc(*read_v.one())

        def scalar(act):
            for g in range(1, len(groups), 2):
                act.wait_ge(*products.at(g + 1))
                for c0, w, dst, scale in groups[g][1]:
                    src = psum[:, g % 8, c0:c0 + w]
                    if len(dst.shape) == 3:
                        src = src.rearrange("p (a b) -> p a b", a=dst.shape[1])
                    ins = act.activation(dst, src, ACT.Copy, scale=scale)
                ins.then_inc(*read_a.one())

        run_stage(tensor, vector, scalar)

    def linear_stage(jobs):
        open_stage()
        groups = []
        for job in jobs:
            keys, kind, items, lhs, dst = job
            for it in items:
                adding = isinstance(dst, tuple)
                groups.append((job, it, "v" if adding or len(groups) % 2 == 0 else "a"))
        order = {"v": 0, "a": 0}
        nth = []
        for _, _, e in groups:
            order[e] += 1
            nth.append(order[e])

        def tensor(pe):
            g = 0
            for job in jobs:
                keys, kind, items, lhs, dst = job
                weights = []
                for j, key in enumerate(keys):
                    n = len(used) + j
                    assert plan[n][0] == key, (plan[n][0], key)
                    pe.wait_ge(*landing[n])
                    weights.append(slot_view(n))
                for it in items:
                    if g >= 8:
                        pe.wait_ge(*(read_v if groups[g - 8][2] == "v" else read_a).at(nth[g - 8]))
                    k_total = sum(w.shape[1] for w in weights)
                    k = 0
                    for w in weights:
                        for kk in range(w.shape[1]):
                            cols = w.shape[2]
                            if kind == "rows":
                                mm = pe.matmul(psum[:, g % 8, 0:cols], lhs(k, it), w[:, kk, :],
                                               start=k == 0, stop=k == k_total - 1)
                            else:
                                rhs = lhs(k, None)
                                mm = pe.matmul(psum[:, g % 8, 0:rhs.shape[1]], w[:, kk, it * P:it * P + P], rhs,
                                               start=k == 0, stop=k == k_total - 1)
                            k += 1
                    mm.then_inc(*products.one())
                    g += 1
                for _ in keys:
                    release()

        def out_of(g):
            (keys, kind, items, lhs, dst), it, _ = groups[g]
            return dst, it

        def vector(dve):
            for g, (job, it, e) in enumerate(groups):
                if e != "v":
                    continue
                dve.wait_ge(*products.at(g + 1))
                dst = job[4]
                if isinstance(dst, tuple):
                    _, gate, c0 = dst
                    x = stream[:, it, c0:c0 + 512]
                    if gate is None:
                        dve.tensor_tensor(out=x, in0=psum[:, g % 8, :], in1=x, op=ALU.add).then_inc(*read_v.one())
                    else:
                        tmp = heads[:, 512 * (g % 8):512 * (g % 8) + 512]
                        dve.tensor_tensor(out=tmp, in0=psum[:, g % 8, :], in1=gate(it)[:, c0:c0 + 512],
                                          op=ALU.mult).then_inc(*read_v.one())
                        dve.wait_ge(*read_v.now())
                        dve.tensor_tensor(out=x, in0=tmp, in1=x, op=ALU.add).then_inc(*step_v.one())
                else:
                    d = dst(it)
                    scale = 1.0
                    if isinstance(d, tuple):
                        d, scale = d
                    dve.tensor_scalar(d, psum[:, g % 8, 0:d.shape[1]], scale, None, ALU.mult).then_inc(*read_v.one())

        def scalar(act):
            for g, (job, it, e) in enumerate(groups):
                if e != "a":
                    continue
                act.wait_ge(*products.at(g + 1))
                d = job[4](it)
                scale = 1.0
                if isinstance(d, tuple):
                    d, scale = d
                act.activation(d, psum[:, g % 8, 0:d.shape[1]], ACT.Copy, scale=scale).then_inc(*read_a.one())

        run_stage(tensor, vector, scalar)

    def normed(k, t):
        return turned_v[:, k, t * P:t * P + P]

    proj1 = proj[:, 0:4 * 1280].rearrange("p (t n) -> p t n", t=4)
    proj2 = proj[:, 0:2 * W2_TOKEN_COLS].rearrange("p (t n) -> p t n", t=2)
    four_t = lifted[:, 0:1024].rearrange("p (c t) -> p c t", c=2)
    pool_t = lifted[:, 1024:2048].rearrange("p (c t) -> p c t", c=2)
    attn_t = lifted[:, 2048:4096].rearrange("p (c t) -> p c t", c=4)
    c_len, s_len = (tables[:, 512 * i:512 * i + 512].rearrange("p (k t) -> p k t", k=2) for i in range(2))
    c_ch, s_ch = tables[:, 1024:1152], tables[:, 1152:1280]
    pools = tables[:, 1280:3328].rearrange("p (w k t) -> p w k t", w=4, k=2)

    def branch_stage(l, streams):
        open_stage()
        units = [(s, ch) for s in streams for ch in range(2)]
        turned_f = mixed[:, 0:2048].rearrange("p (u n) -> p u n", u=4)
        pooled = mixed[:, 2048:3072].rearrange("p (u n) -> p u n", u=4)

        def tensor(pe):
            for u, (s, ch) in enumerate(units):
                for i, table in enumerate((c_len, s_len)):
                    for k in range(2):
                        mm = pe.matmul(psum[:, 2 * u, 256 * i:256 * i + 256], proj1[:, 2 * s + k, ch * P:ch * P + P],
                                       table[:, k, :], start=k == 0, stop=k == 1)
                mm.then_inc(*products.one())
                for half in range(2):
                    g = 2 * ch + half
                    for k in range(2):
                        mm = pe.matmul(psum[64 * half:64 * half + 64, 2 * u + 1, 0:256],
                                       proj1[:, 2 * s + k, 256 + 64 * g:320 + 64 * g], pools[:, g, k, :],
                                       start=k == 0, stop=k == 1)
                mm.then_inc(*products.one())
            for u, (s, ch) in enumerate(units):
                pe.wait_ge(*read_v.at(u + 1))
                pe.matmul(psum[:, 2 * u, 0:256], c_ch, turned_f[:, u, 0:256], start=True, stop=False)
                pe.matmul(psum[:, 2 * u, 0:256], s_ch, turned_f[:, u, 256:512], start=False, stop=True).then_inc(*products.one())
                pe.wait_ge(*read_a.at(u + 1))
                pe.matmul(psum[:, 2 * u + 1, 0:256], pool_blocks[:, (2 * l + ch) * P:(2 * l + ch + 1) * P], pooled[:, u, :],
                          start=True, stop=True).then_inc(*products.one())

        def vector(dve):
            for u in range(len(units)):
                dve.wait_ge(*products.at(2 * u + 1))
                dve.tensor_copy(turned_f[:, u, :], psum[:, 2 * u, :]).then_inc(*read_v.one())
            for u, (s, ch) in enumerate(units):
                dve.wait_ge(*products.at(2 * len(units) + 2 * u + 1))
                dve.tensor_copy(four_t[:, ch, s * 256:s * 256 + 256], psum[:, 2 * u, 0:256]).then_inc(*read_v.one())

        def scalar(act):
            for u in range(len(units)):
                act.wait_ge(*products.at(2 * u + 2))
                act.copy(pooled[:, u, :], psum[:, 2 * u + 1, 0:256]).then_inc(*read_a.one())
            for u, (s, ch) in enumerate(units):
                act.wait_ge(*products.at(2 * len(units) + 2 * u + 2))
                act.activation(pool_t[:, ch, s * 256:s * 256 + 256], psum[:, 2 * u + 1, 0:256], ACT.Copy,
                               scale=column("pool_scale", 2 * l + ch)).then_inc(*read_a.one())

        run_stage(tensor, vector, scalar)

    def rotate_stage(l, tiles, base, cos, sin, axes, gains):
        open_stage()
        f = HD // (2 * axes)
        work = [heads[:, 640 * i:640 * i + 640] for i in range(3)]

        def final(dve, t, a, b):
            dst = mixed_v[:, t, 0:640]
            op = ALU.add
            q = dst[:, 0:512].rearrange("p (c h d) -> p h c d", h=2, d=HD)
            chain(dve, step_v, dve.tensor_tensor(out=q, in0=a[:, 0:512].rearrange("p (h c d) -> p h c d", h=2, d=HD),
                                                 in1=b[:, 0:512].rearrange("p (h c d) -> p h c d", h=2, d=HD), op=op))
            chain(dve, step_v, dve.tensor_tensor(out=dst[:, 512:640], in0=a[:, 512:640], in1=b[:, 512:640], op=op))

        def vector(dve):
            zero = work[2]
            for i, t in enumerate(tiles):
                x = base(t)
                if gains:
                    a = work[0]
                    chain(dve, step_v, dve.tensor_tensor(out=a, in0=x, in1=x, op=ALU.mult))
                    chain(dve, step_v, dve.tensor_reduce(stats[:, 0:10], a.rearrange("p (h d) -> p h d", d=HD), AX, ALU.add))
                    dve.tensor_scalar(stats[:, 10:20], stats[:, 0:10], 1.0 / HD, NORM_EPS, ALU.mult, ALU.add)\
                       .then_inc(*ready_v.one())
                    dve.wait_ge(*ready_g.at(i + 1))
                    chain(dve, step_v, dve.tensor_tensor(
                        out=x.rearrange("p (h d) -> p h d", d=HD), in0=x.rearrange("p (h d) -> p h d", d=HD),
                        in1=stats[:, 20:30].unsqueeze(2).broadcast_to([P, 10, HD]), op=ALU.mult))
                    for h0, hn, j in ((0, 8, 0), (8, 2, 1)):
                        xs = x[:, h0 * HD:(h0 + hn) * HD].rearrange("p (h d) -> p h d", d=HD)
                        g = head_gain[:, (2 * l + j) * HD:(2 * l + j + 1) * HD]
                        chain(dve, step_v, dve.tensor_tensor(out=xs, in0=xs, in1=g.unsqueeze(1).broadcast_to([P, hn, HD]),
                                                             op=ALU.mult))
                if t < 2:
                    a, b = work[0], work[1]
                    c, s = cos[:, t, :], sin[:, t, :]
                    chain(dve, step_v, dve.tensor_tensor(
                        out=a.rearrange("p (h d) -> p h d", d=HD), in0=x.rearrange("p (h d) -> p h d", d=HD),
                        in1=c.unsqueeze(1).broadcast_to([P, 10, HD]), op=ALU.mult))
                    xv = x.rearrange("p (h a b f) -> p h a b f", h=10, a=axes, b=2)
                    bv = b.rearrange("p (h a b f) -> p h a b f", h=10, a=axes, b=2)
                    sv = s.rearrange("p (a b f) -> p a b f", a=axes, b=2)
                    for side in range(2):
                        chain(dve, step_v, dve.tensor_tensor(
                            out=bv[:, :, :, side, :], in0=xv[:, :, :, 1 - side, :],
                            in1=sv[:, :, side, :].unsqueeze(1).broadcast_to([P, 10, axes, f]), op=ALU.mult))
                    final(dve, t, a, b)
                else:
                    chain(dve, step_v, dve.memset(zero, 0.0))
                    final(dve, t, x, zero)

        def gpsimd(pool):
            if gains:
                for i in range(len(tiles)):
                    pool.wait_ge(*ready_v.at(i + 1))
                    inverse_root(pool, stats[:, 20:30], stats[:, 10:20], 10).then_inc(*ready_g.one())

        run_stage(vector=vector, gpsimd=gpsimd)

    def attention_stage(units, temps):
        open_stage()
        n = len(units)
        s_buf, p_buf, t_buf = ([temps[:, (3 * b + i) * 512:(3 * b + i + 1) * 512] for b in range(2)] for i in range(3))

        def nth_product(i, what):
            count = 0
            for r in range(n + 2):
                for w, ok in ((0, r < n), (1, 1 <= r <= n), (2, r >= 2)):
                    if ok:
                        count += 1
                        if (r - w, w) == (i, what):
                            return count

        def vector(dve):
            for i in range(n + 2):
                if i < n:
                    u = units[i]
                    keys = u["keys"]
                    dve.wait_ge(*products.at(nth_product(i, 0)))
                    src = psum[:, i % 2, 0:keys]
                    if u.get("mask") is not None:
                        dst = s_buf[i % 2][:, 0:keys]
                        if u.get("shift") is not None:
                            chain(dve, step_v, dve.scalar_tensor_tensor(out=dst, in0=src, scalar=u["shift"], in1=u["mask"],
                                                                        op0=ALU.add, op1=ALU.add))
                        else:
                            chain(dve, step_v, dve.tensor_tensor(out=dst, in0=src, in1=u["mask"], op=ALU.add))
                        src = dst
                    neg = soft[:, 4 * (i % 2):4 * (i % 2) + 1]
                    if u.get("sink") is None:
                        dve.tensor_reduce(neg, src, AX, ALU.max, negate=True).then_inc(*ready_v.one())
                    else:
                        chain(dve, step_v, dve.tensor_reduce(neg, src, AX, ALU.max, negate=False))
                        chain(dve, step_v, dve.tensor_scalar(neg, neg, u["sink"], None, ALU.max))
                        dve.tensor_scalar(neg, neg, -1.0, None, ALU.mult).then_inc(*ready_v.one())
                if 1 <= i <= n:
                    j = i - 1
                    u = units[j]
                    keys = u["keys"]
                    total, inv = soft[:, 4 * (j % 2) + 1:4 * (j % 2) + 2], soft[:, 4 * (j % 2) + 3:4 * (j % 2) + 4]
                    dve.wait_ge(*ready_a.at(2 * j + 2))
                    if u.get("sink") is not None:
                        chain(dve, step_v, dve.tensor_tensor(out=total, in0=total, in1=soft[:, 4 * (j % 2) + 2:4 * (j % 2) + 3],
                                                             op=ALU.add))
                    chain(dve, step_v, dve.reciprocal(inv, total))
                    dve.tensor_scalar(p_buf[j % 2][:, 0:keys], p_buf[j % 2][:, 0:keys], inv, None,
                                      ALU.mult).then_inc(*ready_v.one())
                if i >= 2:
                    u = units[i - 2]
                    dve.wait_ge(*products.at(nth_product(i - 2, 2)))
                    for mk in u["outputs"]:
                        ins = dve.tensor_copy(mk["dst"], psum[mk["p0"]:mk["p0"] + mk["np"], 4 + (i - 2) % 2,
                                                              mk["c0"]:mk["c0"] + mk["w"]])
                    ins.then_inc(*read_v.one())

        def scalar(act):
            for i in range(n + 1):
                if i < n:
                    u = units[i]
                    keys = u["keys"]
                    act.wait_ge(*ready_v.at(vector_ready(i)))
                    if i >= 2:
                        act.wait_ge(*products.at(nth_product(i - 2, 1)))
                    src = psum[:, i % 2, 0:keys] if u.get("mask") is None else s_buf[i % 2][:, 0:keys]
                    neg = soft[:, 4 * (i % 2):4 * (i % 2) + 1]
                    act.activation(p_buf[i % 2][:, 0:keys], src, ACT.Exp, bias=neg,
                                   accum_out=soft[:, 4 * (i % 2) + 1:4 * (i % 2) + 2]).then_inc(*ready_a.one())
                    sink = u.get("sink") if u.get("sink") is not None else neg
                    act.activation(soft[:, 4 * (i % 2) + 2:4 * (i % 2) + 3], sink, ACT.Exp, bias=neg).then_inc(*ready_a.one())
                if i >= 1:
                    keys = units[i - 1]["keys"]
                    act.wait_ge(*products.at(nth_product(i - 1, 1)))
                    if i >= 3:
                        act.wait_ge(*products.at(nth_product(i - 3, 2)))
                    act.copy(t_buf[(i - 1) % 2][:, 0:keys], psum[:, 2 + (i - 1) % 2, 0:keys]).then_inc(*read_a.one())

        def vector_ready(i):
            return 1 if i == 0 else 2 * i

        def divided(j):
            return 2 * j + 3 if j < n - 1 else 2 * n

        def tensor(pe):
            for i in range(n + 2):
                if i < n:
                    u = units[i]
                    if i >= 2:
                        pe.wait_ge(*ready_a.at(2 * (i - 2) + 1))
                    for j, (a, b) in enumerate(u["scores"]):
                        mm = pe.matmul(psum[:, i % 2, 0:u["keys"]], a, b, start=j == 0, stop=j == len(u["scores"]) - 1)
                    mm.then_inc(*products.one())
                if 1 <= i <= n:
                    u = units[i - 1]
                    pe.wait_ge(*ready_v.at(divided(i - 1)))
                    if i >= 3:
                        pe.wait_ge(*read_a.at(i - 2))
                    for k in range(u["keys"] // P):
                        mm = pe.transpose(psum[:, 2 + (i - 1) % 2, k * P:k * P + P],
                                          p_buf[(i - 1) % 2][:, k * P:k * P + P], ident)
                    mm.then_inc(*products.one())
                if i >= 2:
                    u = units[i - 2]
                    pe.wait_ge(*read_a.at(i - 1))
                    if i >= 4:
                        pe.wait_ge(*read_v.at(i - 3))
                    for mk in u["outputs"]:
                        kt = u["keys"] // P
                        for k in range(kt):
                            probs = t_buf[(i - 2) % 2][:, k * P:k * P + P]
                            v = mk["values"](k)
                            o = psum[mk["p0"]:mk["p0"] + mk["np"], 4 + (i - 2) % 2, mk["c0"]:mk["c0"] + mk["w"]]
                            a, b = (v, probs) if mk["turned"] else (probs, v)
                            mm = pe.matmul(o, a, b, start=k == 0, stop=k == kt - 1)
                    mm.then_inc(*products.one())

        run_stage(tensor, vector, scalar)

    def merge_stage(l, tiles):
        open_stage()
        units = [(cb, br, t) for cb in range(2) for br in range(3) for t in tiles]
        sources = (four_t, pool_t, attn_t)
        tanh = [heads[:, 512 * i:512 * i + 512] for i in range(2)]
        tmp = heads[:, 1024:1536]

        def tensor(pe):
            q = 0
            for cb in range(2):
                for br in range(3):
                    n = len(used)
                    assert plan[n][0] == ("gate", l, cb, br) and plan[n + 1][0] == ("branch", l, cb, br)
                    pe.wait_ge(*landing[n])
                    pe.wait_ge(*landing[n + 1])
                    wg, wb = slot_view(n), slot_view(n + 1)
                    for t in tiles:
                        if q >= 4:
                            pe.wait_ge(*read_v.at(q - 3))
                        for k in range(KD):
                            mm = pe.matmul(psum[:, 2 * (q % 4), :], normed(k, t), wg[:, k, :], start=k == 0, stop=k == KD - 1)
                        mm.then_inc(*products.one())
                        src = sources[br]
                        for k in range(src.shape[1]):
                            mm = pe.matmul(psum[:, 2 * (q % 4) + 1, :], src[:, k, t * P:t * P + P], wb[:, k, :],
                                           start=k == 0, stop=k == src.shape[1] - 1)
                        mm.then_inc(*products.one())
                        q += 1
                    release()
                    release()

        def scalar(act):
            for q in range(len(units)):
                act.wait_ge(*products.at(2 * q + 1))
                if q >= 2:
                    act.wait_ge(*read_v.at(q - 1))
                act.activation(tanh[q % 2], psum[:, 2 * (q % 4), :], ACT.Tanh, scale=0.5).then_inc(*read_a.one())

        def vector(dve):
            for q, (cb, br, t) in enumerate(units):
                dve.wait_ge(*read_a.at(q + 1))
                dve.wait_ge(*products.at(2 * q + 2))
                acc = mixed_v[:, t, 512 * cb:512 * cb + 512]
                dst = acc if br == 0 else tmp
                dve.scalar_tensor_tensor(out=dst, in0=tanh[q % 2], scalar=1.0, in1=psum[:, 2 * (q % 4) + 1, :],
                                         op0=ALU.add, op1=ALU.mult).then_inc(*read_v.one())
                dve.wait_ge(*read_v.now())
                if br:
                    chain(dve, step_v, dve.tensor_tensor(out=acc, in0=acc, in1=tmp, op=ALU.add))

        run_stage(tensor, vector, scalar)

    def turn_mixed(tiles, scale):
        turn_stage([([mixed_v[:, t, (4 * g + q) * P:(4 * g + q + 1) * P] for q in range(4)],
                     [(0, 512, turned_v[:, 4 * g:4 * g + 4, t * P:t * P + P], scale)])
                    for t in tiles for g in range(2)])

    def turn_back(tiles):
        turn_stage([([turned_v[:, 4 * g + q, t * P:t * P + P] for q in range(4)],
                     [(0, 512, mixed_v[:, t, 512 * g:512 * g + 512], 1.0)])
                    for t in tiles for g in range(2)])

    sims = proj[:, 0:8192].rearrange("p (t h n) -> p t h n", t=4, h=16)
    picks_u = area("picks_u", 4 * PICKS, U32).rearrange("p (t j) -> p t j", t=4)
    probs_g = area("probs_g", 4 * PICKS).rearrange("p (t j) -> p t j", t=4)

    def keys_stage(l, tiles):
        open_stage()
        n_tok = P * len(tiles)
        keys_t = lifted[:, 0:2048]
        qt = [heads[:, 512 * i:512 * i + n_tok] for i in range(4)]
        nt = len(tiles)

        def tensor(pe):
            w = take(pe, ("keys", l))
            for g in range(4):
                for q in range(4):
                    mm = pe.transpose(psum[:, g, q * P:q * P + P], w[:, 4 * g + q, :], ident)
                mm.then_inc(*products.one())
            release()
            for h in range(16):
                if h % 4 == 0:
                    w = take(pe, ("wq", l, h // 4))
                pe.wait_ge(*read_v.at(max(4, 4 + h - 3)))
                for k in range(KD):
                    mm = pe.matmul(psum[:, h % 4, 0:n_tok], w[:, k, (h % 4) * P:(h % 4) * P + P], turned_v[:, k, 0:n_tok],
                                   start=k == 0, stop=k == KD - 1)
                mm.then_inc(*products.one())
                if h % 4 == 3:
                    release()
                if h >= 1:
                    dot(pe, h - 1)
            dot(pe, 15)

        def dot(pe, h):
            pe.wait_ge(*read_v.at(4 + h + 1))
            if h >= 4:
                pe.wait_ge(*read_a.at(h - 3))
            for i, t in enumerate(tiles):
                mm = pe.matmul(psum[:, 4 + h % 4, i * P:i * P + P], qt[h % 4][:, i * P:i * P + P],
                               keys_t[:, h * P:h * P + P], start=True, stop=True)
            mm.then_inc(*products.one())

        def vector(dve):
            for g in range(4):
                dve.wait_ge(*products.at(g + 1))
                dve.tensor_copy(keys_t[:, 512 * g:512 * g + 512], psum[:, g, :]).then_inc(*read_v.one())
            for h in range(16):
                dve.wait_ge(*products.at(4 + (1 if h == 0 else 2 * h)))
                if h >= 4:
                    dve.wait_ge(*products.at(4 + dots_at(h - 4)))
                dve.tensor_copy(qt[h % 4], psum[:, h % 4, 0:n_tok]).then_inc(*read_v.one())

        def dots_at(h):
            return 2 * h + 3 if h < 15 else 32

        def scalar(act):
            for h in range(16):
                act.wait_ge(*products.at(4 + dots_at(h)))
                act.copy(sims[:, 0:nt, h, :], psum[:, 4 + h % 4, 0:n_tok].rearrange("p (t n) -> p t n", t=nt))\
                   .then_inc(*read_a.one())

        run_stage(tensor, vector, scalar)

    def topk_stage(tiles):
        open_stage()
        best = heads[:, 0:256].rearrange("p (h k) -> p h k", h=16)
        best_u = heads[:, 256:512].bitcast(U32).rearrange("p (h k) -> p h k", h=16)
        best_i = heads[:, 512:768].rearrange("p (h k) -> p h k", h=16)
        cand = heads[:, 768:1024]
        pos_u = heads[:, 1024:1152].bitcast(U32)
        side_u = heads[:, 1152:1280].bitcast(U32)
        side_f = heads[:, 1280:1408]
        gathered_i = [heads[:, 1408:1536], heads[:, 1536:1664]]
        hot = lifted[:, 2048:4096]
        top = heads[:, 1664:1792]
        spare = heads[:, 1792:1920]

        def step(dve, ins):
            chain(dve, step_v, ins)

        def sixteen(dve, values, indices, src):
            step(dve, dve.max(values[:, 0:8], src))
            step(dve, dve.max_index(indices[:, 0:8], values[:, 0:8], src))
            step(dve, dve.match_replace(src, values[:, 0:8], src, -3e38))
            step(dve, dve.max(values[:, 8:16], src))
            step(dve, dve.max_index(indices[:, 8:16], values[:, 8:16], src))

        def vector(dve):
            for i, t in enumerate(tiles):
                for h in range(16):
                    sixteen(dve, best[:, h, :], best_u[:, h, :], sims[:, t, h, :])
                step(dve, dve.tensor_copy(best_i, best_u))
                for h in range(PEER_HEADS):
                    a = best[:, 2 * h, :].unsqueeze(2).broadcast_to([P, 16, 16])
                    b = best[:, 2 * h + 1, :].unsqueeze(1).broadcast_to([P, 16, 16])
                    step(dve, dve.tensor_tensor(out=cand.rearrange("p (a b) -> p a b", a=16), in0=a, in1=b, op=ALU.add))
                    sixteen(dve, top[:, 16 * h:16 * h + 16], pos_u[:, 16 * h:16 * h + 16], cand)
                for side in range(2):
                    if side == 0:
                        step(dve, dve.tensor_scalar(side_u, pos_u, 4, None, ALU.logical_shift_right))
                    else:
                        step(dve, dve.tensor_scalar(side_u, pos_u, 15, None, ALU.bitwise_and))
                    step(dve, dve.tensor_copy(side_f, side_u))
                    eq = hot.rearrange("p (j r) -> p j r", r=16)
                    step(dve, dve.tensor_tensor(out=eq, in0=side_f.unsqueeze(2).broadcast_to([P, PICKS, 16]),
                                                in1=iota16.unsqueeze(1).broadcast_to([P, PICKS, 16]), op=ALU.is_equal))
                    eq4 = hot.rearrange("p (h j r) -> p h j r", h=PEER_HEADS, r=16)
                    keys = best_i.rearrange("p (h s) k -> p h s k", s=2)[:, :, side, :]
                    step(dve, dve.tensor_tensor(out=eq4, in0=eq4, in1=keys.unsqueeze(2).broadcast_to([P, PEER_HEADS, TOPK, 16]),
                                                op=ALU.mult))
                    step(dve, dve.tensor_reduce(gathered_i[side], eq, AX, ALU.add))
                step(dve, dve.scalar_tensor_tensor(out=side_f, in0=gathered_i[0], scalar=128.0, in1=gathered_i[1],
                                                   op0=ALU.mult, op1=ALU.add))
                if layer_offset[0]:
                    step(dve, dve.tensor_scalar(side_f, side_f, float(layer_offset[0]), None, ALU.add))
                step(dve, dve.tensor_copy(picks_u[:, t, :], side_f))
                tv = top.rearrange("p (h k) -> p h k", k=TOPK)
                step(dve, dve.tensor_reduce(spare[:, 0:8], tv, AX, ALU.max))
                dve.tensor_tensor(out=tv, in0=tv, in1=spare[:, 0:8].unsqueeze(2).broadcast_to([P, 8, TOPK]),
                                  op=ALU.subtract).then_inc(*ready_v.one())
                dve.wait_ge(*ready_a.at(i + 1))
                gv = probs_g[:, t, :].rearrange("p (h k) -> p h k", k=TOPK)
                step(dve, dve.tensor_reduce(spare[:, 8:16], gv, AX, ALU.add))
                step(dve, dve.reciprocal(spare[:, 16:24], spare[:, 8:16]))
                step(dve, dve.tensor_tensor(out=gv, in0=gv, in1=spare[:, 16:24].unsqueeze(2).broadcast_to([P, 8, TOPK]),
                                            op=ALU.mult))

        def scalar(act):
            for i, t in enumerate(tiles):
                act.wait_ge(*ready_v.at(i + 1))
                act.activation(probs_g[:, t, :], top, ACT.Exp).then_inc(*ready_a.one())

        run_stage(vector=vector, scalar=scalar)

    layer_offset = [0]
    row_ring = proj[:, 0:ROWS * DM].rearrange("p (r d) -> p r d", r=ROWS)
    index_stage = area("index_stage", 16, U32)
    dots = area("dots", PICKS)

    def experts_stage(l, tiles):
        open_stage()
        sums = [heads[:, 0:1024], heads[:, 1024:2048]]
        cube, arg = lifted[:, 0:128], lifted[:, 128:256]
        base0 = rows_used.total
        stage0 = staged.total
        tables_dram = [io[n].rearrange("l n d -> (l n) d") for n in ("peer_u", "peer_v")]
        phases = [(t, which) for t in tiles for which in range(2)]
        rounds = PICKS // 16

        def gpsimd(pool):
            for ph, (t, which) in enumerate(phases):
                rows0 = base0 + ph * PICKS
                with pool.Fori(0, rounds) as i:
                    for half in range(2):
                        pool.wait_ge(rows_used.sem, i * 16 + (rows0 + 8 * half - ROWS + 1))
                        pool.tensor_copy(index_stage[:, 8 * half:8 * half + 8],
                                         picks_u[:, t, bass.ds(i * 16 + 8 * half, 8)]).then_inc(staged.sem, 1)
                        for u in range(ROWS):
                            if u == 0:
                                pool.wait_ge(staged.sem, i * 2 + (stage0 + ph * 2 * rounds + half + 1))
                            pool.wait_ge(rows_used.sem, i * 16 + (rows0 + 8 * half + u - ROWS + 1))
                            pool.sem_inc(*admitted.one())
                            pool.indirect_dma_start(
                                out=row_ring[:, u, :], out_offset=None, in_=tables_dram[which],
                                in_offset=bass.IndirectOffsetOnAxis(ap=index_stage[:, 8 * half + u:8 * half + u + 1], axis=0),
                            ).then_inc(gathered[u].sem, 16)

        def vector(dve):
            for ph, (t, which) in enumerate(phases):
                rows0 = base0 + ph * PICKS
                turns0 = (base0 - ROWS) // ROWS + ph * PICKS // ROWS
                if which == 1:
                    chain(dve, step_v, dve.tensor_tensor(out=cube, in0=dots, in1=dots, op=ALU.mult))
                    chain(dve, step_v, dve.tensor_scalar(cube, cube, 0.044715, 1.0, ALU.mult, ALU.add))
                    dve.tensor_tensor(out=arg, in0=cube, in1=dots, op=ALU.mult).then_inc(*ready_v.one())
                    dve.wait_ge(*ready_a.at(ph // 2 + 1))
                    chain(dve, step_v, dve.scalar_tensor_tensor(out=cube, in0=arg, scalar=1.0, in1=dots, op0=ALU.add, op1=ALU.mult))
                    chain(dve, step_v, dve.scalar_tensor_tensor(out=dots, in0=cube, scalar=HALVED, in1=probs_g[:, t, :],
                                                                op0=ALU.mult, op1=ALU.mult))
                    chain(dve, step_v, dve.memset(heads[:, 0:2048], 0.0))
                with dve.Fori(0, PICKS // ROWS) as i:
                    for u in range(ROWS):
                        dve.wait_ge(gathered[u].sem, i * 16 + 16 * (turns0 + 1))
                        weight = dots[:, bass.ds(i * ROWS + u, 1)]
                        if which == 0:
                            dve.scalar_tensor_tensor(out=row_ring[:, u, :], in0=row_ring[:, u, :], scalar=1.0, in1=mixed_v[:, t, :],
                                                     op0=ALU.mult, op1=ALU.mult, accum_out=weight).then_inc(rows_used.sem, 1)
                        else:
                            if u >= 2:
                                dve.wait_ge(rows_used.sem, i * ROWS + (rows0 + u - 1))
                            elif u < 2:
                                dve.wait_ge(rows_used.sem, i * ROWS + (rows0 + u - 1))
                            dve.scalar_tensor_tensor(out=sums[u % 2], in0=row_ring[:, u, :], scalar=weight, in1=sums[u % 2],
                                                     op0=ALU.mult, op1=ALU.add).then_inc(rows_used.sem, 1)
                dve.wait_ge(rows_used.sem, rows0 + PICKS)
                if which == 1:
                    chain(dve, step_v, dve.tensor_tensor(out=sums[0], in0=sums[0], in1=sums[1], op=ALU.add))
                    chain(dve, step_v, dve.tensor_tensor(out=sums[0], in0=sums[0], in1=gate_row(1, t // 2), op=ALU.mult))
                    chain(dve, step_v, dve.tensor_tensor(out=stream[:, t, :], in0=stream[:, t, :], in1=sums[0], op=ALU.add))

        def scalar(act):
            for i in range(len(tiles)):
                act.wait_ge(*ready_v.at(i + 1))
                act.activation(arg, arg, ACT.Tanh, scale=float(np.sqrt(2 / np.pi))).then_inc(*ready_a.one())

        run_stage(vector=vector, scalar=scalar, gpsimd=gpsimd, drain=True)
        rows_used.total += PICKS * len(phases)
        staged.total += 2 * rounds * len(phases)

    def first_attention(tiles):
        q_t = heads[:, 0:2048].rearrange("p (c t) -> p c t", c=4)
        k_t = heads[:, 2048:2560]
        groups = []
        for t in range(4):
            if t in tiles:
                groups.append(([mixed_v[:, t, c * P:c * P + P] for c in range(4)],
                               [(0, 512, q_t[:, :, t * P:t * P + P], HD ** -0.5)]))
            groups.append(([mixed_v[:, t, 512:640]], [(0, 128, k_t[:, t * P:t * P + P], 1.0)]))
        turn_stage(groups)
        units = []
        for t in tiles:
            k0 = 0 if t < 2 else 2
            for half in range(2):
                for c in range(4):
                    rows = slice(64 * half, 64 * half + 64)
                    units.append(dict(
                        keys=P * (4 - k0), scores=[(q_t[rows, c, t * P:t * P + P], k_t[rows, k0 * P:512])],
                        outputs=[dict(values=lambda k, half=half, k0=k0: proj1[:, k0 + k, 1152 + 64 * half:1216 + 64 * half],
                                      p0=64 * half, np=64, c0=0, w=128, turned=True,
                                      dst=attn_t[rows, c, t * P:t * P + P])]))
        attention_stage(units, proj[:, 5120:8192])

    cos1 = tables[:, 3328:3456].rearrange("p (t d) -> p t d", t=2)
    sin1 = tables[:, 3456:3584].rearrange("p (t d) -> p t d", t=2)

    def first_layer(l):
        last = l == DEPTH - 1
        tiles = [0, 1] if last else [0, 1, 2, 3]
        ada_stage(l)
        norm_stage([0, 1, 2, 3], lambda k, t: first_gain(0, k, t // 2), lambda k, t: first_shift(0, k, t // 2))
        linear_stage([([("w_in", l, b)], "rows", tiles if b < 2 else [0, 1, 2, 3], normed,
                       lambda t, b=b: proj1[:, t, 512 * b:min(512 * b + 512, 1280)]) for b in range(3)])
        branch_stage(l, [0] if last else [0, 1])
        if last:
            zero_stage(proj1[:, 2:4, 0:1024])
        rotate_stage(l, [0, 1, 2, 3], lambda t: proj1[:, t, 512:1152], cos1, sin1, 2, True)
        first_attention(tiles)
        merge_stage(l, tiles)
        turn_mixed(tiles, HALVED)
        linear_stage([([("w_out", l, b)], "rows", tiles, normed, ("add", lambda t: gate_row(0, t // 2), 512 * b))
                      for b in range(2)])
        norm_stage(tiles, lambda k, t: first_gain(1, k, t // 2), lambda k, t: first_shift(1, k, t // 2))
        turn_back(tiles)
        keys_stage(l, tiles)
        layer_offset[0] = l * EXPERTS
        topk_stage(tiles)
        experts_stage(l, tiles)

    def zero_stage(dst):
        open_stage()

        def vector(dve):
            chain(dve, step_v, dve.memset(dst, 0.0))

        run_stage(vector=vector)

    upper = tables[:, 0:512].rearrange("p (k t) -> p k t", k=2)
    band = tables[:, 512:1024].rearrange("p (t k) -> p t k", t=2)
    causal = tables[:, 1024:1536].rearrange("p (t k) -> p t k", t=2)
    causal_t = tables[:, 1536:2048].rearrange("p (t k) -> p t k", t=2)
    cos2 = tables[:, 2048:2176].rearrange("p (t d) -> p t d", t=2)
    sin2 = tables[:, 2176:2304].rearrange("p (t d) -> p t d", t=2)
    sinks = [small_rows[:, 8 * l:8 * l + 8] for l in range(2)]
    forget_bias = [small_rows[:, 16 + 8 * l:24 + 8 * l] for l in range(2)]
    dt_bias = [small_rows[:, 32 + 16 * l:48 + 16 * l] for l in range(2)]
    a_log = [small_rows[:, 64 + 16 * l:80 + 16 * l] for l in range(2)]
    d_skip = [small_rows[:, 96 + 16 * l:112 + 16 * l] for l in range(2)]
    raw_conv = gate_rows[:, 0:12 * 259].rearrange("p (c t) -> p c t", c=12)
    conv = lifted[:, 0:3072].rearrange("p (c t) -> p c t", c=12)
    dt_raw = soft[:, 16:48].rearrange("p (t h) -> p t h", t=2)
    softened = soft[:, 48:96].rearrange("p (t h) -> p t h", t=2)
    cum_f = soft[:, 96:112].rearrange("p (t h) -> p t h", t=2)
    decays = soft[:, 112:144].rearrange("p (t h) -> p t h", t=2)
    neg_acs = soft[:, 144:176].rearrange("p (t h) -> p t h", t=2)
    y_v = mixed.rearrange("p (t d) -> p t d", t=2)

    def load_second_stage():
        open_stage()

        def sync(sp):
            sp.dma_start(tables[:, 0:2304], io["second"]).then_inc(*loaded.one(16))
            for t in range(2):
                sp.dma_start(stream[:, 2 + t, :], io["mem_2"][0, t * P:t * P + P, :]).then_inc(*loaded.one(16))
            sp.wait_ge(*loaded.now())

        run_stage(sync=sync)

    def softplus_stage(l):
        open_stage()
        z = soft[:, 176:224].rearrange("p (t h) -> p t h", t=2)
        e, r, s, acc = (soft[:, 224 + 48 * i:272 + 48 * i].rearrange("p (t h) -> p t h", t=2) for i in range(4))
        a_row = soft[:, 416:432]

        def bc(v, n):
            return v.unsqueeze(1).broadcast_to([P, 2, n])

        def vector(dve):
            def step(ins):
                chain(dve, step_v, ins)
            dve.wait_ge(*ready_a.at(1))
            step(dve.tensor_scalar(a_row, a_row, -1.0, None, ALU.mult))
            step(dve.tensor_tensor(out=z[:, :, 0:8], in0=proj2[:, :, 2816:2824], in1=bc(forget_bias[l], 8), op=ALU.add))
            step(dve.tensor_scalar(z[:, :, 0:8], z[:, :, 0:8], -1.0, None, ALU.mult))
            step(dve.tensor_tensor(out=z[:, :, 8:24], in0=dt_raw, in1=bc(dt_bias[l], 16), op=ALU.add))
            step(dve.tensor_scalar(r, z, -1.0, None, ALU.mult))
            dve.tensor_tensor(out=e, in0=z, in1=r, op=ALU.min).then_inc(*ready_v.one())
            dve.wait_ge(*ready_a.at(2))
            step(dve.tensor_scalar(r, e, 2.0, None, ALU.add))
            step(dve.reciprocal(s, r))
            step(dve.tensor_tensor(out=r, in0=e, in1=s, op=ALU.mult))
            step(dve.tensor_tensor(out=s, in0=r, in1=r, op=ALU.mult))
            step(dve.tensor_scalar(acc, s, 1.0 / 19, None, ALU.mult))
            for odd in (17, 15, 13, 11, 9, 7, 5, 3):
                step(dve.scalar_tensor_tensor(out=acc, in0=acc, scalar=1.0 / odd, in1=s, op0=ALU.add, op1=ALU.mult))
            step(dve.scalar_tensor_tensor(out=acc, in0=acc, scalar=1.0, in1=r, op0=ALU.add, op1=ALU.mult))
            step(dve.tensor_scalar(acc, acc, 2.0, None, ALU.mult))
            step(dve.scalar_tensor_tensor(out=softened, in0=z, scalar=0.0, in1=acc, op0=ALU.max, op1=ALU.add))
            step(dve.tensor_scalar(z[:, :, 0:8], softened[:, :, 0:8], -1.0, None, ALU.mult))
            dve.tensor_tensor(out=decays, in0=softened[:, :, 8:24], in1=bc(a_row, 16), op=ALU.mult).then_inc(*ready_v.one())
            dve.wait_ge(*products.at(1))
            step(dve.tensor_copy(cum_f, psum[:, 0, 0:16].rearrange("p (t h) -> p t h", t=2)))
            step(dve.tensor_scalar(neg_acs, psum[:, 1, 0:32].rearrange("p (t h) -> p t h", t=2), -1.0, None, ALU.mult))

        def scalar(act):
            act.activation(a_row, a_log[l], ACT.Exp).then_inc(*ready_a.one())
            act.wait_ge(*ready_v.at(1))
            act.activation(e, e, ACT.Exp).then_inc(*ready_a.one())

        def tensor(pe):
            pe.wait_ge(*ready_v.at(2))
            for bank, src, n in ((0, z[:, :, 0:8], 8), (1, decays, 16)):
                for t in range(2):
                    for k in range(2):
                        mm = pe.matmul(psum[:, bank, n * t:n * t + n], upper[:, k, t * P:t * P + P], src[:, k, :],
                                       start=k == 0, stop=k == 1)
            mm.then_inc(*products.one())

        run_stage(tensor, vector, scalar)

    def second_attention(l):
        qa_t = heads[:, 0:1024].rearrange("p (c t) -> p c t", c=4)
        ka_t = heads[:, 1024:1280]
        qb_t = heads[:, 1280:2304].rearrange("p (c t) -> p c t", c=4)
        kb_t = heads[:, 2304:3328].rearrange("p (c t) -> p c t", c=4)
        groups = []
        for t in range(2):
            span = slice(t * P, t * P + P)
            groups.append(([mixed_v[:, t, c * P:c * P + P] for c in range(4)], [(0, 512, qa_t[:, :, span], HD ** -0.5)]))
            groups.append(([mixed_v[:, t, 512:640]], [(0, 128, ka_t[:, span], 1.0)]))
            groups.append(([proj2[:, t, 1280 + c * P:1408 + c * P] for c in range(4)], [(0, 512, qb_t[:, :, span], HD ** -0.5)]))
            groups.append(([proj2[:, t, 1792 + c * P:1920 + c * P] for c in range(4)], [(0, 512, kb_t[:, :, span], 1.0)]))
        turn_stage(groups)
        units = []
        for t in range(2):
            for half in range(2):
                for c in range(4):
                    rows = slice(64 * half, 64 * half + 64)
                    h = 4 * half + c
                    units.append(dict(
                        keys=256, scores=[(qa_t[rows, c, t * P:t * P + P], ka_t[rows, :])], mask=band[:, t, :],
                        sink=sinks[l][:, h:h + 1],
                        outputs=[dict(values=lambda k, half=half: proj2[:, k, 640 + 64 * half:704 + 64 * half],
                                      p0=0, np=128, c0=0, w=64, turned=False, dst=y_v[:, t, h * 64:h * 64 + 64])]))
        for t in range(2):
            for h in range(8):
                rows = slice(64 * (h % 2), 64 * (h % 2) + 64)
                scores = [(qb_t[rows, h // 2, t * P:t * P + P], kb_t[rows, h // 2, :])]
                scores += [(softened[:, k, h:h + 1].broadcast_to([P, P]), upper[:, k, :]) for k in range(2)]
                units.append(dict(
                    keys=256, scores=scores, mask=causal[:, t, :], shift=cum_f[:, t, h:h + 1],
                    outputs=[dict(values=lambda k, h=h: proj2[:, k, 2304 + 64 * h:2368 + 64 * h],
                                  p0=0, np=128, c0=0, w=64, turned=False, dst=y_v[:, t, 512 + h * 64:576 + h * 64])]))
        attention_stage(units, turned[:, 0:3072])

    def conv_stage(l):
        open_stage()
        cw, cb = where["conv_w_2"][0] + 48 * l, where["conv_b_2"][0] + 12 * l
        tanh = [heads[:, 256 * i:256 * i + 256] for i in range(4)]

        def vector(dve):
            chain(dve, step_v, dve.memset(raw_conv[:, :, 0:3], 0.0))
            for c in range(12):
                dst = conv[:, c, :]
                chain(dve, step_v, dve.tensor_scalar(dst, raw_conv[:, c, 0:256], columns[:, cw + c:cw + c + 1],
                                                     columns[:, cb + c:cb + c + 1], ALU.mult, ALU.add))
                for k in range(1, 4):
                    ins = dve.scalar_tensor_tensor(out=dst, in0=raw_conv[:, c, k:k + 256],
                                                   scalar=columns[:, cw + 12 * k + c:cw + 12 * k + c + 1],
                                                   in1=dst, op0=ALU.mult, op1=ALU.add)
                    if k < 3:
                        chain(dve, step_v, ins)
                ins.then_inc(*ready_v.one())
                if c >= 2:
                    finish(dve, c - 2)
            finish(dve, 10)
            finish(dve, 11)

        def finish(dve, c):
            dve.wait_ge(*ready_a.at(c + 1))
            dve.wait_ge(*ready_v.at(c + 1))
            dve.scalar_tensor_tensor(out=conv[:, c, :], in0=tanh[c % 4], scalar=1.0, in1=conv[:, c, :],
                                     op0=ALU.add, op1=ALU.mult).then_inc(*read_v.one())

        def scalar(act):
            for c in range(12):
                act.wait_ge(*ready_v.at(c + 1))
                if c >= 4:
                    act.wait_ge(*read_v.at(c - 3))
                act.activation(tanh[c % 4], conv[:, c, :], ACT.Tanh).then_inc(*ready_a.one())

        run_stage(vector=vector, scalar=scalar)

    x_rows = turned[:, 0:2048].rearrange("p (t d) -> p t d", t=2)
    x_dt = turned[:, 2048:4096].rearrange("p (t d) -> p t d", t=2)

    def ssm_stage(l):
        open_stage()
        cb = heads[:, 0:768].rearrange("p (g n) -> p g n", g=2)
        decay = [heads[:, 768 + 384 * i:1152 + 384 * i] for i in range(2)]
        kernel_ = [heads[:, 1536 + 384 * i:1920 + 384 * i] for i in range(2)]

        def tensor(pe):
            for g in range(2):
                pe.matmul(psum[:, g, 0:256], conv[:, 8 + g, 0:128], conv[:, 10 + g, :], start=True, stop=True)
                pe.matmul(psum[:, g, 256:384], conv[:, 8 + g, 128:256], conv[:, 10 + g, 128:256],
                          start=True, stop=True).then_inc(*products.one())
            for h in range(17):
                if h < 16:
                    bank = 2 + h % 2
                    if h >= 2:
                        pe.wait_ge(*ready_a.at(h - 1))
                    for o, l0, n, s in ((0, 0, 256, 0), (256, 128, 128, 1)):
                        for k in range(2):
                            pe.matmul(psum[:, bank, o:o + n], decays[:, k, h:h + 1].broadcast_to([P, P]),
                                      upper[:, k, l0:l0 + n], start=k == 0, stop=False)
                        mm = pe.matmul(psum[:, bank, o:o + n], ident, causal_t[:, s, l0:l0 + n], start=False, stop=True)
                    mm.then_inc(*products.one())
                if h >= 1:
                    j = h - 1
                    m = kernel_[j % 2]
                    pe.wait_ge(*ready_v.at(j + 1))
                    if j >= 2:
                        pe.wait_ge(*read_v.at(2 + j - 1))
                    xs = [x_dt[:, t, j * 64:j * 64 + 64] for t in range(2)]
                    bank = 4 + j % 2
                    pe.matmul(psum[:, bank, 0:64], m[:, 0:128], xs[0], start=True, stop=True)
                    pe.matmul(psum[:, bank, 64:128], m[:, 128:256], xs[0], start=True, stop=False)
                    pe.matmul(psum[:, bank, 64:128], m[:, 256:384], xs[1], start=False, stop=True).then_inc(*products.one())

        def vector(dve):
            chain(dve, step_v, dve.tensor_tensor(
                out=x_dt.rearrange("p t (h d) -> p t h d", d=64), in0=x_rows.rearrange("p t (h d) -> p t h d", d=64),
                in1=softened[:, :, 8:24].unsqueeze(3).broadcast_to([P, 2, 16, 64]), op=ALU.mult))
            for g in range(2):
                dve.wait_ge(*products.at(g + 1))
                dve.tensor_copy(cb[:, g, :], psum[:, g, 0:384]).then_inc(*read_v.one())
            dve.wait_ge(*read_v.now())
            for h in range(17):
                if h < 16:
                    dve.wait_ge(*ready_a.at(h + 1))
                    if h >= 2:
                        dve.wait_ge(*products.at(2 + 2 * (h - 2) + 3))
                    dve.tensor_tensor(out=kernel_[h % 2], in0=decay[h % 2], in1=cb[:, h // 8, :], op=ALU.mult)\
                       .then_inc(*ready_v.one())
                if h >= 1:
                    j = h - 1
                    dve.wait_ge(*products.at(2 + (2 * j + 3 if j < 15 else 32)))
                    for t in range(2):
                        ins = dve.scalar_tensor_tensor(
                            out=y_v[:, t, 1024 + j * 64:1088 + j * 64], in0=x_rows[:, t, j * 64:j * 64 + 64],
                            scalar=d_skip[l][:, j:j + 1], in1=psum[:, 4 + j % 2, 64 * t:64 * t + 64],
                            op0=ALU.mult, op1=ALU.add)
                    ins.then_inc(*read_v.one())

        def scalar(act):
            for h in range(16):
                act.wait_ge(*products.at(2 + (1 if h == 0 else 2 * h)))
                if h >= 2:
                    act.wait_ge(*ready_v.at(h - 1))
                for o, n, s in ((0, 256, 0), (256, 128, 1)):
                    ins = act.activation(decay[h % 2][:, o:o + n], psum[:, 2 + h % 2, o:o + n], ACT.Exp,
                                         bias=neg_acs[:, s, h:h + 1])
                ins.then_inc(*ready_a.one())

        run_stage(tensor, vector, scalar)

    def gating_stage():
        open_stage()
        tanh = turned.rearrange("p (t d) -> p t d", t=2)
        spans = ((0, 512, 768), (512, 2048, 2824))

        def scalar(act):
            for t in range(2):
                for y0, y1, g0 in spans:
                    act.activation(tanh[:, t, y0:y1], proj2[:, t, g0:g0 + y1 - y0], ACT.Tanh, scale=0.5).then_inc(*ready_a.one())
            for t in range(2):
                act.wait_ge(*ready_v.at(t + 1))
                act.activation(tanh[:, t, 1024:2048], y_v[:, t, 1024:2048], ACT.Square,
                               accum_out=stats[:, t:t + 1]).then_inc(*ready_a.one())

        def vector(dve):
            for t in range(2):
                for i, (y0, y1, g0) in enumerate(spans):
                    g = proj2[:, t, g0:g0 + y1 - y0]
                    dve.wait_ge(*ready_a.at(2 * t + i + 1))
                    chain(dve, step_v, dve.scalar_tensor_tensor(out=g, in0=tanh[:, t, y0:y1], scalar=1.0, in1=g,
                                                                op0=ALU.add, op1=ALU.mult))
                    ins = dve.scalar_tensor_tensor(out=y_v[:, t, y0:y1], in0=g, scalar=HALVED, in1=y_v[:, t, y0:y1],
                                                   op0=ALU.mult, op1=ALU.mult)
                ins.then_inc(*ready_v.one())
            for t in range(2):
                dve.wait_ge(*ready_a.at(4 + t + 1))
                dve.tensor_scalar(stats[:, 8 + t:9 + t], stats[:, t:t + 1], 1.0 / DM, NORM_EPS,
                                  ALU.mult, ALU.add).then_inc(*ready_v.one())
            for t in range(2):
                dve.wait_ge(*ready_g.at(t + 1))
                dve.tensor_scalar(y_v[:, t, 1024:2048], y_v[:, t, 1024:2048], stats[:, 16 + t:17 + t], None,
                                  ALU.mult).then_inc(*step_v.one())

        def gpsimd(pool):
            for t in range(2):
                pool.wait_ge(*ready_v.at(2 + t + 1))
                inverse_root(pool, stats[:, 16 + t:17 + t], stats[:, 8 + t:9 + t], 1).then_inc(*ready_g.one())

        run_stage(vector=vector, scalar=scalar, gpsimd=gpsimd)

    def second_layer(l):
        norm_stage([0, 1], lambda k, t: column("norm_mix_w_2", 8 * l + k), None)
        linear_stage(
            [([("w_in2", l, b)], "rows", [0, 1], normed,
              lambda t, b=b: proj2[:, t, 512 * b:min(512 * b + 512, W2_TOKEN_COLS)]) for b in range(9)]
            + [([("conv", l, b)], "cols", [0, 1, 2, 3], lambda k, _: turned_v[:, k, 0:256],
                lambda c, b=b: raw_conv[:, 4 * b + c, 3:259]) for b in range(3)]
            + [([("dt", l)], "rows", [0, 1], normed, lambda t: dt_raw[:, t, :])])
        rotate_stage(l, [0, 1], lambda t: proj2[:, t, 0:640], cos2, sin2, 1, False)
        softplus_stage(l)
        second_attention(l)
        conv_stage(l)
        turn_stage([([conv[:, 4 * g + q, t * P:t * P + P] for q in range(4)],
                     [(0, 512, x_rows[:, t, 512 * g:512 * g + 512], 1.0)]) for t in range(2) for g in range(2)])
        ssm_stage(l)
        gating_stage()
        y_t = lifted.rearrange("p (k t) -> p k t", k=16)
        groups = []
        for t in range(2):
            for g in range(4):
                srcs = [y_v[:, t, (4 * g + q) * P:(4 * g + q + 1) * P] for q in range(4)]
                if g < 2:
                    outs = [(0, 512, y_t[:, 4 * g:4 * g + 4, t * P:t * P + P], 1.0)]
                else:
                    outs = [(q * P, P, y_t[:, 4 * g + q, t * P:t * P + P], column("ssm_norm_w_2", 8 * l + 4 * (g - 2) + q))
                            for q in range(4)]
                groups.append((srcs, outs))
        turn_stage(groups)
        linear_stage([([("w_out2", l, b, 0), ("w_out2", l, b, 1)], "rows", [0, 1],
                       lambda k, t: y_t[:, k, t * P:t * P + P], ("add", None, 512 * b)) for b in range(2)])
        norm_stage([0, 1, 2, 3], lambda k, t: column("norm_xq_w_2" if t < 2 else "norm_mem_w_2", 8 * l + k), None)
        q_t = heads[:, 0:2048].rearrange("p (c t) -> p c t", c=8)
        k_t = heads[:, 2048:4096].rearrange("p (c t) -> p c t", c=8)
        v_m = proj[:, 0:2048].rearrange("p (t n) -> p t n", t=2)
        o_t = lifted[:, 0:2048].rearrange("p (c t) -> p c t", c=8)
        linear_stage(
            [([("w_mq_2", l, b)], "cols", [0, 1, 2, 3], lambda k, _: turned_v[:, k, 0:256],
              lambda c, b=b: (q_t[:, 4 * b + c, :], 256 ** -0.5)) for b in range(2)]
            + [([("w_mk_2", l, b)], "cols", [0, 1, 2, 3], lambda k, _: turned_v[:, k, 256:512],
                lambda c, b=b: k_t[:, 4 * b + c, :]) for b in range(2)]
            + [([("w_mv_2", l, b)], "rows", [2, 3], normed, lambda t, b=b: v_m[:, t - 2, 512 * b:512 * b + 512])
               for b in range(2)])
        units = []
        for t in range(2):
            for h in range(4):
                units.append(dict(
                    keys=256, scores=[(q_t[:, 2 * h + j, t * P:t * P + P], k_t[:, 2 * h + j, :]) for j in range(2)],
                    outputs=[dict(values=lambda k, c=2 * h + j: v_m[:, k, c * P:c * P + P],
                                  p0=0, np=128, c0=128 * j, w=128, turned=True, dst=o_t[:, 2 * h + j, t * P:t * P + P])
                             for j in range(2)]))
        attention_stage(units, turned[:, 0:3072])
        linear_stage([([("w_mo_2", l, b)], "rows", [0, 1], lambda k, t: o_t[:, k, t * P:t * P + P],
                       ("add", None, 512 * b)) for b in range(2)])

    def final_stage():
        open_stage()
        gain = lifted[:, 0:DM]

        def sync(sp):
            sp.dma_start(gain, io["final_norm_w_2"].rearrange("(a d) -> a d", a=1).broadcast_to([P, DM]))\
              .then_inc(*loaded.one(16))
            for t in range(2):
                sp.wait_ge(*ready_v.at(2 + t + 1))
                sp.dma_start(out[0, t * P:t * P + P, :], mixed_v[:, t, :]).then_inc(*stored.one(16))
            sp.wait_ge(*stored.now())

        def scalar(act):
            for t in range(2):
                act.activation(mixed_v[:, t, :], stream[:, t, :], ACT.Square,
                               accum_out=stats[:, t:t + 1]).then_inc(*ready_a.one())

        def vector(dve):
            for t in range(2):
                dve.wait_ge(*ready_a.at(t + 1))
                dve.tensor_scalar(stats[:, 8 + t:9 + t], stats[:, t:t + 1], 1.0 / DM, NORM_EPS,
                                  ALU.mult, ALU.add).then_inc(*ready_v.one())
            dve.wait_ge(*loaded.at(16))
            for t in range(2):
                dve.wait_ge(*ready_g.at(t + 1))
                dve.scalar_tensor_tensor(out=mixed_v[:, t, :], in0=stream[:, t, :], scalar=stats[:, 16 + t:17 + t],
                                         in1=gain, op0=ALU.mult, op1=ALU.mult).then_inc(*ready_v.one())

        def gpsimd(pool):
            for t in range(2):
                pool.wait_ge(*ready_v.at(t + 1))
                inverse_root(pool, stats[:, 16 + t:17 + t], stats[:, 8 + t:9 + t], 1).then_inc(*ready_g.one())

        run_stage(vector=vector, scalar=scalar, gpsimd=gpsimd, sync=sync)

    run_stage()
    for l in range(DEPTH):
        first_layer(l)
        if stop == ("first", l):
            return
    load_second_stage()
    for l in range(DEPTH):
        second_layer(l)
        if stop == ("second", l):
            return
    final_stage()


_INS = ['x', 'c', 'ctx', 'c_ctx', 'ada_w', 'ada_b', 'norm_mix', 'w_in', 'fourier_w', 'pool_w', 'pool_scale',
        'pool_proj', 'q_norm', 'k_norm', 'attn_proj', 'w_out', 'norm_ffn', 'peer_wq', 'peer_keys', 'peer_u', 'peer_v',
        'mem_2', 'norm_mix_w_2', 'w_in_2', 'b_forget_2', 'swa_sinks_2', 'conv_w_2', 'conv_b_2', 'dt_bias_2',
        'a_log_2', 'd_skip_2', 'ssm_norm_w_2', 'w_out_2', 'norm_xq_w_2', 'norm_mem_w_2', 'w_mq_2', 'w_mk_2',
        'w_mv_2', 'w_mo_2', 'final_norm_w_2']
_OUTS = [((1, 256, 1024), 'float32')]


def kernel(**inputs):
    import numpy as _np
    import concourse.bacc as _bacc
    from concourse import mybir as _mybir
    from concourse.bass_utils import run_bass_kernel_spmd as _run

    nc = _bacc.Bacc("TRN2", target_bir_lowering=False, num_devices=1)
    arrays, io = {}, {}
    named = {name: inputs[name] for name in _INS}
    named.update(zip(("common", "first", "second"), shape_constants()))
    for name, a in named.items():
        a = _np.ascontiguousarray(a)
        arrays[f"in_{name}_dram"] = a
        io[name] = nc.dram_tensor(f"in_{name}_dram", a.shape, _mybir.dt.from_np(a.dtype), kind="ExternalInput").ap()
    outs = [nc.dram_tensor(f"out_{i}_dram", shape, _mybir.dt.from_np(_np.dtype(dtype)), kind="ExternalOutput").ap()
            for i, (shape, dtype) in enumerate(_OUTS)]
    build_kernel(nc, io, outs[0])
    r = _run(nc, [arrays], core_ids=[0])
    return r.results[0]["out_0_dram"]
```

```python
from contextlib import ExitStack

import numpy as np

import concourse.bass as bass
from concourse import mybir
from concourse.alu_op_type import AluOpType as ALU

ACT = mybir.ActivationFunctionType
F32 = mybir.dt.float32
U32 = mybir.dt.uint32
I32 = mybir.dt.int32
AX = mybir.AxisListType.X

P = 128
DM = 1024
KD = DM // P
SEQ = 256
DEPTH = 2
HD = 64
NORM_EPS = 1e-6
MASKED = -1e30
RING = 3
SLOT = 4096
TOPK = 16
PEER_HEADS = 8
PICKS = PEER_HEADS * TOPK
EXPERTS = 128 * 128
ROWS = 8
IN_COLS = 4352
OFF_G = 1280
HALVED = 0.5
LN2_HIGH = 0.693359375
LN2_LOW = float(np.log(2.0)) - LN2_HIGH
W2_TOKEN_COLS = 4360
W2_COLS = 5912


class Signal:

    def __init__(self, nc, name):
        self.sem = nc.alloc_semaphore(name)
        self.total = 0
        self.base = 0

    def one(self, by=1):
        self.total += by
        return self.sem, by

    def at(self, n):
        return self.sem, self.base + n

    def now(self):
        return self.sem, self.total


def window_mean(win):
    m = np.zeros((SEQ, SEQ), np.float64)
    for t in range(SEQ):
        lo, hi = max(t - win // 2, 0), min(t + win - win // 2, SEQ)
        m[lo:hi, t] = 1.0 / (hi - lo)
    return m - np.eye(SEQ)


def tiled(m):
    return m.reshape(2, P, -1).transpose(1, 0, 2).reshape(P, -1)


def rotary(angles, axes):
    cos, sin = np.cos(angles), np.sin(angles)
    c = np.concatenate([cos, cos], -1).reshape(SEQ, -1)
    s = np.concatenate([-sin, sin], -1).reshape(SEQ, -1)
    return c, s


def shape_constants():
    tok = np.arange(SEQ)
    common = np.concatenate([np.eye(P), np.ones((P, P)), np.tile(np.arange(16), (P, 1))], 1)
    ang = 2 * np.pi * (np.outer(tok, tok) % SEQ) / SEQ
    c_len, s_len = np.cos(ang) / np.sqrt(SEQ), np.sin(ang) / np.sqrt(SEQ)
    ch = np.arange(64)
    ang = 2 * np.pi * (np.outer(ch, ch) % 64) / 64
    two = np.eye(2)
    c_ch, s_ch = np.kron(two, np.cos(ang) / 8), np.kron(two, -np.sin(ang) / 8)
    pools = np.concatenate([tiled(window_mean(w)) for w in (2, 4, 8, 16)], 1)
    inv = (10000.0 ** (-np.arange(16, dtype=np.float32) / 16)).astype(np.float32)
    row = (tok // 64).astype(np.float32)[:, None] * inv
    col = (tok % 64).astype(np.float32)[:, None] * inv
    c1, s1 = rotary(np.stack([row, col], 1), 2)
    first = np.concatenate([tiled(c_len), tiled(s_len), c_ch, s_ch, pools, tiled(c1), tiled(s1)], 1)
    upper = (tok[:, None] <= tok[None, :]).astype(np.float64)
    rel = tok[:, None] - tok[None, :]
    band = np.where((rel >= 0) & (rel < 128), 0.0, MASKED)
    causal = np.where(rel >= 0, 0.0, MASKED)
    inv = (1.0 / (10000.0 ** (np.arange(0, 64, 2, dtype=np.float32) / 64))).astype(np.float32)
    c2, s2 = rotary((tok.astype(np.float32)[:, None] * inv)[:, None, :], 1)
    second = np.concatenate([tiled(upper), tiled(band), tiled(causal), tiled(causal.T), tiled(c2), tiled(s2)], 1)
    return [np.ascontiguousarray(a, np.float32) for a in (common, first, second)]


def build_kernel(nc, io, out, stop=None):
    ctx = ExitStack()

    def area(name, cols, dt=F32):
        return nc.alloc_sbuf_tensor(name, [P, cols], dt)[:, :]

    ring = area("ring", 2 * SLOT)
    stream = area("stream", 4 * DM).rearrange("p (t d) -> p t d", t=4)
    turned = area("turned", KD * 512)
    turned_s = [turned[:, 2048 * s:2048 * s + 2048].rearrange("p (k t) -> p k t", k=KD) for s in range(2)]
    proj = area("proj", 9216)
    mixed = area("mixed", 4 * DM)
    mixed_v = mixed.rearrange("p (t d) -> p t d", t=4)
    lifted = area("lifted", 4096)
    gate_rows = area("gate_rows", 4 * DM)
    heads = area("heads", 4096)
    tables = area("tables", 3584)
    common = area("common", 272)
    columns = area("columns", 352)
    lent = area("lent", SLOT)
    row_packs = mixed[:, 0:384].rearrange("p (a b) -> p a b", a=3)
    head_gain = area("head_gain", 256)
    small_rows = area("small_rows", 160)
    pool_blocks = area("pool_blocks", 512)
    stats = area("stats", 64)
    silu_c = area("silu_c", 32)
    mods = area("mods", 96)
    norm_cols = area("norm_cols", 64)
    soft = area("soft", 512)
    psum = nc.alloc_psum_tensor("psum", [P, 8, 512], F32)

    ident, ones, iota16 = common[:, 0:128], common[:, 128:256], common[:, 256:272]

    def signal(name):
        return Signal(nc, name)

    products = signal("products")
    read_v, read_a = signal("read_v"), signal("read_a")
    step_v, step_a = signal("step_v"), signal("step_a")
    ready_v, ready_a, ready_g = signal("ready_v"), signal("ready_a"), signal("ready_g")
    loaded = signal("loaded")
    stored = signal("stored")
    landed = [signal(f"landed{i}") for i in range(RING)]
    gathered = [signal(f"gathered{i}") for i in range(ROWS)]
    rows_used = signal("rows_used")
    staged = signal("staged")
    admitted = signal("admitted")
    picked = signal("picked")
    half_used = signal("half_used")
    meeting = signal("meeting")
    every = [products, read_v, read_a, step_v, step_a, ready_v, ready_a, ready_g, loaded, stored]

    def open_stage():
        for s in every:
            s.base = s.total

    def chain(eng, step, ins):
        ins.then_inc(*step.one())
        eng.wait_ge(*step.now())

    plan = []
    guest_loads = set()

    def merge_jobs(part):
        jobs = [(cb, br) for cb in range(2) for br in range(3)]
        if part == "late":
            return [(cb, br, False, True) for cb, br in jobs if br == 2]
        return [(cb, br, True, part == "all" or br < 2) for cb, br in jobs]

    def plan_block(key, w, c0, c1):
        plan.append((key, (c1 - c0), [(0, P, w[:, c0:c1].rearrange("(k p) n -> p k n", p=P))]))

    def plan_ada(l):
        for b in range(12):
            plan_block(("ada", l, b), io["ada_w"][l], 512 * b, 512 * b + 512)

    def plan_w_in(l):
        for b, (c0, c1) in enumerate(((0, 512), (512, 1024), (1024, 1280))):
            plan_block(("w_in", l, b), io["w_in"][l], c0, c1)

    def plan_merge(l, part):
        for cb, br, gates, branches in merge_jobs(part):
            c0 = 512 * cb
            if gates:
                g0 = OFF_G + br * DM + c0
                plan_block(("gate", l, cb, br), io["w_in"][l], g0, g0 + 512)
            if branches and br < 2:
                plan_block(("branch", l, cb, br), io["fourier_w" if br == 0 else "pool_proj"][l], c0, c0 + 512)
            elif branches:
                w = io["attn_proj"][l]
                plan.append((("branch", l, cb, br), 512,
                             [(64 * h, 64, w[256 * h:256 * h + 256, c0:c0 + 512].rearrange("(c d) n -> d c n", d=64))
                              for h in range(2)]))

    def plan_out(l):
        for b in range(2):
            plan_block(("w_out", l, b), io["w_out"][l], 512 * b, 512 * b + 512)
        plan.append((("keys", l), 128, [(0, P, io["peer_keys"][l].rearrange("h s n k -> n (h s) k"))]))
        for b in range(4):
            plan_block(("wq", l, b), io["peer_wq"][l], 512 * b, 512 * b + 512)

    def plan_second(l):
        w = io["w_in_2"][l]
        for b in range(9):
            plan_block(("w_in2", l, b), w, 512 * b, min(512 * b + 512, W2_TOKEN_COLS))
        for b in range(3):
            plan_block(("conv", l, b), w, W2_TOKEN_COLS + 512 * b, W2_TOKEN_COLS + 512 * b + 512)
        plan_block(("dt", l), w, W2_COLS - 16, W2_COLS)
        for b in range(2):
            for half in range(2):
                plan_block(("w_out2", l, b, half), io["w_out_2"][l][1024 * half:1024 * half + 1024, :],
                           512 * b, 512 * b + 512)
        for name in ("w_mq_2", "w_mk_2", "w_mv_2", "w_mo_2"):
            for b in range(2):
                plan_block((name, l, b), io[name][l], 512 * b, 512 * b + 512)

    plan_ada(0)
    for _ in range(2):
        plan_w_in(0)
        plan_merge(0, "all")
        plan_out(0)
        if not guest_loads:
            first_guest = len(plan)
            guest_loads.add(first_guest)
    plan_ada(1)
    plan_w_in(1)
    plan_merge(1, "early")
    guest_loads.update(range(first_guest, len(plan)))
    after_gathers = [(len(plan), 2)]
    plan_block(("w_in_kv", 1), io["w_in"][1], 1024, 1280)
    plan_merge(1, "late")
    plan_out(1)
    after_gathers.append((len(plan), 3))
    plan_second(0)
    plan_second(1)
    used = []
    landing = []
    slot_of = []
    last_user = []
    turn = 0
    in_slot = [None] * RING
    for n_load, (_, _, load_parts) in enumerate(plan):
        turn = (turn + 1) % (2 if n_load in guest_loads else RING)
        slot_of.append(turn)
        last_user.append(in_slot[turn])
        in_slot[turn] = n_load
        landed[turn].one(16 * len(load_parts))
        landing.append(landed[turn].now())
    gathers_done = [0]
    issued = [0]

    def gathers_ahead(n):
        return max([count for first, count in after_gathers if n >= first], default=0)

    def slot_view(n):
        key, cols, parts = plan[n]
        k = parts[0][2].shape[1]
        place = lent if slot_of[n] == 2 else ring[:, slot_of[n] * SLOT:(slot_of[n] + 1) * SLOT]
        return place[:, 0:k * cols].rearrange("p (k n) -> p k n", k=k)

    def issue_loads(sp):
        while issued[0] < len(plan):
            n = issued[0]
            before = last_user[n]
            if before is not None and before >= len(used):
                return
            if slot_of[n] == 2 and gathers_ahead(n):
                if gathers_done[0] < gathers_ahead(n):
                    return
                sp.wait_ge(rows_used.sem, ROWS + gathers_ahead(n) * 4 * PICKS)
            if before is not None:
                sp.wait_ge(*used[before])
            for p0, np_, src in plan[n][2]:
                sp.dma_start(slot_view(n)[p0:p0 + np_, :, :], src).then_inc(landed[slot_of[n]].sem, 16)
            issued[0] += 1

    def take(pe, key):
        n = len(used)
        assert plan[n][0] == key, (plan[n][0], key)
        pe.wait_ge(*landing[n])
        return slot_view(n)

    def release(signal_=None):
        used.append((signal_ or products).now())

    gather_count = [0]
    host = [None]

    def run_vector(vector, dve):
        for us in vector(dve) or ():
            if host[0]:
                host[0].advance(dve, us)

    def run_stage(tensor=None, vector=None, scalar=None, sync=None):
        if host[0]:
            return run_guest(host[0].block, tensor, vector, scalar)
        with nc.Block(no_gpsimd_drain=True) as block:
            if tensor:
                block.tensor(tensor)
            if vector:
                @block.vector
                def _(dve):
                    run_vector(vector, dve)
            if scalar:
                block.scalar(scalar)

            @block.sync
            def _(sp):
                if sync:
                    sync(sp)
                issue_loads(sp)

    def run_guest(block, tensor, vector, scalar):
        start = meeting.total

        def meet(eng):
            eng.drain()
            eng.sem_inc(*meeting.one())
            eng.wait_ge(meeting.sem, start + 3)

        @block.tensor
        def _(pe):
            if tensor:
                tensor(pe)
            meet(pe)

        @block.vector
        def _(dve):
            if vector:
                run_vector(vector, dve)
            meet(dve)

        @block.scalar
        def _(act):
            if scalar:
                scalar(act)
            meet(act)

        @block.sync
        def _(sp):
            issue_loads(sp)

    def setup_stage():
        open_stage()
        packs = [
            [("norm_mix", 16), ("norm_ffn", 16), ("ada_b", 96)],
            [("c", 8), ("c_ctx", 8), ("norm_mix_w_2", 16), ("norm_xq_w_2", 16), ("norm_mem_w_2", 16),
             ("ssm_norm_w_2", 16), ("conv_b_2", 24), ("pool_scale", 4)],
            [("conv_w_2", 96)],
        ]
        heights = [sum(n for _, n in pack) for pack in packs]
        where = {}
        for a, pack in enumerate(packs):
            r = 0
            for name, n in pack:
                where[name] = (a * P + r, n)
                r += n

        def sync(sp):
            sp.dma_start(common, io["common"]).then_inc(*loaded.one(16))
            for a, pack in enumerate(packs):
                r = 0
                for name, n in pack:
                    src = io[name]
                    if len(src.shape) == 3:
                        src = src.rearrange("a b c -> (a b c)")
                    elif len(src.shape) == 2:
                        src = src.rearrange("a b -> (a b)")
                    sp.dma_start(row_packs[r:r + n, a, :], src.rearrange("(r q) -> r q", q=P)).then_inc(*loaded.one(16))
                    r += n
            for t in range(2):
                sp.dma_start(stream[:, t, :], io["x"][0, t * P:t * P + P, :]).then_inc(*loaded.one(16))
                sp.dma_start(stream[:, 2 + t, :], io["ctx"][0, t * P:t * P + P, :]).then_inc(*loaded.one(16))
            sp.dma_start(tables[:, 0:3584], io["first"]).then_inc(*loaded.one(16))
            for l in range(DEPTH):
                for j, name in enumerate(("q_norm", "k_norm")):
                    sp.dma_start(head_gain[:, (2 * l + j) * HD:(2 * l + j + 1) * HD],
                                 io[name][l:l + 1, :].broadcast_to([P, HD])).then_inc(*loaded.one(16))
            r = 0
            for name in ("swa_sinks_2", "b_forget_2", "dt_bias_2", "a_log_2", "d_skip_2"):
                w = io[name].shape[1]
                for l in range(DEPTH):
                    sp.dma_start(small_rows[:, r:r + w], io[name][l:l + 1, :].broadcast_to([P, w])).then_inc(*loaded.one(16))
                    r += w
            sp.wait_ge(*ready_g.at(1))
            for l in range(DEPTH):
                for g in range(4):
                    c0 = (2 * l + g // 2) * P + 64 * (g % 2)
                    sp.dma_start(pool_blocks[64 * (g % 2):64 * (g % 2) + 64, c0:c0 + 64],
                                 io["pool_w"][l, g]).then_inc(*loaded.one(16))
            sp.wait_ge(*loaded.now())

        def gpsimd(pool):
            pool.memset(pool_blocks, 0.0).then_inc(*ready_g.one())

        def vector(dve):
            dve.memset(columns, 0.0).then_inc(*step_v.one())
            dve.wait_ge(*step_v.now())
            for a, rows in enumerate(heights):
                dve.wait_ge(*products.at(a + 1))
                c0 = a * P if a < 2 else 2 * P
                chain(dve, step_v, dve.tensor_copy(columns[:, c0:c0 + rows], psum[:, a, 0:rows]))
            for name in ("conv_w_2", "conv_b_2"):
                c0, n = where[name]
                chain(dve, step_v, dve.tensor_scalar(columns[:, c0:c0 + n], columns[:, c0:c0 + n], HALVED, None, ALU.mult))

        with nc.Block() as block:
            block.sync(sync)
            loads = loaded.total

            @block.gpsimd
            def _(pool):
                gpsimd(pool)

            @block.tensor
            def _(pe):
                pe.wait_ge(loaded.sem, loads)
                for a, rows in enumerate(heights):
                    pe.transpose(psum[:, a, 0:rows], row_packs[0:rows, a, :], ident[0:rows, 0:rows]).then_inc(*products.one())

            @block.vector
            def _(dve):
                dve.memset(soft, 0.0).then_inc(rows_used.sem, ROWS)
                rows_used.total += ROWS
                vector(dve)
                dve.wait_ge(*step_a.at(1))
                c0 = where["c"][0]
                th = silu_c[:, 0:16]
                chain(dve, step_v, dve.scalar_tensor_tensor(out=th, in0=th, scalar=1.0, in1=columns[:, c0:c0 + 16],
                                                            op0=ALU.add, op1=ALU.mult))
                chain(dve, step_v, dve.tensor_scalar(
                    silu_c[:, 16:32].rearrange("p (k s) -> p s k", s=2),
                    th.rearrange("p (s k) -> p s k", s=2), HALVED, None, ALU.mult))

            @block.scalar
            def _(act):
                act.wait_ge(*step_v.at(6))
                c0 = where["c"][0]
                act.activation(silu_c[:, 0:16], columns[:, c0:c0 + 16], ACT.Tanh, scale=0.5).then_inc(*step_a.one())
        return where

    where = setup_stage()

    def column(name, j):
        return columns[:, where[name][0] + j:where[name][0] + j + 1]

    def gate_row(which, s):
        return gate_rows[:, (2 * which + s) * DM:(2 * which + s + 1) * DM]

    def ada_stage(l):
        open_stage()
        mods_v = mods.rearrange("p (j s) -> p j s", s=2)
        cond = silu_c[:, 16:32].rearrange("p (k s) -> p k s", s=2)
        gain1, gain2 = (norm_cols[:, 16 * i:16 * i + 16].rearrange("p (k s) -> p k s", s=2) for i in range(2))
        diag = [soft[:, 128 * i:128 * i + 128] for i in range(4)]
        streams = range(2) if l < DEPTH - 1 else range(1)
        gate_list = [(w, s, k) for w in range(2) for s in streams for k in range(KD)]

        rows = soft[0:2, 0:512]

        def turn(pe, b):
            pe.wait_ge(*ready_a.at(b + 1))
            for c in range(4):
                j = 4 * b + c
                mm = pe.transpose(psum[:, 7, 2 * j:2 * j + 2], rows[:, c * P:c * P + P], ident[0:2, 0:2])
            mm.then_inc(*products.one())

        def tensor(pe):
            for b in range(12):
                w = take(pe, ("ada", l, b))
                if b >= 2:
                    pe.wait_ge(*ready_a.at(b - 1))
                for k in range(KD):
                    mm = pe.matmul(psum[0:2, b % 2, :], cond[:, k, :], w[:, k, :], start=k == 0, stop=k == KD - 1)
                mm.then_inc(*products.one())
                release()
                if b >= 1:
                    turn(pe, b - 1)
            turn(pe, 11)
            for i in range(len(gate_list)):
                pe.wait_ge(*ready_v.at(i + 1))
                bank = (i // 4) % 7
                if i // 4 >= 7 and i % 4 == 0:
                    pe.wait_ge(*read_a.at(i // 4 - 6))
                pe.matmul(psum[:, bank, 128 * (i % 4):128 * (i % 4) + 128], ones, diag[i % 4],
                          start=True, stop=True).then_inc(*products.one())

        def vector(dve):
            yield 93.0
            dve.wait_ge(*products.at(24))
            bias = columns[:, where["ada_b"][0] + 48 * l:where["ada_b"][0] + 48 * l + 48]
            chain(dve, step_v, dve.tensor_tensor(out=mods_v, in0=psum[:, 7, 0:96].rearrange("p (j s) -> p j s", s=2),
                                                 in1=bias.unsqueeze(2).broadcast_to([P, 48, 2]), op=ALU.add))
            for gain, m, name in ((gain1, 1, "norm_mix"), (gain2, 4, "norm_ffn")):
                g = columns[:, where[name][0] + 8 * l:where[name][0] + 8 * l + 8]
                chain(dve, step_v, dve.scalar_tensor_tensor(
                    out=gain, in0=mods_v[:, 8 * m:8 * m + 8, :], scalar=1.0,
                    in1=g.unsqueeze(2).broadcast_to([P, 8, 2]), op0=ALU.add, op1=ALU.mult))
            for i, (w, s, k) in enumerate(gate_list):
                if i >= 4:
                    dve.wait_ge(*products.at(24 + i - 3))
                dve.tensor_scalar(diag[i % 4], ident, mods_v[:, 8 * (2 + 3 * w) + k, s:s + 1], None, ALU.mult).then_inc(*ready_v.one())

        def scalar(act):
            for b in range(12):
                act.wait_ge(*products.at(1 if b == 0 else 2 * b))
                if b >= 1:
                    act.wait_ge(*products.at(2 * b + 1 if b < 12 else 24))
                act.copy(rows, psum[0:2, b % 2, :]).then_inc(*ready_a.one())
            for q in range(len(gate_list) // 4):
                act.wait_ge(*products.at(24 + 4 * q + 4))
                w, s, k = gate_list[4 * q]
                act.copy(gate_row(w, s)[:, P * k:P * k + 512], psum[:, q % 7, :]).then_inc(*read_a.one())

        run_stage(tensor, vector, scalar)

    def first_gain(which, k, s):
        return norm_cols[:, 16 * which + 2 * k + s:16 * which + 2 * k + s + 1]

    def first_shift(which, k, s):
        j = (0 if which == 0 else 3) * 8 + k
        return mods[:, 2 * j + s:2 * j + s + 1]

    def inverse_root(dve, dst, sums, scratch, count):
        w = dst.shape[1]
        v, y, t = (scratch[:, w * i:w * i + w] for i in range(3))
        chain(dve, step_v, dve.tensor_scalar(v, sums, 1.0 / count, NORM_EPS, ALU.mult, ALU.add))
        chain(dve, step_v, dve.tensor_scalar(y.bitcast(I32), v.bitcast(I32), 1, None, ALU.logical_shift_right))
        chain(dve, step_v, dve.tensor_scalar(y.bitcast(I32), y.bitcast(I32), -1.0, float(0x5F3759DF), ALU.mult, ALU.add))
        for i in range(4):
            chain(dve, step_v, dve.tensor_tensor(out=t, in0=y, in1=y, op=ALU.mult))
            chain(dve, step_v, dve.scalar_tensor_tensor(out=t, in0=t, scalar=-0.5, in1=v, op0=ALU.mult, op1=ALU.mult))
            chain(dve, step_v, dve.scalar_tensor_tensor(out=dst if i == 3 else y, in0=t, scalar=1.5, in1=y,
                                                        op0=ALU.add, op1=ALU.mult))

    def norm_stage(tiles, gain, shift, place=None):
        open_stage()
        n = len(tiles)

        def scalar(act):
            for i, t in enumerate(tiles):
                act.activation(mixed_v[:, t, :], stream[:, t, :], ACT.Square,
                               accum_out=stats[:, t:t + 1]).then_inc(*ready_a.one())
            for g in range(1, 2 * n, 2):
                act.wait_ge(*products.at(g + 1))
                for q in range(4):
                    k, t = 4 * (g % 2) + q, tiles[g // 2]
                    ins = act.activation(turned_s[t // 2 if place is None else place][:, k, (t % 2) * P:(t % 2) * P + P], psum[:, g % 8, q * P:q * P + P], ACT.Identity,
                                         scale=gain(k, t), bias=shift(k, t) if shift else 0.0)
                ins.then_inc(*read_a.one())

        def vector(dve):
            for i0 in range(0, n, 2):
                t = tiles[i0]
                yield 5.0
                dve.wait_ge(*ready_a.at(i0 + 2))
                inverse_root(dve, stats[:, 16 + t:18 + t], stats[:, t:t + 2], stats[:, 32:38], DM)
                for t in tiles[i0:i0 + 2]:
                    dve.tensor_scalar(mixed_v[:, t, :], stream[:, t, :], stats[:, 16 + t:17 + t], None,
                                      ALU.mult).then_inc(*ready_v.one())
            for g in range(0, 2 * n, 2):
                yield 5.0
                dve.wait_ge(*products.at(g + 1))
                for q in range(4):
                    k, t = 4 * (g % 2) + q, tiles[g // 2]
                    ins = dve.tensor_scalar(turned_s[t // 2 if place is None else place][:, k, (t % 2) * P:(t % 2) * P + P], psum[:, g % 8, q * P:q * P + P],
                                            gain(k, t), shift(k, t) if shift else 0.0, ALU.mult, ALU.add)
                ins.then_inc(*read_v.one())

        def tensor(pe):
            for g in range(2 * n):
                t = tiles[g // 2]
                pe.wait_ge(*ready_v.at(g // 2 + 1))
                for q in range(4):
                    k = 4 * (g % 2) + q
                    mm = pe.transpose(psum[:, g % 8, q * P:q * P + P], mixed_v[:, t, k * P:k * P + P], ident)
                mm.then_inc(*products.one())

        run_stage(tensor, vector, scalar)

    def turn_stage(groups):
        open_stage()

        def tensor(pe):
            for g, (sources, _) in enumerate(groups):
                if g >= 8:
                    pe.wait_ge(*(read_v if g % 2 == 0 else read_a).at((g - 8) // 2 + 1))
                for q, src in enumerate(sources):
                    mm = pe.transpose(psum[:, g % 8, q * P:q * P + P], src, ident)
                mm.then_inc(*products.one())

        def vector(dve):
            for g in range(0, len(groups), 2):
                yield 3.0
                dve.wait_ge(*products.at(g + 1))
                for c0, w, dst, scale in groups[g][1]:
                    src = psum[:, g % 8, c0:c0 + w]
                    if len(dst.shape) == 3:
                        src = src.rearrange("p (a b) -> p a b", a=dst.shape[1])
                    if isinstance(scale, float):
                        ins = dve.tensor_scalar(dst, src, scale, None, ALU.mult) if scale != 1.0 else dve.tensor_copy(dst, src)
                    else:
                        ins = dve.tensor_scalar(dst, src, scale, None, ALU.mult)
                ins.then_inc(*read_v.one())

        def scalar(act):
            for g in range(1, len(groups), 2):
                act.wait_ge(*products.at(g + 1))
                for c0, w, dst, scale in groups[g][1]:
                    src = psum[:, g % 8, c0:c0 + w]
                    if len(dst.shape) == 3:
                        src = src.rearrange("p (a b) -> p a b", a=dst.shape[1])
                    ins = act.activation(dst, src, ACT.Copy, scale=scale)
                ins.then_inc(*read_a.one())

        run_stage(tensor, vector, scalar)

    def linear_stage(jobs):
        open_stage()
        groups = []
        for job in jobs:
            keys, kind, items, lhs, dst = job
            for it in items:
                adding = isinstance(dst, tuple)
                groups.append((job, it, "v" if adding or len(groups) % 2 == 0 else "a"))
        order = {"v": 0, "a": 0}
        nth = []
        for _, _, e in groups:
            order[e] += 1
            nth.append(order[e])

        def tensor(pe):
            g = 0
            for job in jobs:
                keys, kind, items, lhs, dst = job
                weights = []
                for j, key in enumerate(keys):
                    n = len(used) + j
                    assert plan[n][0] == key, (plan[n][0], key)
                    weights.append(slot_view(n))
                k_total = sum(w.shape[1] for w in weights)
                k0 = 0
                for j, w in enumerate(weights):
                    pe.wait_ge(*landing[len(used)])
                    for q, it in enumerate(items):
                        b = g + q
                        if j == 0 and b >= 8:
                            pe.wait_ge(*(read_v if groups[b - 8][2] == "v" else read_a).at(nth[b - 8]))
                        for kk in range(w.shape[1]):
                            k, cols = k0 + kk, w.shape[2]
                            if kind == "rows":
                                mm = pe.matmul(psum[:, b % 8, 0:cols], lhs(k, it), w[:, kk, :],
                                               start=k == 0, stop=k == k_total - 1)
                            else:
                                rhs = lhs(k, None)
                                mm = pe.matmul(psum[:, b % 8, 0:rhs.shape[1]], w[:, kk, it * P:it * P + P], rhs,
                                               start=k == 0, stop=k == k_total - 1)
                        if j == len(weights) - 1:
                            mm.then_inc(*products.one())
                    if j < len(weights) - 1:
                        mm.then_inc(*half_used.one())
                        release(half_used)
                    else:
                        release()
                    k0 += w.shape[1]
                g += len(items)

        def vector(dve):
            for g, (job, it, e) in enumerate(groups):
                if e != "v":
                    continue
                yield 13.6 if not isinstance(job[4], tuple) else 8.0
                dve.wait_ge(*products.at(g + 1))
                dst = job[4]
                if isinstance(dst, tuple):
                    _, gate, c0 = dst
                    x = stream[:, it, c0:c0 + 512]
                    if gate is None:
                        dve.tensor_tensor(out=x, in0=psum[:, g % 8, :], in1=x, op=ALU.add).then_inc(*read_v.one())
                    else:
                        tmp = heads[:, 2048 + 512 * (g % 4):2560 + 512 * (g % 4)]
                        dve.tensor_tensor(out=tmp, in0=psum[:, g % 8, :], in1=gate(it)[:, c0:c0 + 512],
                                          op=ALU.mult).then_inc(*read_v.one())
                        dve.wait_ge(*read_v.now())
                        dve.tensor_tensor(out=x, in0=tmp, in1=x, op=ALU.add).then_inc(*step_v.one())
                else:
                    d = dst(it)
                    scale = 1.0
                    if isinstance(d, tuple):
                        d, scale = d
                    dve.tensor_scalar(d, psum[:, g % 8, 0:d.shape[1]], scale, None, ALU.mult).then_inc(*read_v.one())

        def scalar(act):
            for g, (job, it, e) in enumerate(groups):
                if e != "a":
                    continue
                act.wait_ge(*products.at(g + 1))
                d = job[4](it)
                scale = 1.0
                if isinstance(d, tuple):
                    d, scale = d
                act.activation(d, psum[:, g % 8, 0:d.shape[1]], ACT.Copy, scale=scale).then_inc(*read_a.one())

        run_stage(tensor, vector, scalar)

    def normed(k, t):
        return turned_s[t // 2][:, k, (t % 2) * P:(t % 2) * P + P]

    proj1 = proj[:, 0:2 * 1280].rearrange("p (t n) -> p t n", t=2)
    context_kv = proj[:, 2560:3072].rearrange("p (t n) -> p t n", t=2)
    sims_area = proj[:, 3072:7168]
    row_slots = ([lent[:, DM * u:DM * u + DM] for u in range(4)]
                 + [proj[:, 7168 + DM * u:8192 + DM * u] for u in range(2)]
                 + [turned[:, DM * u:DM * u + DM] for u in range(2)])
    proj2 = proj[:, 0:2 * W2_TOKEN_COLS].rearrange("p (t n) -> p t n", t=2)
    lifted_s = [lifted[:, 2048 * s:2048 * s + 2048].rearrange("p (c t) -> p c t", c=8) for s in range(2)]
    attention_gate = lifted_s[1].rearrange("p c t -> p (c t)").rearrange("p (t d) -> p t d", t=2)
    four_t, pool_t, attn_t = ([v[:, c0:c1, :] for v in lifted_s] for c0, c1 in ((0, 2), (2, 4), (4, 8)))
    c_len, s_len = (tables[:, 512 * i:512 * i + 512].rearrange("p (k t) -> p k t", k=2) for i in range(2))
    c_ch, s_ch = tables[:, 1024:1152], tables[:, 1152:1280]
    pools = tables[:, 1280:3328].rearrange("p (w k t) -> p w k t", w=4, k=2)

    def branch_stage(l, s):
        open_stage()
        units = range(2)
        turned_f = mixed[:, 2048 * s:2048 * s + 1024].rearrange("p (u n) -> p u n", u=2)
        pooled = mixed[:, 2048 * s + 1024:2048 * s + 1536].rearrange("p (u n) -> p u n", u=2)

        def tensor(pe):
            for u, ch in enumerate(units):
                for i, table in enumerate((c_len, s_len)):
                    for k in range(2):
                        mm = pe.matmul(psum[:, 2 * u, 256 * i:256 * i + 256], proj1[:, k, ch * P:ch * P + P],
                                       table[:, k, :], start=k == 0, stop=k == 1)
                mm.then_inc(*products.one())
                for half in range(2):
                    g = 2 * ch + half
                    for k in range(2):
                        mm = pe.matmul(psum[64 * half:64 * half + 64, 2 * u + 1, 0:256],
                                       proj1[:, k, 256 + 64 * g:320 + 64 * g], pools[:, g, k, :],
                                       start=k == 0, stop=k == 1)
                mm.then_inc(*products.one())
            for u, ch in enumerate(units):
                pe.wait_ge(*read_v.at(u + 1))
                pe.matmul(psum[:, 2 * u, 0:256], c_ch, turned_f[:, u, 0:256], start=True, stop=False)
                pe.matmul(psum[:, 2 * u, 0:256], s_ch, turned_f[:, u, 256:512], start=False, stop=True).then_inc(*products.one())
                pe.wait_ge(*read_a.at(u + 1))
                pe.matmul(psum[:, 2 * u + 1, 0:256], pool_blocks[:, (2 * l + ch) * P:(2 * l + ch + 1) * P], pooled[:, u, :],
                          start=True, stop=True).then_inc(*products.one())

        def vector(dve):
            for u in range(len(units)):
                yield 4.0
                dve.wait_ge(*products.at(2 * u + 1))
                dve.tensor_copy(turned_f[:, u, :], psum[:, 2 * u, :]).then_inc(*read_v.one())
            for u, ch in enumerate(units):
                dve.wait_ge(*products.at(2 * len(units) + 2 * u + 1))
                dve.tensor_copy(four_t[s][:, ch, :], psum[:, 2 * u, 0:256]).then_inc(*read_v.one())

        def scalar(act):
            for u in range(len(units)):
                act.wait_ge(*products.at(2 * u + 2))
                act.copy(pooled[:, u, :], psum[:, 2 * u + 1, 0:256]).then_inc(*read_a.one())
            for u, ch in enumerate(units):
                act.wait_ge(*products.at(2 * len(units) + 2 * u + 2))
                act.activation(pool_t[s][:, ch, :], psum[:, 2 * u + 1, 0:256], ACT.Copy,
                               scale=column("pool_scale", 2 * l + ch)).then_inc(*read_a.one())

        run_stage(tensor, vector, scalar)

    def rotate_stage(l, tiles, base, cos, sin, axes, gains):
        open_stage()
        f = HD // (2 * axes)
        work = ([sims_area[:, 640 * i:640 * i + 640] for i in range(2)] if gains else
                [heads[:, 2048 + 640 * i:2688 + 640 * i] for i in range(2)])

        def paired(v):
            return v.rearrange("p (c h d) -> p h c d", h=2, d=HD)

        def halves(v):
            return v.rearrange("p (h c d) -> p h c d", h=2, d=HD)

        def vector(dve):
            for t in tiles:
                x, dst = base(t), mixed_v[:, t, 0:640]
                n = x.shape[1] // HD
                h0 = 10 - n
                xh = x.rearrange("p (h d) -> p h d", d=HD)
                yield 20.0
                if gains:
                    a = work[0].rearrange("p (h d) -> p h d", d=HD)[:, h0:10, :]
                    chain(dve, step_v, dve.tensor_tensor(out=a, in0=xh, in1=xh, op=ALU.mult))
                    chain(dve, step_v, dve.tensor_reduce(stats[:, h0:10], a, AX, ALU.add))
                    inverse_root(dve, stats[:, 10 + h0:20], stats[:, h0:10], stats[:, 24:24 + 3 * n], HD)
                    chain(dve, step_v, dve.tensor_tensor(
                        out=xh, in0=xh, in1=stats[:, 10 + h0:20].unsqueeze(2).broadcast_to([P, n, HD]), op=ALU.mult))
                    q_gain, k_gain = (head_gain[:, (2 * l + j) * HD:(2 * l + j + 1) * HD] for j in range(2))
                    if h0 == 0:
                        q = x[:, 0:512]
                        chain(dve, step_v, dve.tensor_tensor(
                            out=q.rearrange("p (h d) -> p h d", d=HD) if t < 2 else paired(dst[:, 0:512]),
                            in0=q.rearrange("p (h d) -> p h d", d=HD) if t < 2 else halves(q),
                            in1=q_gain.unsqueeze(1).broadcast_to([P, 8, HD]) if t < 2 else
                            q_gain.unsqueeze(1).unsqueeze(1).broadcast_to([P, 2, 4, HD]), op=ALU.mult))
                    yield 25.0
                    k_dst = (x if t < 2 else dst)[:, 512:640].rearrange("p (h d) -> p h d", d=HD)
                    chain(dve, step_v, dve.tensor_tensor(out=k_dst, in0=xh[:, n - 2:n, :],
                                                         in1=k_gain.unsqueeze(1).broadcast_to([P, 2, HD]), op=ALU.mult))
                if t < 2:
                    a, b = work[0], work[1]
                    c, s = cos[:, t, :], sin[:, t, :]
                    chain(dve, step_v, dve.tensor_tensor(out=a.rearrange("p (h d) -> p h d", d=HD), in0=xh,
                                                         in1=c.unsqueeze(1).broadcast_to([P, 10, HD]), op=ALU.mult))
                    xv = x.rearrange("p (h a b f) -> p h a b f", h=10, a=axes, b=2)
                    bv = b.rearrange("p (h a b f) -> p h a b f", h=10, a=axes, b=2)
                    sv = s.rearrange("p (a b f) -> p a b f", a=axes, b=2)
                    for side in range(2):
                        chain(dve, step_v, dve.tensor_tensor(
                            out=bv[:, :, :, side, :], in0=xv[:, :, :, 1 - side, :],
                            in1=sv[:, :, side, :].unsqueeze(1).broadcast_to([P, 10, axes, f]), op=ALU.mult))
                    chain(dve, step_v, dve.tensor_tensor(out=paired(dst[:, 0:512]), in0=halves(a[:, 0:512]),
                                                         in1=halves(b[:, 0:512]), op=ALU.add))
                    chain(dve, step_v, dve.tensor_tensor(out=dst[:, 512:640], in0=a[:, 512:640], in1=b[:, 512:640],
                                                         op=ALU.add))

        run_stage(vector=vector)

    def attention_stage(units, temps, wide):
        open_stage()
        n = len(units)
        s_buf, p_buf, t_buf = ([temps[:, w * i:w * i + w] for i in range(i0, i0 + m)]
                               for i0, m, w in ((0, 2, wide), (2, 3, wide), (5, 2, wide)))

        def nth_product(i, what):
            count = 0
            for r in range(n + 3):
                for w, lag in ((0, 0), (1, 2), (2, 3)):
                    if 0 <= r - lag < n:
                        count += 1
                        if (r - lag, w) == (i, what):
                            return count

        def maxima(i):
            return 1 if i == 0 else 2 * i

        def divided(i):
            return 2 * i + 3 if i < n - 1 else 2 * n

        def tensor(pe):
            for i in range(n + 3):
                if i < n:
                    u = units[i]
                    if i >= 3:
                        pe.wait_ge(*ready_a.at(i - 2))
                    for j, (a, b) in enumerate(u["scores"]):
                        mm = pe.matmul(psum[:, i % 3, 0:u["keys"]], a, b, start=j == 0, stop=j == len(u["scores"]) - 1)
                    mm.then_inc(*products.one())
                if 0 <= i - 2 < n:
                    j = i - 2
                    pe.wait_ge(*ready_v.at(divided(j)))
                    if j >= 2:
                        pe.wait_ge(*read_a.at(j - 1))
                    for k in range(units[j]["keys"] // P):
                        mm = pe.transpose(psum[:, 3 + j % 2, k * P:k * P + P], p_buf[j % 3][:, k * P:k * P + P], ident)
                    mm.then_inc(*products.one())
                if i >= 3:
                    j = i - 3
                    pe.wait_ge(*read_a.at(j + 1))
                    if j >= 2:
                        pe.wait_ge(*read_v.at(j - 1))
                    kt = units[j]["keys"] // P
                    for mk in units[j]["outputs"]:
                        o = psum[mk["p0"]:mk["p0"] + mk["np"], 5 + j % 2, mk["c0"]:mk["c0"] + mk["w"]]
                        for k in range(kt):
                            probs, v = t_buf[j % 2][:, k * P:k * P + P], mk["values"](k)
                            a, b = (v, probs) if mk["turned"] else (probs, v)
                            mm = pe.matmul(o, a, b, start=k == 0, stop=k == kt - 1)
                    mm.then_inc(*products.one())

        def vector(dve):
            for i in range(n + 4):
                if i < n:
                    u = units[i]
                    keys = u["keys"]
                    yield 7.0
                    dve.wait_ge(*products.at(nth_product(i, 0)))
                    src = psum[:, i % 3, 0:keys]
                    if u.get("mask") is not None:
                        dst = s_buf[i % 2][:, 0:keys]
                        if i >= 2:
                            dve.wait_ge(*ready_a.at(i - 1))
                        if u.get("shift") is not None:
                            chain(dve, step_v, dve.scalar_tensor_tensor(out=dst, in0=src, scalar=u["shift"], in1=u["mask"],
                                                                        op0=ALU.add, op1=ALU.add))
                        else:
                            chain(dve, step_v, dve.tensor_tensor(out=dst, in0=src, in1=u["mask"], op=ALU.add))
                        src = dst
                    neg = soft[:, 4 * (i % 3):4 * (i % 3) + 1]
                    if u.get("sink") is None:
                        dve.tensor_reduce(neg, src, AX, ALU.max, negate=True).then_inc(*ready_v.one())
                    else:
                        chain(dve, step_v, dve.tensor_reduce(neg, src, AX, ALU.max))
                        dve.tensor_scalar(neg, neg, u["sink"], -1.0, ALU.max, ALU.mult).then_inc(*ready_v.one())
                if 1 <= i <= n:
                    j = i - 1
                    keys = units[j]["keys"]
                    total, extra, inv = (soft[:, 4 * (j % 3) + q:4 * (j % 3) + q + 1] for q in (1, 2, 3))
                    dve.wait_ge(*ready_a.at(j + 1))
                    if units[j].get("sink") is not None:
                        chain(dve, step_v, dve.tensor_tensor(out=total, in0=total, in1=extra, op=ALU.add))
                    chain(dve, step_v, dve.reciprocal(inv, total))
                    dve.tensor_scalar(p_buf[j % 3][:, 0:keys], p_buf[j % 3][:, 0:keys], inv, None,
                                      ALU.mult).then_inc(*ready_v.one())
                if i >= 4:
                    j = i - 4
                    dve.wait_ge(*products.at(nth_product(j, 2)))
                    for mk in units[j]["outputs"]:
                        ins = dve.tensor_copy(mk["dst"], psum[mk["p0"]:mk["p0"] + mk["np"], 5 + j % 2,
                                                              mk["c0"]:mk["c0"] + mk["w"]])
                    ins.then_inc(*read_v.one())

        def scalar(act):
            for i in range(n + 2):
                if i < n:
                    u = units[i]
                    keys = u["keys"]
                    act.wait_ge(*ready_v.at(maxima(i)))
                    if i >= 3:
                        act.wait_ge(*products.at(nth_product(i - 3, 1)))
                    neg, total, extra = (soft[:, 4 * (i % 3) + q:4 * (i % 3) + q + 1] for q in range(3))
                    if u.get("sink") is not None:
                        act.activation(extra, u["sink"], ACT.Exp, bias=neg).then_inc(*step_a.one())
                    src = psum[:, i % 3, 0:keys] if u.get("mask") is None else s_buf[i % 2][:, 0:keys]
                    act.activation(p_buf[i % 3][:, 0:keys], src, ACT.Exp, bias=neg, accum_out=total).then_inc(*ready_a.one())
                if i >= 2:
                    j = i - 2
                    keys = units[j]["keys"]
                    act.wait_ge(*products.at(nth_product(j, 1)))
                    if j >= 2:
                        act.wait_ge(*products.at(nth_product(j - 2, 2)))
                    act.copy(t_buf[j % 2][:, 0:keys], psum[:, 3 + j % 2, 0:keys]).then_inc(*read_a.one())

        run_stage(tensor, vector, scalar)

    def merge_stage(l, s, part="all", place=None):
        open_stage()
        tiles = [2 * s, 2 * s + 1]
        jobs = merge_jobs(part)
        place = s if place is None else place
        sources = (four_t[s], pool_t[s], attn_t[s])
        tanh = [sims_area[:, 512 * i:512 * i + 512] for i in range(2)]
        tmp = sims_area[:, 1024:1536]
        units, gate_at, branch_at = [], [], []
        count = 0
        for job in jobs:
            gates, branches = job[2:]
            units += [(job, t) for t in tiles]
            gate_at += [count + 1, count + 2]
            count += 2 if gates else 0
            branch_at += [count + 1, count + 2]
            count += 2 if branches else 0

        def tensor(pe):
            q = 0
            for cb, br, gates, branches in jobs:
                src = sources[br]
                if gates:
                    w = take(pe, ("gate", l, cb, br))
                    for i in range(2):
                        if q + i >= 4:
                            pe.wait_ge(*read_v.at(q + i - 3))
                        for k in range(KD):
                            mm = pe.matmul(psum[:, 2 * ((q + i) % 4), :], turned_s[place][:, k, i * P:i * P + P], w[:, k, :],
                                           start=k == 0, stop=k == KD - 1)
                        mm.then_inc(*products.one())
                    release()
                if branches:
                    w = take(pe, ("branch", l, cb, br))
                    for i in range(2):
                        for k in range(src.shape[1]):
                            mm = pe.matmul(psum[:, 2 * ((q + i) % 4) + 1, :], src[:, k, i * P:i * P + P],
                                           w[:, k, :], start=k == 0, stop=k == src.shape[1] - 1)
                        mm.then_inc(*products.one())
                    release()
                q += 2

        def scalar(act):
            for q, ((_, _, gates, _), _) in enumerate(units):
                if not gates:
                    continue
                act.wait_ge(*products.at(gate_at[q]))
                if q >= 2:
                    act.wait_ge(*read_v.at(q - 1))
                act.activation(tanh[q % 2], psum[:, 2 * (q % 4), :], ACT.Tanh, scale=0.5).then_inc(*read_a.one())

        def vector(dve):
            for q, ((cb, br, gates, branches), t) in enumerate(units):
                yield 9.5
                kept = attention_gate[:, t % 2, 512 * cb:512 * cb + 512]
                if gates:
                    dve.wait_ge(*read_a.at(q + 1))
                if not branches:
                    dve.tensor_scalar(kept, tanh[q % 2], 1.0, None, ALU.add).then_inc(*read_v.one())
                    continue
                dve.wait_ge(*products.at(branch_at[q]))
                acc = mixed_v[:, t, 512 * cb:512 * cb + 512]
                dst = acc if br == 0 else tmp
                branch = psum[:, 2 * (q % 4) + 1, :]
                if gates:
                    ins = dve.scalar_tensor_tensor(out=dst, in0=tanh[q % 2], scalar=1.0, in1=branch, op0=ALU.add, op1=ALU.mult)
                else:
                    ins = dve.tensor_tensor(out=dst, in0=kept, in1=branch, op=ALU.mult)
                ins.then_inc(*read_v.one())
                dve.wait_ge(*read_v.now())
                if br:
                    chain(dve, step_v, dve.tensor_tensor(out=acc, in0=acc, in1=tmp, op=ALU.add))

        run_stage(tensor, vector, scalar)

    def turn_mixed(s, scale):
        turn_stage([([mixed_v[:, t, (4 * g + q) * P:(4 * g + q + 1) * P] for q in range(4)],
                     [(0, 512, turned_s[s][:, 4 * g:4 * g + 4, (t % 2) * P:(t % 2) * P + P], scale)])
                    for t in (2 * s, 2 * s + 1) for g in range(2)])

    def turn_back(s):
        turn_stage([([turned_s[s][:, 4 * g + q, (t % 2) * P:(t % 2) * P + P] for q in range(4)],
                     [(0, 512, mixed_v[:, t, 512 * g:512 * g + 512], 1.0)])
                    for t in (2 * s, 2 * s + 1) for g in range(2)])

    sims = sims_area.rearrange("p (t h n) -> p t h n", t=2, h=16)
    picks_u = area("picks_u", 4 * PICKS, U32).rearrange("p (t j) -> p t j", t=4)
    probs_g = area("probs_g", 4 * PICKS).rearrange("p (t j) -> p t j", t=4)

    def keys_stage(l, s):
        open_stage()
        nt = 2
        n_tok = P * nt
        keys_t = lifted[:, 2048 * s:2048 * s + 2048]
        qt = [heads[:, 2048 + n_tok * i:2048 + n_tok * (i + 1)] for i in range(4)]

        def tensor(pe):
            w = take(pe, ("keys", l))
            for g in range(4):
                for q in range(4):
                    mm = pe.transpose(psum[:, g, q * P:q * P + P], w[:, 4 * g + q, :], ident)
                mm.then_inc(*products.one())
            release()
            for h in range(16):
                if h % 4 == 0:
                    w = take(pe, ("wq", l, h // 4))
                pe.wait_ge(*read_v.at(max(4, 4 + h - 3)))
                for k in range(KD):
                    mm = pe.matmul(psum[:, h % 4, 0:n_tok], w[:, k, (h % 4) * P:(h % 4) * P + P], turned_s[s][:, k, :],
                                   start=k == 0, stop=k == KD - 1)
                mm.then_inc(*products.one())
                if h % 4 == 3:
                    release()
                if h >= 1:
                    dot(pe, h - 1)
            dot(pe, 15)

        def dot(pe, h):
            pe.wait_ge(*read_v.at(4 + h + 1))
            if h >= 4:
                pe.wait_ge(*read_a.at(h - 3))
            for i in range(nt):
                mm = pe.matmul(psum[:, 4 + h % 4, i * P:i * P + P], qt[h % 4][:, i * P:i * P + P],
                               keys_t[:, h * P:h * P + P], start=True, stop=True)
            mm.then_inc(*products.one())

        def vector(dve):
            for g in range(4):
                dve.wait_ge(*products.at(g + 1))
                dve.tensor_copy(keys_t[:, 512 * g:512 * g + 512], psum[:, g, :]).then_inc(*read_v.one())
            for h in range(16):
                yield 4.0
                dve.wait_ge(*products.at(4 + (1 if h == 0 else 2 * h)))
                if h >= 4:
                    dve.wait_ge(*products.at(4 + dots_at(h - 4)))
                dve.tensor_copy(qt[h % 4], psum[:, h % 4, 0:n_tok]).then_inc(*read_v.one())

        def dots_at(h):
            return 2 * h + 3 if h < 15 else 32

        def scalar(act):
            for h in range(16):
                act.wait_ge(*products.at(4 + dots_at(h)))
                act.copy(sims[:, 0:nt, h, :], psum[:, 4 + h % 4, 0:n_tok].rearrange("p (t n) -> p t n", t=nt))\
                   .then_inc(*read_a.one())

        run_stage(tensor, vector, scalar)

    def topk_stage(l, t):
        open_stage()
        heads_hi = heads[:, 2048:4096]
        best = heads_hi[:, 0:256].rearrange("p (h k) -> p h k", h=16)
        best_u = heads_hi[:, 256:512].bitcast(U32).rearrange("p (h k) -> p h k", h=16)
        best_i = heads_hi[:, 512:768].rearrange("p (h k) -> p h k", h=16)
        pos_u = heads_hi[:, 1024:1152].bitcast(U32)
        side_u = heads_hi[:, 1152:1280].bitcast(U32)
        side_f = heads_hi[:, 1280:1408]
        gathered_i = [heads_hi[:, 1408:1536], heads_hi[:, 1536:1664]]
        hot = lifted[:, 0:2048]
        cand = [hot[:, 256 * i:256 * i + 256] for i in range(2)]
        top = heads_hi[:, 1664:1792]
        spare = heads_hi[:, 1792:1920]

        def step(dve, ins):
            chain(dve, step_v, ins)

        def sixteen(dve, *searches):
            last = [None] * len(searches)
            for part in range(5):
                for i, (values, indices, src) in enumerate(searches):
                    if last[i]:
                        dve.wait_ge(*last[i])
                    first, second = (v[:, 0:8] for v in (values, indices))
                    if part >= 3:
                        first, second = (v[:, 8:16] for v in (values, indices))
                    if part in (0, 3):
                        ins = dve.max(first, src)
                    elif part in (1, 4):
                        ins = dve.max_index(second, first, src)
                    else:
                        ins = dve.match_replace(src, first, src, -3e38)
                    ins.then_inc(*step_v.one())
                    last[i] = step_v.now()

        def vector(dve):
            for h in range(0, 16, 2):
                sixteen(dve, *[(best[:, g, :], best_u[:, g, :], sims[:, t % 2, g, :]) for g in (h, h + 1)])
                yield 9.0
            dve.wait_ge(*step_v.now())
            step(dve, dve.tensor_copy(best_i, best_u))
            for h in range(0, PEER_HEADS, 2):
                dve.wait_ge(*step_v.now())
                for i in range(2):
                    a = best[:, 2 * (h + i), :].unsqueeze(2).broadcast_to([P, 16, 16])
                    b = best[:, 2 * (h + i) + 1, :].unsqueeze(1).broadcast_to([P, 16, 16])
                    dve.tensor_tensor(out=cand[i].rearrange("p (a b) -> p a b", a=16), in0=a, in1=b,
                                      op=ALU.add).then_inc(*step_v.one())
                dve.wait_ge(*step_v.now())
                sixteen(dve, *[(top[:, 16 * g:16 * g + 16], pos_u[:, 16 * g:16 * g + 16], cand[g - h]) for g in (h, h + 1)])
                yield 18.0
            dve.wait_ge(*step_v.now())
            for side in range(2):
                if side == 0:
                    step(dve, dve.tensor_scalar(side_u, pos_u, 4, None, ALU.logical_shift_right))
                else:
                    step(dve, dve.tensor_scalar(side_u, pos_u, 15, None, ALU.bitwise_and))
                yield 12.0
                step(dve, dve.tensor_copy(side_f, side_u))
                eq = hot.rearrange("p (j r) -> p j r", r=16)
                step(dve, dve.tensor_tensor(out=eq, in0=side_f.unsqueeze(2).broadcast_to([P, PICKS, 16]),
                                            in1=iota16.unsqueeze(1).broadcast_to([P, PICKS, 16]), op=ALU.is_equal))
                eq4 = hot.rearrange("p (h j r) -> p h j r", h=PEER_HEADS, r=16)
                keys = best_i.rearrange("p (h s) k -> p h s k", s=2)[:, :, side, :]
                step(dve, dve.tensor_tensor(out=eq4, in0=eq4, in1=keys.unsqueeze(2).broadcast_to([P, PEER_HEADS, TOPK, 16]),
                                            op=ALU.mult))
                yield 12.0
                step(dve, dve.tensor_reduce(gathered_i[side], eq, AX, ALU.add))
            step(dve, dve.scalar_tensor_tensor(out=side_f, in0=gathered_i[0], scalar=128.0, in1=gathered_i[1],
                                               op0=ALU.mult, op1=ALU.add))
            if l:
                step(dve, dve.tensor_scalar(side_f, side_f, float(l * EXPERTS), None, ALU.add))
            dve.tensor_copy(picks_u[:, t, :], side_f).then_inc(*picked.one())
            tv = top.rearrange("p (h k) -> p h k", k=TOPK)
            step(dve, dve.tensor_reduce(spare[:, 0:8], tv, AX, ALU.max))
            dve.tensor_tensor(out=tv, in0=tv, in1=spare[:, 0:8].unsqueeze(2).broadcast_to([P, 8, TOPK]),
                              op=ALU.subtract).then_inc(*ready_v.one())
            yield 12.0
            dve.wait_ge(*ready_a.at(1))
            gv = probs_g[:, t, :].rearrange("p (h k) -> p h k", k=TOPK)
            step(dve, dve.tensor_reduce(spare[:, 8:16], gv, AX, ALU.add))
            step(dve, dve.reciprocal(spare[:, 16:24], spare[:, 8:16]))
            step(dve, dve.tensor_tensor(out=gv, in0=gv, in1=spare[:, 16:24].unsqueeze(2).broadcast_to([P, 8, TOPK]),
                                        op=ALU.mult))

        def scalar(act):
            act.wait_ge(*ready_v.at(1))
            act.activation(probs_g[:, t, :], top, ACT.Exp).then_inc(*ready_a.one())

        run_stage(vector=vector, scalar=scalar)

    index_stage = area("index_stage", 16, U32)
    dots = area("dots", PICKS)
    ROW_US = 1.456
    tables_dram = [io[n].rearrange("l n d -> (l n) d") for n in ("peer_u", "peer_v")]

    class RowWork:

        def __init__(self, block, s, scratch):
            self.block, self.s = block, s
            self.phases = [(t, which) for t in (2 * s, 2 * s + 1) for which in range(2)]
            self.base = rows_used.total
            self.row = 0
            self.owed = 0.0
            self.scratch = scratch

        def advance(self, dve, us):
            self.owed += us
            while self.owed >= ROW_US and self.row < len(self.phases) * PICKS:
                self.owed -= ROW_US
                self.rows(dve, 1)

        def finish(self, dve):
            while self.row < len(self.phases) * PICKS:
                left = PICKS - self.row % PICKS
                if self.row % ROWS:
                    self.rows(dve, 1)
                else:
                    self.rows(dve, left)

        def rows(self, dve, n):
            ph, j = divmod(self.row, PICKS)
            t, which = self.phases[ph]
            if j == 0 and which == 1:
                self.weigh(dve, t)
            if n == 1:
                self.one_row(dve, t, which, self.row % ROWS, j, self.base + self.row, None)
            else:
                with dve.Fori(0, n // ROWS) as i:
                    for u in range(ROWS):
                        self.one_row(dve, t, which, u, j + u, self.base + self.row + u, i)
            self.row += n
            if self.row % PICKS == 0:
                dve.wait_ge(rows_used.sem, self.base + self.row)
                if which == 1:
                    self.store(dve, t)

        def one_row(self, dve, t, which, u, j, row, i):
            step = 0 if i is None else i
            if i is None:
                dve.wait_ge(gathered[u].sem, 16 * ((row - ROWS) // ROWS + 1))
                weight = dots[:, j:j + 1]
            else:
                dve.wait_ge(gathered[u].sem, step * 16 + 16 * ((row - ROWS) // ROWS + 1))
                weight = dots[:, bass.ds(step * ROWS + j, 1)]
            src = row_slots[u]
            if which == 0:
                dve.scalar_tensor_tensor(out=src, in0=src, scalar=1.0, in1=mixed_v[:, t, :], op0=ALU.mult, op1=ALU.mult,
                                         accum_out=weight).then_inc(rows_used.sem, 1)
            else:
                acc = heads[:, DM * (u % 2):DM * (u % 2) + DM]
                dve.wait_ge(rows_used.sem, row - 1 if i is None else step * ROWS + (row - 1))
                dve.scalar_tensor_tensor(out=acc, in0=src, scalar=weight, in1=acc, op0=ALU.mult, op1=ALU.add)\
                   .then_inc(rows_used.sem, 1)

        def weigh(self, dve, t):
            cube, arg, n, f, poly, power = self.scratch
            c = -2.0 * float(np.sqrt(2.0 / np.pi))
            shift = 1.5 * 2.0 ** 23
            chain(dve, step_v, dve.tensor_tensor(out=cube, in0=dots, in1=dots, op=ALU.mult))
            chain(dve, step_v, dve.tensor_scalar(cube, cube, 0.044715 * c, c, ALU.mult, ALU.add))
            chain(dve, step_v, dve.tensor_tensor(out=arg, in0=cube, in1=dots, op=ALU.mult))
            chain(dve, step_v, dve.tensor_scalar(arg, arg, 80.0, -80.0, ALU.min, ALU.max))
            chain(dve, step_v, dve.tensor_scalar(n, arg, 1.0 / float(np.log(2.0)), shift, ALU.mult, ALU.add))
            chain(dve, step_v, dve.tensor_scalar(n, n, -shift, None, ALU.add))
            chain(dve, step_v, dve.scalar_tensor_tensor(out=f, in0=n, scalar=-LN2_HIGH, in1=arg, op0=ALU.mult, op1=ALU.add))
            dve.tensor_scalar(power, n, 2.0 ** 23, 127 * 2.0 ** 23, ALU.mult, ALU.add).then_inc(*step_v.one())
            chain(dve, step_v, dve.scalar_tensor_tensor(out=f, in0=n, scalar=-LN2_LOW, in1=f, op0=ALU.mult, op1=ALU.add))
            dve.tensor_copy(n.bitcast(U32), power).then_inc(*step_v.one())
            chain(dve, step_v, dve.tensor_scalar(poly, f, 1.0 / 5040, None, ALU.mult))
            for factorial in (720, 120, 24, 6, 2, 1):
                chain(dve, step_v, dve.scalar_tensor_tensor(out=poly, in0=poly, scalar=1.0 / factorial, in1=f,
                                                            op0=ALU.add, op1=ALU.mult))
            chain(dve, step_v, dve.scalar_tensor_tensor(out=arg, in0=poly, scalar=1.0, in1=n, op0=ALU.add, op1=ALU.mult))
            chain(dve, step_v, dve.tensor_scalar(cube, arg, 1.0, None, ALU.add))
            dve.memset(heads[:, 0:2 * DM], 0.0).then_inc(*step_v.one())
            chain(dve, step_v, dve.reciprocal(arg, cube))
            chain(dve, step_v, dve.tensor_tensor(out=cube, in0=arg, in1=dots, op=ALU.mult))
            chain(dve, step_v, dve.tensor_tensor(out=dots, in0=cube, in1=probs_g[:, t, :], op=ALU.mult))

        def store(self, dve, t):
            acc, other = heads[:, 0:DM], heads[:, DM:2 * DM]
            chain(dve, step_v, dve.tensor_tensor(out=acc, in0=acc, in1=other, op=ALU.add))
            chain(dve, step_v, dve.tensor_tensor(out=acc, in0=acc, in1=gate_row(1, t // 2), op=ALU.mult))
            chain(dve, step_v, dve.tensor_tensor(out=stream[:, t, :], in0=stream[:, t, :], in1=acc, op=ALU.add))

    def experts_stage(s, gelu_row, guests):
        base, stage0, picked0 = rows_used.total, staged.total, 2 * gather_count[0]
        gather_count[0] += 1

        def turn_of_ring(pool, t, which, half, row0, turn, i):
            reg = i is not None
            pool.wait_ge(rows_used.sem, i * 16 + (row0 - ROWS + 1) if reg else row0 - ROWS + 1)
            src = picks_u[:, t, bass.ds(i * 16 + 8 * half, 8)] if reg else picks_u[:, t, 8 * half:8 * half + 8]
            pool.tensor_copy(index_stage[:, 8 * half:8 * half + 8], src).then_inc(staged.sem, 1)
            for u in range(ROWS):
                if u == 0:
                    pool.wait_ge(staged.sem, i * 2 + (turn + 1) if reg else turn + 1)
                pool.wait_ge(rows_used.sem, i * 16 + (row0 + u - ROWS + 1) if reg else row0 + u - ROWS + 1)
                pool.sem_inc(*admitted.one())
                pool.indirect_dma_start(
                    out=row_slots[u], out_offset=None, in_=tables_dram[which],
                    in_offset=bass.IndirectOffsetOnAxis(ap=index_stage[:, 8 * half + u:8 * half + u + 1], axis=0),
                ).then_inc(gathered[u].sem, 16)

        def gpsimd(pool):
            for ph in range(4):
                t, which = 2 * s + ph // 2, ph % 2
                row0, turn0 = base + ph * PICKS, stage0 + ph * PICKS // ROWS
                if which == 0:
                    pool.wait_ge(picked.sem, picked0 + t % 2 + 1)
                for half in range(2):
                    turn_of_ring(pool, t, which, half, row0 + 8 * half, turn0 + half, None)
                with pool.Fori(1, PICKS // 16) as i:
                    for half in range(2):
                        turn_of_ring(pool, t, which, half, row0 + 8 * half, turn0 + half, i)

        with nc.Block() as block:
            work = RowWork(block, s, [gelu_row[:, PICKS * i:PICKS * i + PICKS] for i in range(6)])
            block.gpsimd(gpsimd)
            host[0] = work
            for guest in guests:
                guest()
            host[0] = None

            @block.vector
            def _(dve):
                work.finish(dve)

            @block.sync
            def _(sp):
                issue_loads(sp)
        rows_used.total += PICKS * 4
        gathers_done[0] += 1
        staged.total += PICKS * 4 // ROWS

    def turn_heads(s, tiles):
        q_t, k_t = heads[:, 2048:3072].rearrange("p (c t) -> p c t", c=4), heads[:, 3072:3584]
        groups = []
        for t in tiles:
            j = t - 2 * s
            if j < 2:
                groups.append(([mixed_v[:, t, c * P:c * P + P] for c in range(4)],
                               [(0, 512, q_t[:, :, j * P:j * P + P], HD ** -0.5)]))
            groups.append(([mixed_v[:, t, 512:640]], [(0, 128, k_t[:, j * P:j * P + P], 1.0)]))
        turn_stage(groups)

    def first_attention(s):
        q_t, k_t = heads[:, 2048:3072].rearrange("p (c t) -> p c t", c=4), heads[:, 3072:3584]
        tiles = (2 * s, 2 * s + 1)
        key_tiles = [0, 1, 2, 3] if s == 0 else [2, 3]

        def values(k, half):
            if k < 2:
                return proj1[:, k, 1152 + 64 * half:1216 + 64 * half]
            return context_kv[:, k - 2, 128 + 64 * half:192 + 64 * half]

        units = []
        for t in tiles:
            for half in range(2):
                for c in range(4):
                    rows = slice(64 * half, 64 * half + 64)
                    span = slice((t % 2) * P, (t % 2) * P + P)
                    units.append(dict(
                        keys=P * len(key_tiles), scores=[(q_t[rows, c, span], k_t[rows, 0:P * len(key_tiles)])],
                        outputs=[dict(values=lambda k, half=half: values(k, half), p0=64 * half, np=64, c0=0, w=128,
                                      turned=True, dst=attn_t[s][rows, c, span])]))
        wide = P * len(key_tiles)
        attention_stage(units, sims_area[:, 0:7 * wide], wide)

    cos1 = tables[:, 3328:3456].rearrange("p (t d) -> p t d", t=2)
    sin1 = tables[:, 3456:3584].rearrange("p (t d) -> p t d", t=2)

    def attention_base(s):
        def base(t):
            if s == 0 and t >= 2:
                return context_kv[:, t - 2, 0:128]
            return proj1[:, t % 2, 512:1152]
        return base

    def input_norm(l, tiles, place=None):
        norm_stage(tiles, lambda k, t: first_gain(0, k, t // 2), lambda k, t: first_shift(0, k, t // 2), place)

    def project(l, s, with_context, place):
        tiles = [2 * s, 2 * s + 1]

        def lhs(k, t):
            return normed(k, t) if place is None else turned_s[place][:, k, (t % 2) * P:(t % 2) * P + P]

        def store(t, b):
            if s == 0 and t >= 2:
                return context_kv[:, t - 2, :]
            return proj1[:, t % 2, 512 * b:min(512 * b + 512, 1280)]

        linear_stage([([("w_in", l, b)], "rows", tiles + [2, 3] if b == 2 and with_context else tiles, lhs,
                       lambda t, b=b: store(t, b)) for b in range(3)])

    def mix_whole(l, s):
        tiles = [0, 1, 2, 3] if s == 0 else [2, 3]
        return [lambda: project(l, s, s == 0, None), lambda: branch_stage(l, s),
                lambda: rotate_stage(l, tiles, attention_base(s), cos1, sin1, 2, True),
                lambda: turn_heads(s, tiles), lambda: first_attention(s), lambda: merge_stage(l, s)]

    def mix_early(l):
        return [lambda: input_norm(l, [0, 1], 1), lambda: project(l, 0, False, 1), lambda: branch_stage(l, 0),
                lambda: rotate_stage(l, [0, 1], attention_base(0), cos1, sin1, 2, True),
                lambda: turn_heads(0, [0, 1]), lambda: merge_stage(l, 0, "early", 1)]

    def mix_late(l):
        return [lambda: input_norm(l, [2, 3]),
                lambda: linear_stage([([("w_in_kv", l)], "rows", [2, 3], normed, lambda t: context_kv[:, t - 2, :])]),
                lambda: rotate_stage(l, [2, 3], attention_base(0), cos1, sin1, 2, True),
                lambda: turn_heads(0, [2, 3]), lambda: first_attention(0), lambda: merge_stage(l, 0, "late")]

    def to_keys(l, s):
        tiles = [2 * s, 2 * s + 1]
        return [lambda: turn_mixed(s, HALVED),
                lambda: linear_stage([([("w_out", l, b)], "rows", tiles, normed, ("add", lambda t: gate_row(0, s), 512 * b))
                                      for b in range(2)]),
                lambda: norm_stage(tiles, lambda k, t: first_gain(1, k, s), lambda k, t: first_shift(1, k, s)),
                lambda: turn_back(s), lambda: keys_stage(l, s)]

    def first_block():
        ada_stage(0)
        input_norm(0, [0, 1, 2, 3])
        for stage in mix_whole(0, 0) + to_keys(0, 0) + [lambda: topk_stage(0, 0)]:
            stage()
        experts_stage(0, gate_row(0, 0), [lambda: topk_stage(0, 1)] + mix_whole(0, 1) + to_keys(0, 1)
                      + [lambda: topk_stage(0, 2)])
        experts_stage(1, gate_row(0, 1), [lambda: topk_stage(0, 3), lambda: ada_stage(1)] + mix_early(1))
        for stage in mix_late(1) + to_keys(1, 0) + [lambda: topk_stage(1, 0)]:
            stage()
        experts_stage(0, gate_row(0, 1), [lambda: topk_stage(1, 1)])

    upper = tables[:, 0:512].rearrange("p (k t) -> p k t", k=2)
    band = tables[:, 512:1024].rearrange("p (t k) -> p t k", t=2)
    causal = tables[:, 1024:1536].rearrange("p (t k) -> p t k", t=2)
    causal_t = tables[:, 1536:2048].rearrange("p (t k) -> p t k", t=2)
    cos2 = tables[:, 2048:2176].rearrange("p (t d) -> p t d", t=2)
    sin2 = tables[:, 2176:2304].rearrange("p (t d) -> p t d", t=2)
    sinks = [small_rows[:, 8 * l:8 * l + 8] for l in range(2)]
    forget_bias = [small_rows[:, 16 + 8 * l:24 + 8 * l] for l in range(2)]
    dt_bias = [small_rows[:, 32 + 16 * l:48 + 16 * l] for l in range(2)]
    a_log = [small_rows[:, 64 + 16 * l:80 + 16 * l] for l in range(2)]
    d_skip = [small_rows[:, 96 + 16 * l:112 + 16 * l] for l in range(2)]
    raw_conv = gate_rows[:, 0:12 * 259].rearrange("p (c t) -> p c t", c=12)
    conv = lifted[:, 0:3072].rearrange("p (c t) -> p c t", c=12)
    dt_raw = soft[:, 16:48].rearrange("p (t h) -> p t h", t=2)
    softened = soft[:, 48:96].rearrange("p (t h) -> p t h", t=2)
    cum_f = soft[:, 96:112].rearrange("p (t h) -> p t h", t=2)
    decays = soft[:, 112:144].rearrange("p (t h) -> p t h", t=2)
    neg_acs = soft[:, 144:176].rearrange("p (t h) -> p t h", t=2)
    y_v = mixed.rearrange("p (t d) -> p t d", t=2)

    def load_second_stage():
        open_stage()

        def sync(sp):
            sp.dma_start(tables[:, 0:2304], io["second"]).then_inc(*loaded.one(16))
            for t in range(2):
                sp.dma_start(stream[:, 2 + t, :], io["mem_2"][0, t * P:t * P + P, :]).then_inc(*loaded.one(16))
            sp.wait_ge(*loaded.now())

        run_stage(sync=sync)

    def softplus_stage(l):
        open_stage()
        z = soft[:, 176:224].rearrange("p (t h) -> p t h", t=2)
        e, r, s, acc = (soft[:, 224 + 48 * i:272 + 48 * i].rearrange("p (t h) -> p t h", t=2) for i in range(4))
        a_row = soft[:, 416:432]

        def bc(v, n):
            return v.unsqueeze(1).broadcast_to([P, 2, n])

        def vector(dve):
            def step(ins):
                chain(dve, step_v, ins)
            dve.wait_ge(*ready_a.at(1))
            step(dve.tensor_scalar(a_row, a_row, -1.0, None, ALU.mult))
            step(dve.tensor_tensor(out=z[:, :, 0:8], in0=proj2[:, :, 2816:2824], in1=bc(forget_bias[l], 8), op=ALU.add))
            step(dve.tensor_scalar(z[:, :, 0:8], z[:, :, 0:8], -1.0, None, ALU.mult))
            step(dve.tensor_tensor(out=z[:, :, 8:24], in0=dt_raw, in1=bc(dt_bias[l], 16), op=ALU.add))
            step(dve.tensor_scalar(r, z, -1.0, None, ALU.mult))
            dve.tensor_tensor(out=e, in0=z, in1=r, op=ALU.min).then_inc(*ready_v.one())
            dve.wait_ge(*ready_a.at(2))
            step(dve.tensor_scalar(r, e, 2.0, None, ALU.add))
            step(dve.reciprocal(s, r))
            step(dve.tensor_tensor(out=r, in0=e, in1=s, op=ALU.mult))
            step(dve.tensor_tensor(out=s, in0=r, in1=r, op=ALU.mult))
            step(dve.tensor_scalar(acc, s, 1.0 / 19, None, ALU.mult))
            for odd in (17, 15, 13, 11, 9, 7, 5, 3):
                step(dve.scalar_tensor_tensor(out=acc, in0=acc, scalar=1.0 / odd, in1=s, op0=ALU.add, op1=ALU.mult))
            step(dve.scalar_tensor_tensor(out=acc, in0=acc, scalar=1.0, in1=r, op0=ALU.add, op1=ALU.mult))
            step(dve.tensor_scalar(acc, acc, 2.0, None, ALU.mult))
            step(dve.scalar_tensor_tensor(out=softened, in0=z, scalar=0.0, in1=acc, op0=ALU.max, op1=ALU.add))
            step(dve.tensor_scalar(z[:, :, 0:8], softened[:, :, 0:8], -1.0, None, ALU.mult))
            dve.tensor_tensor(out=decays, in0=softened[:, :, 8:24], in1=bc(a_row, 16), op=ALU.mult).then_inc(*ready_v.one())
            dve.wait_ge(*products.at(1))
            step(dve.tensor_copy(cum_f, psum[:, 0, 0:16].rearrange("p (t h) -> p t h", t=2)))
            step(dve.tensor_scalar(neg_acs, psum[:, 1, 0:32].rearrange("p (t h) -> p t h", t=2), -1.0, None, ALU.mult))

        def scalar(act):
            act.activation(a_row, a_log[l], ACT.Exp).then_inc(*ready_a.one())
            act.wait_ge(*ready_v.at(1))
            act.activation(e, e, ACT.Exp).then_inc(*ready_a.one())

        def tensor(pe):
            pe.wait_ge(*ready_v.at(2))
            for bank, src, n in ((0, z[:, :, 0:8], 8), (1, decays, 16)):
                for t in range(2):
                    for k in range(2):
                        mm = pe.matmul(psum[:, bank, n * t:n * t + n], upper[:, k, t * P:t * P + P], src[:, k, :],
                                       start=k == 0, stop=k == 1)
            mm.then_inc(*products.one())

        run_stage(tensor, vector, scalar)

    def second_attention(l):
        qa_t = heads[:, 0:1024].rearrange("p (c t) -> p c t", c=4)
        ka_t = heads[:, 1024:1280]
        qb_t = heads[:, 1280:2304].rearrange("p (c t) -> p c t", c=4)
        kb_t = heads[:, 2304:3328].rearrange("p (c t) -> p c t", c=4)
        groups = []
        for t in range(2):
            span = slice(t * P, t * P + P)
            groups.append(([mixed_v[:, t, c * P:c * P + P] for c in range(4)], [(0, 512, qa_t[:, :, span], HD ** -0.5)]))
            groups.append(([mixed_v[:, t, 512:640]], [(0, 128, ka_t[:, span], 1.0)]))
            groups.append(([proj2[:, t, 1280 + c * P:1408 + c * P] for c in range(4)], [(0, 512, qb_t[:, :, span], HD ** -0.5)]))
            groups.append(([proj2[:, t, 1792 + c * P:1920 + c * P] for c in range(4)], [(0, 512, kb_t[:, :, span], 1.0)]))
        turn_stage(groups)
        units = []
        for t in range(2):
            seen = P * (t + 1)
            for half in range(2):
                for c in range(4):
                    rows = slice(64 * half, 64 * half + 64)
                    h = 4 * half + c
                    units.append(dict(
                        keys=seen, scores=[(qa_t[rows, c, t * P:t * P + P], ka_t[rows, 0:seen])], mask=band[:, t, 0:seen],
                        sink=sinks[l][:, h:h + 1],
                        outputs=[dict(values=lambda k, half=half: proj2[:, k, 640 + 64 * half:704 + 64 * half],
                                      p0=0, np=128, c0=0, w=64, turned=False, dst=y_v[:, t, h * 64:h * 64 + 64])]))
        for t in range(2):
            seen = P * (t + 1)
            for h in range(8):
                rows = slice(64 * (h % 2), 64 * (h % 2) + 64)
                scores = [(qb_t[rows, h // 2, t * P:t * P + P], kb_t[rows, h // 2, 0:seen])]
                scores += [(softened[:, k, h:h + 1].broadcast_to([P, P]), upper[:, k, 0:seen]) for k in range(t + 1)]
                units.append(dict(
                    keys=seen, scores=scores, mask=causal[:, t, 0:seen], shift=cum_f[:, t, h:h + 1],
                    outputs=[dict(values=lambda k, h=h: proj2[:, k, 2304 + 64 * h:2368 + 64 * h],
                                  p0=0, np=128, c0=0, w=64, turned=False, dst=y_v[:, t, 512 + h * 64:576 + h * 64])]))
        attention_stage(units, turned[:, 0:1792], 256)

    def conv_stage(l):
        open_stage()
        cw, cb = where["conv_w_2"][0] + 48 * l, where["conv_b_2"][0] + 12 * l
        tanh = [heads[:, 256 * i:256 * i + 256] for i in range(4)]

        def vector(dve):
            chain(dve, step_v, dve.memset(raw_conv[:, :, 0:3], 0.0))
            for c in range(12):
                dst = conv[:, c, :]
                chain(dve, step_v, dve.tensor_scalar(dst, raw_conv[:, c, 0:256], columns[:, cw + c:cw + c + 1],
                                                     columns[:, cb + c:cb + c + 1], ALU.mult, ALU.add))
                for k in range(1, 4):
                    ins = dve.scalar_tensor_tensor(out=dst, in0=raw_conv[:, c, k:k + 256],
                                                   scalar=columns[:, cw + 12 * k + c:cw + 12 * k + c + 1],
                                                   in1=dst, op0=ALU.mult, op1=ALU.add)
                    if k < 3:
                        chain(dve, step_v, ins)
                ins.then_inc(*ready_v.one())
                if c >= 2:
                    finish(dve, c - 2)
            finish(dve, 10)
            finish(dve, 11)

        def finish(dve, c):
            dve.wait_ge(*ready_a.at(c + 1))
            dve.wait_ge(*ready_v.at(c + 1))
            dve.scalar_tensor_tensor(out=conv[:, c, :], in0=tanh[c % 4], scalar=1.0, in1=conv[:, c, :],
                                     op0=ALU.add, op1=ALU.mult).then_inc(*read_v.one())

        def scalar(act):
            for c in range(12):
                act.wait_ge(*ready_v.at(c + 1))
                if c >= 4:
                    act.wait_ge(*read_v.at(c - 3))
                act.activation(tanh[c % 4], conv[:, c, :], ACT.Tanh).then_inc(*ready_a.one())

        run_stage(vector=vector, scalar=scalar)

    x_rows = turned[:, 0:2048].rearrange("p (t d) -> p t d", t=2)
    x_dt = turned[:, 2048:4096].rearrange("p (t d) -> p t d", t=2)

    def ssm_stage(l):
        open_stage()
        cb = heads[:, 0:768].rearrange("p (g n) -> p g n", g=2)
        decay = [heads[:, 768 + 384 * i:1152 + 384 * i] for i in range(2)]
        kernel_ = [heads[:, 1536 + 384 * i:1920 + 384 * i] for i in range(2)]

        def tensor(pe):
            for g in range(2):
                pe.matmul(psum[:, g, 0:256], conv[:, 8 + g, 0:128], conv[:, 10 + g, :], start=True, stop=True)
                pe.matmul(psum[:, g, 256:384], conv[:, 8 + g, 128:256], conv[:, 10 + g, 128:256],
                          start=True, stop=True).then_inc(*products.one())
            for h in range(17):
                if h < 16:
                    bank = 2 + h % 2
                    if h >= 2:
                        pe.wait_ge(*ready_a.at(h - 1))
                    for o, l0, n, s in ((0, 0, 256, 0), (256, 128, 128, 1)):
                        for k in range(2):
                            pe.matmul(psum[:, bank, o:o + n], decays[:, k, h:h + 1].broadcast_to([P, P]),
                                      upper[:, k, l0:l0 + n], start=k == 0, stop=False)
                        mm = pe.matmul(psum[:, bank, o:o + n], ident, causal_t[:, s, l0:l0 + n], start=False, stop=True)
                    mm.then_inc(*products.one())
                if h >= 1:
                    j = h - 1
                    m = kernel_[j % 2]
                    pe.wait_ge(*ready_v.at(j + 1))
                    if j >= 2:
                        pe.wait_ge(*read_v.at(2 + j - 1))
                    xs = [x_dt[:, t, j * 64:j * 64 + 64] for t in range(2)]
                    bank = 4 + j % 2
                    pe.matmul(psum[:, bank, 0:64], m[:, 0:128], xs[0], start=True, stop=True)
                    pe.matmul(psum[:, bank, 64:128], m[:, 128:256], xs[0], start=True, stop=False)
                    pe.matmul(psum[:, bank, 64:128], m[:, 256:384], xs[1], start=False, stop=True).then_inc(*products.one())

        def vector(dve):
            chain(dve, step_v, dve.tensor_tensor(
                out=x_dt.rearrange("p t (h d) -> p t h d", d=64), in0=x_rows.rearrange("p t (h d) -> p t h d", d=64),
                in1=softened[:, :, 8:24].unsqueeze(3).broadcast_to([P, 2, 16, 64]), op=ALU.mult))
            for g in range(2):
                dve.wait_ge(*products.at(g + 1))
                dve.tensor_copy(cb[:, g, :], psum[:, g, 0:384]).then_inc(*read_v.one())
            dve.wait_ge(*read_v.now())
            for h in range(17):
                if h < 16:
                    dve.wait_ge(*ready_a.at(h + 1))
                    if h >= 2:
                        dve.wait_ge(*products.at(2 + 2 * (h - 2) + 3))
                    dve.tensor_tensor(out=kernel_[h % 2], in0=decay[h % 2], in1=cb[:, h // 8, :], op=ALU.mult)\
                       .then_inc(*ready_v.one())
                if h >= 1:
                    j = h - 1
                    dve.wait_ge(*products.at(2 + (2 * j + 3 if j < 15 else 32)))
                    for t in range(2):
                        ins = dve.scalar_tensor_tensor(
                            out=y_v[:, t, 1024 + j * 64:1088 + j * 64], in0=x_rows[:, t, j * 64:j * 64 + 64],
                            scalar=d_skip[l][:, j:j + 1], in1=psum[:, 4 + j % 2, 64 * t:64 * t + 64],
                            op0=ALU.mult, op1=ALU.add)
                    ins.then_inc(*read_v.one())

        def scalar(act):
            for h in range(16):
                act.wait_ge(*products.at(2 + (1 if h == 0 else 2 * h)))
                if h >= 2:
                    act.wait_ge(*ready_v.at(h - 1))
                for o, n, s in ((0, 256, 0), (256, 128, 1)):
                    ins = act.activation(decay[h % 2][:, o:o + n], psum[:, 2 + h % 2, o:o + n], ACT.Exp,
                                         bias=neg_acs[:, s, h:h + 1])
                ins.then_inc(*ready_a.one())

        run_stage(tensor, vector, scalar)

    def gating_stage():
        open_stage()
        tanh = turned.rearrange("p (t d) -> p t d", t=2)
        spans = ((0, 512, 768), (512, 2048, 2824))

        def scalar(act):
            for t in range(2):
                for y0, y1, g0 in spans:
                    act.activation(tanh[:, t, y0:y1], proj2[:, t, g0:g0 + y1 - y0], ACT.Tanh, scale=0.5).then_inc(*ready_a.one())
            for t in range(2):
                act.wait_ge(*ready_v.at(t + 1))
                act.activation(tanh[:, t, 1024:2048], y_v[:, t, 1024:2048], ACT.Square,
                               accum_out=stats[:, t:t + 1]).then_inc(*ready_a.one())

        def vector(dve):
            for t in range(2):
                for i, (y0, y1, g0) in enumerate(spans):
                    g = proj2[:, t, g0:g0 + y1 - y0]
                    dve.wait_ge(*ready_a.at(2 * t + i + 1))
                    chain(dve, step_v, dve.scalar_tensor_tensor(out=g, in0=tanh[:, t, y0:y1], scalar=1.0, in1=g,
                                                                op0=ALU.add, op1=ALU.mult))
                    ins = dve.scalar_tensor_tensor(out=y_v[:, t, y0:y1], in0=g, scalar=HALVED, in1=y_v[:, t, y0:y1],
                                                   op0=ALU.mult, op1=ALU.mult)
                ins.then_inc(*ready_v.one())
            dve.wait_ge(*ready_a.at(6))
            inverse_root(dve, stats[:, 16:18], stats[:, 0:2], stats[:, 32:38], DM)
            for t in range(2):
                dve.tensor_scalar(y_v[:, t, 1024:2048], y_v[:, t, 1024:2048], stats[:, 16 + t:17 + t], None,
                                  ALU.mult).then_inc(*step_v.one())

        run_stage(vector=vector, scalar=scalar)

    def second_layer(l):
        norm_stage([0, 1], lambda k, t: column("norm_mix_w_2", 8 * l + k), None)
        linear_stage(
            [([("w_in2", l, b)], "rows", [0, 1], normed,
              lambda t, b=b: proj2[:, t, 512 * b:min(512 * b + 512, W2_TOKEN_COLS)]) for b in range(9)]
            + [([("conv", l, b)], "cols", [0, 1, 2, 3], lambda k, _: turned_s[0][:, k, :],
                lambda c, b=b: raw_conv[:, 4 * b + c, 3:259]) for b in range(3)]
            + [([("dt", l)], "rows", [0, 1], normed, lambda t: dt_raw[:, t, :])])
        rotate_stage(l, [0, 1], lambda t: proj2[:, t, 0:640], cos2, sin2, 1, False)
        softplus_stage(l)
        second_attention(l)
        conv_stage(l)
        turn_stage([([conv[:, 4 * g + q, t * P:t * P + P] for q in range(4)],
                     [(0, 512, x_rows[:, t, 512 * g:512 * g + 512], 1.0)]) for t in range(2) for g in range(2)])
        ssm_stage(l)
        gating_stage()
        y_t = lifted.rearrange("p (k t) -> p k t", k=16)
        groups = []
        for t in range(2):
            for g in range(4):
                srcs = [y_v[:, t, (4 * g + q) * P:(4 * g + q + 1) * P] for q in range(4)]
                if g < 2:
                    outs = [(0, 512, y_t[:, 4 * g:4 * g + 4, t * P:t * P + P], 1.0)]
                else:
                    outs = [(q * P, P, y_t[:, 4 * g + q, t * P:t * P + P], column("ssm_norm_w_2", 8 * l + 4 * (g - 2) + q))
                            for q in range(4)]
                groups.append((srcs, outs))
        turn_stage(groups)
        linear_stage([([("w_out2", l, b, 0), ("w_out2", l, b, 1)], "rows", [0, 1],
                       lambda k, t: y_t[:, k, t * P:t * P + P], ("add", None, 512 * b)) for b in range(2)])
        norm_stage([0, 1, 2, 3], lambda k, t: column("norm_xq_w_2" if t < 2 else "norm_mem_w_2", 8 * l + k), None)
        q_t = heads[:, 0:2048].rearrange("p (c t) -> p c t", c=8)
        k_t = heads[:, 2048:4096].rearrange("p (c t) -> p c t", c=8)
        v_m = proj[:, 0:2048].rearrange("p (t n) -> p t n", t=2)
        o_t = lifted[:, 0:2048].rearrange("p (c t) -> p c t", c=8)
        linear_stage(
            [([("w_mq_2", l, b)], "cols", [0, 1, 2, 3], lambda k, _: turned_s[0][:, k, :],
              lambda c, b=b: (q_t[:, 4 * b + c, :], 256 ** -0.5)) for b in range(2)]
            + [([("w_mk_2", l, b)], "cols", [0, 1, 2, 3], lambda k, _: turned_s[1][:, k, :],
                lambda c, b=b: k_t[:, 4 * b + c, :]) for b in range(2)]
            + [([("w_mv_2", l, b)], "rows", [2, 3], normed, lambda t, b=b: v_m[:, t - 2, 512 * b:512 * b + 512])
               for b in range(2)])
        units = []
        for t in range(2):
            for h in range(4):
                units.append(dict(
                    keys=256, scores=[(q_t[:, 2 * h + j, t * P:t * P + P], k_t[:, 2 * h + j, :]) for j in range(2)],
                    outputs=[dict(values=lambda k, c=2 * h + j: v_m[:, k, c * P:c * P + P],
                                  p0=0, np=128, c0=128 * j, w=128, turned=True, dst=o_t[:, 2 * h + j, t * P:t * P + P])
                             for j in range(2)]))
        attention_stage(units, turned[:, 0:1792], 256)
        linear_stage([([("w_mo_2", l, b)], "rows", [0, 1], lambda k, t: o_t[:, k, t * P:t * P + P],
                       ("add", None, 512 * b)) for b in range(2)])

    def final_stage():
        open_stage()
        gain = lifted[:, 0:DM]

        def sync(sp):
            sp.dma_start(gain, io["final_norm_w_2"].rearrange("(a d) -> a d", a=1).broadcast_to([P, DM]))\
              .then_inc(*loaded.one(16))
            for t in range(2):
                sp.wait_ge(*ready_v.at(t + 1))
                sp.dma_start(out[0, t * P:t * P + P, :], mixed_v[:, t, :]).then_inc(*stored.one(16))
            sp.wait_ge(*stored.now())

        def scalar(act):
            for t in range(2):
                act.activation(mixed_v[:, t, :], stream[:, t, :], ACT.Square,
                               accum_out=stats[:, t:t + 1]).then_inc(*ready_a.one())

        def vector(dve):
            dve.wait_ge(*ready_a.at(2))
            inverse_root(dve, stats[:, 16:18], stats[:, 0:2], stats[:, 32:38], DM)
            dve.wait_ge(*loaded.at(16))
            for t in range(2):
                dve.scalar_tensor_tensor(out=mixed_v[:, t, :], in0=stream[:, t, :], scalar=stats[:, 16 + t:17 + t],
                                         in1=gain, op0=ALU.mult, op1=ALU.mult).then_inc(*ready_v.one())

        run_stage(vector=vector, scalar=scalar, sync=sync)

    run_stage()
    first_block()
    if stop == ("first", 1):
        return
    load_second_stage()
    for l in range(DEPTH):
        second_layer(l)
        if stop == ("second", l):
            return
    final_stage()


_INS = ['x', 'c', 'ctx', 'c_ctx', 'ada_w', 'ada_b', 'norm_mix', 'w_in', 'fourier_w', 'pool_w', 'pool_scale',
        'pool_proj', 'q_norm', 'k_norm', 'attn_proj', 'w_out', 'norm_ffn', 'peer_wq', 'peer_keys', 'peer_u', 'peer_v',
        'mem_2', 'norm_mix_w_2', 'w_in_2', 'b_forget_2', 'swa_sinks_2', 'conv_w_2', 'conv_b_2', 'dt_bias_2',
        'a_log_2', 'd_skip_2', 'ssm_norm_w_2', 'w_out_2', 'norm_xq_w_2', 'norm_mem_w_2', 'w_mq_2', 'w_mk_2',
        'w_mv_2', 'w_mo_2', 'final_norm_w_2']
_OUTS = [((1, 256, 1024), 'float32')]


def kernel(**inputs):
    import numpy as _np
    import concourse.bacc as _bacc
    from concourse import mybir as _mybir
    from concourse.bass_utils import run_bass_kernel_spmd as _run

    nc = _bacc.Bacc("TRN2", target_bir_lowering=False, num_devices=1)
    arrays, io = {}, {}
    named = {name: inputs[name] for name in _INS}
    named.update(zip(("common", "first", "second"), shape_constants()))
    for name, a in named.items():
        a = _np.ascontiguousarray(a)
        arrays[f"in_{name}_dram"] = a
        io[name] = nc.dram_tensor(f"in_{name}_dram", a.shape, _mybir.dt.from_np(a.dtype), kind="ExternalInput").ap()
    outs = [nc.dram_tensor(f"out_{i}_dram", shape, _mybir.dt.from_np(_np.dtype(dtype)), kind="ExternalOutput").ap()
            for i, (shape, dtype) in enumerate(_OUTS)]
    build_kernel(nc, io, outs[0])
    r = _run(nc, [arrays], core_ids=[0])
    return r.results[0]["out_0_dram"]
```

```python
from contextlib import ExitStack

import numpy as np

import concourse.bass as bass
from concourse import mybir
from concourse.alu_op_type import AluOpType as ALU

ACT = mybir.ActivationFunctionType
F32 = mybir.dt.float32
U32 = mybir.dt.uint32
I32 = mybir.dt.int32
AX = mybir.AxisListType.X

P = 128
DM = 1024
KD = DM // P
SEQ = 256
DEPTH = 2
HD = 64
NORM_EPS = 1e-6
MASKED = -1e30
RING = 3
SLOT = 4096
TOPK = 16
PEER_HEADS = 8
PICKS = PEER_HEADS * TOPK
EXPERTS = 128 * 128
ROWS = 8
IN_COLS = 4352
OFF_G = 1280
HALVED = 0.5
LN2_HIGH = 0.693359375
LN2_LOW = float(np.log(2.0)) - LN2_HIGH
W2_TOKEN_COLS = 4360
W2_COLS = 5912
W2_FIRST, W2_REST = [0, 1, 5], [2, 3, 4, 6, 7, 8]


class Signal:

    def __init__(self, nc, name):
        self.sem = nc.alloc_semaphore(name)
        self.total = 0
        self.base = 0

    def one(self, by=1):
        self.total += by
        return self.sem, by

    def at(self, n):
        return self.sem, self.base + n

    def now(self):
        return self.sem, self.total


def window_mean(win):
    m = np.zeros((SEQ, SEQ), np.float64)
    for t in range(SEQ):
        lo, hi = max(t - win // 2, 0), min(t + win - win // 2, SEQ)
        m[lo:hi, t] = 1.0 / (hi - lo)
    return m - np.eye(SEQ)


def tiled(m):
    return m.reshape(2, P, -1).transpose(1, 0, 2).reshape(P, -1)


def rotary(angles, axes):
    cos, sin = np.cos(angles), np.sin(angles)
    c = np.concatenate([cos, cos], -1).reshape(SEQ, -1)
    s = np.concatenate([-sin, sin], -1).reshape(SEQ, -1)
    return c, s


def shape_constants():
    tok = np.arange(SEQ)
    common = np.concatenate([np.eye(P), np.ones((P, P)), np.tile(np.arange(16), (P, 1))], 1)
    ang = 2 * np.pi * (np.outer(tok, tok) % SEQ) / SEQ
    c_len, s_len = np.cos(ang) / np.sqrt(SEQ), np.sin(ang) / np.sqrt(SEQ)
    ch = np.arange(64)
    ang = 2 * np.pi * (np.outer(ch, ch) % 64) / 64
    two = np.eye(2)
    c_ch, s_ch = np.kron(two, np.cos(ang) / 8), np.kron(two, -np.sin(ang) / 8)
    pools = np.concatenate([tiled(window_mean(w)) for w in (2, 4, 8, 16)], 1)
    inv = (10000.0 ** (-np.arange(16, dtype=np.float32) / 16)).astype(np.float32)
    row = (tok // 64).astype(np.float32)[:, None] * inv
    col = (tok % 64).astype(np.float32)[:, None] * inv
    c1, s1 = rotary(np.stack([row, col], 1), 2)
    first = np.concatenate([tiled(c_len), tiled(s_len), c_ch, s_ch, pools, tiled(c1), tiled(s1)], 1)
    upper = (tok[:, None] <= tok[None, :]).astype(np.float64)
    rel = tok[:, None] - tok[None, :]
    band = np.where((rel >= 0) & (rel < 128), 0.0, MASKED)
    causal = np.where(rel >= 0, 0.0, MASKED)
    inv = (1.0 / (10000.0 ** (np.arange(0, 64, 2, dtype=np.float32) / 64))).astype(np.float32)
    c2, s2 = rotary((tok.astype(np.float32)[:, None] * inv)[:, None, :], 1)
    second = np.concatenate([tiled(upper), tiled(band), tiled(causal), tiled(causal.T), tiled(c2), tiled(s2)], 1)
    return [np.ascontiguousarray(a, np.float32) for a in (common, first, second)]


def build_kernel(nc, io, out):
    ctx = ExitStack()

    def area(name, cols, dt=F32):
        return nc.alloc_sbuf_tensor(name, [P, cols], dt)[:, :]

    ring = area("ring", 2 * SLOT)
    stream = area("stream", 4 * DM).rearrange("p (t d) -> p t d", t=4)
    turned = area("turned", KD * 512)
    turned_s = [turned[:, 2048 * s:2048 * s + 2048].rearrange("p (k t) -> p k t", k=KD) for s in range(2)]
    proj = area("proj", 9216)
    mixed = area("mixed", 4 * DM)
    mixed_v = mixed.rearrange("p (t d) -> p t d", t=4)
    lifted = area("lifted", 4096)
    gate_rows = area("gate_rows", 4 * DM)
    heads = area("heads", 4096)
    tables = area("tables", 3584)
    common = area("common", 272)
    columns = area("columns", 352)
    lent = area("lent", SLOT)
    row_packs = mixed[:, 0:384].rearrange("p (a b) -> p a b", a=3)
    head_gain = area("head_gain", 256)
    small_rows = area("small_rows", 160)
    pool_blocks = area("pool_blocks", 512)
    stats = area("stats", 64)
    silu_c = area("silu_c", 32)
    mods = area("mods", 96)
    norm_cols = area("norm_cols", 64)
    soft = area("soft", 512)
    psum = nc.alloc_psum_tensor("psum", [P, 8, 512], F32)

    ident, ones, iota16 = common[:, 0:128], common[:, 128:256], common[:, 256:272]

    def signal(name):
        return Signal(nc, name)

    products = signal("products")
    read_v, read_a = signal("read_v"), signal("read_a")
    step_v, step_a = signal("step_v"), signal("step_a")
    ready_v, ready_a, ready_g = signal("ready_v"), signal("ready_a"), signal("ready_g")
    packs_loaded = signal("packs_loaded")
    loaded = signal("loaded")
    stored = signal("stored")
    landed = [signal(f"landed{i}") for i in range(RING)]
    gathered = [signal(f"gathered{i}") for i in range(ROWS)]
    rows_used = signal("rows_used")
    staged = signal("staged")
    admitted = signal("admitted")
    picked = signal("picked")
    half_used = signal("half_used")
    meeting = signal("meeting")
    every = [products, read_v, read_a, step_v, step_a, ready_v, ready_a, ready_g, loaded, stored]

    def open_stage():
        for s in every:
            s.base = s.total

    def chain(eng, step, ins):
        ins.then_inc(*step.one())
        eng.wait_ge(*step.now())

    plan = []
    guest_loads = set()

    def merge_jobs(part):
        jobs = [(cb, br) for cb in range(2) for br in range(3)]
        if part == "late":
            return [(cb, br, False, True) for cb, br in jobs if br == 2]
        return [(cb, br, True, part == "all" or br < 2) for cb, br in jobs]

    def plan_block(key, w, c0, c1):
        plan.append((key, (c1 - c0), [(0, P, w[:, c0:c1].rearrange("(k p) n -> p k n", p=P))]))

    def plan_ada(l):
        for b in range(12):
            plan_block(("ada", l, b), io["ada_w"][l], 512 * b, 512 * b + 512)

    def plan_w_in(l):
        for b, (c0, c1) in enumerate(((0, 512), (512, 1024), (1024, 1280))):
            plan_block(("w_in", l, b), io["w_in"][l], c0, c1)

    def plan_merge(l, part):
        for cb, br, gates, branches in merge_jobs(part):
            c0 = 512 * cb
            if gates:
                g0 = OFF_G + br * DM + c0
                plan_block(("gate", l, cb, br), io["w_in"][l], g0, g0 + 512)
            if branches and br < 2:
                plan_block(("branch", l, cb, br), io["fourier_w" if br == 0 else "pool_proj"][l], c0, c0 + 512)
            elif branches:
                w = io["attn_proj"][l]
                plan.append((("branch", l, cb, br), 512,
                             [(64 * h, 64, w[256 * h:256 * h + 256, c0:c0 + 512].rearrange("(c d) n -> d c n", d=64))
                              for h in range(2)]))

    def plan_out(l):
        for b in range(2):
            plan_block(("w_out", l, b), io["w_out"][l], 512 * b, 512 * b + 512)
        plan.append((("keys", l), 128, [(0, P, io["peer_keys"][l].rearrange("h s n k -> n (h s) k"))]))
        for b in range(4):
            plan_block(("wq", l, b), io["peer_wq"][l], 512 * b, 512 * b + 512)

    def plan_second(l):
        w = io["w_in_2"][l]
        for b in range(3):
            plan_block(("conv", l, b), w, W2_TOKEN_COLS + 512 * b, W2_TOKEN_COLS + 512 * b + 512)
        plan_block(("dt", l), w, W2_COLS - 16, W2_COLS)
        for b in W2_FIRST + W2_REST:
            plan_block(("w_in2", l, b), w, 512 * b, min(512 * b + 512, W2_TOKEN_COLS))
        for b in range(2):
            for half in range(2):
                plan_block(("w_out2", l, b, half), io["w_out_2"][l][1024 * half:1024 * half + 1024, :],
                           512 * b, 512 * b + 512)
        plan_memory(l, ("w_mq_2", "w_mo_2"))

    def plan_memory(l, names):
        for name in names:
            for b in range(2):
                plan_block((name, l, b), io[name][l], 512 * b, 512 * b + 512)

    plan_ada(0)
    for _ in range(2):
        plan_w_in(0)
        if not guest_loads:
            plan_merge(0, "early")
            plan_merge(0, "late")
        else:
            plan_merge(0, "all")
        plan_out(0)
        if not guest_loads:
            first_guest = len(plan)
            guest_loads.add(first_guest)
    plan_ada(1)
    plan_w_in(1)
    plan_merge(1, "early")
    guest_loads.update(range(first_guest, len(plan)))
    after_gathers = [(len(plan), 2)]
    plan_block(("w_in_kv", 1), io["w_in"][1], 1024, 1280)
    plan_merge(1, "late")
    plan_out(1)
    first_guest = len(plan)
    for l in range(DEPTH):
        plan_memory(l, ("w_mk_2", "w_mv_2"))
    guest_loads.update(range(first_guest, len(plan)))
    after_gathers.append((len(plan), 3))
    plan_second(0)
    plan_second(1)
    used = []
    landing = []
    slot_of = []
    last_user = []
    turn = 0
    in_slot = [None] * RING
    for n_load, (_, _, load_parts) in enumerate(plan):
        turn = (turn + 1) % (2 if n_load in guest_loads else RING)
        slot_of.append(turn)
        last_user.append(in_slot[turn])
        in_slot[turn] = n_load
        landed[turn].one(16 * len(load_parts))
        landing.append(landed[turn].now())
    memory_kv = nc.dram_tensor("memory_kv", (DEPTH, P, 2, 2048), F32).ap()
    gathers_done = [0]
    issued = [0]

    def gathers_ahead(n):
        return max([count for first, count in after_gathers if n >= first], default=0)

    def slot_view(n):
        key, cols, parts = plan[n]
        k = parts[0][2].shape[1]
        place = lent if slot_of[n] == 2 else ring[:, slot_of[n] * SLOT:(slot_of[n] + 1) * SLOT]
        return place[:, 0:k * cols].rearrange("p (k n) -> p k n", k=k)

    def issue_loads(sp):
        while issued[0] < len(plan):
            n = issued[0]
            before = last_user[n]
            if before is not None and before >= len(used):
                return
            if slot_of[n] == 2 and gathers_ahead(n):
                if gathers_done[0] < gathers_ahead(n):
                    return
                sp.wait_ge(rows_used.sem, ROWS + gathers_ahead(n) * 4 * PICKS)
            if before is not None:
                sp.wait_ge(*used[before])
            for p0, np_, src in plan[n][2]:
                sp.dma_start(slot_view(n)[p0:p0 + np_, :, :], src).then_inc(landed[slot_of[n]].sem, 16)
            issued[0] += 1

    def take(pe, key):
        n = len(used)
        assert plan[n][0] == key, (plan[n][0], key)
        pe.wait_ge(*landing[n])
        return slot_view(n)

    def release(signal_=None):
        used.append((signal_ or products).now())

    gather_count = [0]
    host = [None]

    def run_vector(vector, dve):
        for us in vector(dve) or ():
            if host[0]:
                host[0].advance(dve, us)

    def run_stage(tensor=None, vector=None, scalar=None, sync=None):
        if host[0]:
            return run_guest(host[0].block, tensor, vector, scalar, sync)
        with nc.Block(no_gpsimd_drain=True) as block:
            if tensor:
                block.tensor(tensor)
            if vector:
                @block.vector
                def _(dve):
                    run_vector(vector, dve)
            if scalar:
                block.scalar(scalar)

            @block.sync
            def _(sp):
                if sync:
                    sync(sp)
                issue_loads(sp)

    def run_guest(block, tensor, vector, scalar, sync):
        start = meeting.total

        def meet(eng):
            eng.drain()
            eng.sem_inc(*meeting.one())
            eng.wait_ge(meeting.sem, start + 3)

        @block.tensor
        def _(pe):
            if tensor:
                tensor(pe)
            meet(pe)

        @block.vector
        def _(dve):
            if vector:
                run_vector(vector, dve)
            meet(dve)

        @block.scalar
        def _(act):
            if scalar:
                scalar(act)
            meet(act)

        @block.sync
        def _(sp):
            if sync:
                sync(sp)
            issue_loads(sp)

    def setup_stage():
        open_stage()
        packs = [
            [("norm_mix", 16), ("norm_ffn", 16), ("ada_b", 96)],
            [("c", 8), ("c_ctx", 8), ("norm_mix_w_2", 16), ("norm_xq_w_2", 16), ("norm_mem_w_2", 16),
             ("ssm_norm_w_2", 16), ("conv_b_2", 24), ("pool_scale", 4)],
            [("conv_w_2", 96)],
        ]
        heights = [sum(n for _, n in pack) for pack in packs]
        where = {}
        for a, pack in enumerate(packs):
            r = 0
            for name, n in pack:
                where[name] = (a * P + r, n)
                r += n

        def sync(sp):
            sp.dma_start(common, io["common"]).then_inc(*packs_loaded.one(16))
            for a, pack in enumerate(packs):
                r = 0
                for name, n in pack:
                    src = io[name]
                    if len(src.shape) == 3:
                        src = src.rearrange("a b c -> (a b c)")
                    elif len(src.shape) == 2:
                        src = src.rearrange("a b -> (a b)")
                    sp.dma_start(row_packs[r:r + n, a, :], src.rearrange("(r q) -> r q", q=P)).then_inc(*packs_loaded.one(16))
                    r += n
            issue_loads(sp)
            for t in range(2):
                sp.dma_start(stream[:, t, :], io["x"][0, t * P:t * P + P, :]).then_inc(*loaded.one(16))
                sp.dma_start(stream[:, 2 + t, :], io["ctx"][0, t * P:t * P + P, :]).then_inc(*loaded.one(16))
            sp.dma_start(tables[:, 0:3584], io["first"]).then_inc(*loaded.one(16))
            for l in range(DEPTH):
                for j, name in enumerate(("q_norm", "k_norm")):
                    sp.dma_start(head_gain[:, (2 * l + j) * HD:(2 * l + j + 1) * HD],
                                 io[name][l:l + 1, :].broadcast_to([P, HD])).then_inc(*loaded.one(16))
            r = 0
            for name in ("swa_sinks_2", "b_forget_2", "dt_bias_2", "a_log_2", "d_skip_2"):
                w = io[name].shape[1]
                for l in range(DEPTH):
                    sp.dma_start(small_rows[:, r:r + w], io[name][l:l + 1, :].broadcast_to([P, w])).then_inc(*loaded.one(16))
                    r += w
            sp.wait_ge(*ready_g.at(1))
            for l in range(DEPTH):
                for g in range(4):
                    c0 = (2 * l + g // 2) * P + 64 * (g % 2)
                    sp.dma_start(pool_blocks[64 * (g % 2):64 * (g % 2) + 64, c0:c0 + 64],
                                 io["pool_w"][l, g]).then_inc(*loaded.one(16))

        def gpsimd(pool):
            pool.memset(pool_blocks, 0.0).then_inc(*ready_g.one())

        def vector(dve):
            dve.memset(columns, 0.0).then_inc(*step_v.one())
            dve.wait_ge(*step_v.now())
            for a, rows in enumerate(heights):
                dve.wait_ge(*products.at(a + 1))
                c0 = a * P if a < 2 else 2 * P
                chain(dve, step_v, dve.tensor_copy(columns[:, c0:c0 + rows], psum[:, a, 0:rows]))
            for name in ("conv_w_2", "conv_b_2"):
                c0, n = where[name]
                chain(dve, step_v, dve.tensor_scalar(columns[:, c0:c0 + n], columns[:, c0:c0 + n], HALVED, None, ALU.mult))

        with nc.Block() as block:
            block.sync(sync)

            @block.gpsimd
            def _(pool):
                gpsimd(pool)

            @block.tensor
            def _(pe):
                pe.wait_ge(*packs_loaded.now())
                for a, rows in enumerate(heights):
                    pe.transpose(psum[:, a, 0:rows], row_packs[0:rows, a, :], ident[0:rows, 0:rows]).then_inc(*products.one())

            @block.vector
            def _(dve):
                dve.memset(soft, 0.0).then_inc(rows_used.sem, ROWS)
                rows_used.total += ROWS
                vector(dve)
                dve.wait_ge(*step_a.at(1))
                c0 = where["c"][0]
                th = silu_c[:, 0:16]
                chain(dve, step_v, dve.scalar_tensor_tensor(out=th, in0=th, scalar=1.0, in1=columns[:, c0:c0 + 16],
                                                            op0=ALU.add, op1=ALU.mult))
                chain(dve, step_v, dve.tensor_scalar(
                    silu_c[:, 16:32].rearrange("p (k s) -> p s k", s=2),
                    th.rearrange("p (s k) -> p s k", s=2), HALVED, None, ALU.mult))

            @block.scalar
            def _(act):
                act.wait_ge(*step_v.at(6))
                c0 = where["c"][0]
                act.activation(silu_c[:, 0:16], columns[:, c0:c0 + 16], ACT.Tanh, scale=0.5).then_inc(*step_a.one())
        return where

    where = setup_stage()

    def column(name, j):
        return columns[:, where[name][0] + j:where[name][0] + j + 1]

    def gate_row(which, s):
        return gate_rows[:, (2 * which + s) * DM:(2 * which + s + 1) * DM]

    def ada_stage(l, sync=None):
        open_stage()
        mods_v = mods.rearrange("p (j s) -> p j s", s=2)
        cond = silu_c[:, 16:32].rearrange("p (k s) -> p k s", s=2)
        gain1, gain2 = (norm_cols[:, 16 * i:16 * i + 16].rearrange("p (k s) -> p k s", s=2) for i in range(2))
        diag = [soft[:, 128 * i:128 * i + 128] for i in range(4)]
        streams = range(2) if l < DEPTH - 1 else range(1)
        gate_list = [(w, s, k) for w in range(2) for s in streams for k in range(KD)]

        rows = soft[0:2, 0:512]

        def turn(pe, b):
            pe.wait_ge(*ready_a.at(b + 1))
            for c in range(4):
                j = 4 * b + c
                mm = pe.transpose(psum[:, 7, 2 * j:2 * j + 2], rows[:, c * P:c * P + P], ident[0:2, 0:2])
            mm.then_inc(*products.one())

        def tensor(pe):
            for b in range(12):
                w = take(pe, ("ada", l, b))
                if b >= 2:
                    pe.wait_ge(*ready_a.at(b - 1))
                for k in range(KD):
                    mm = pe.matmul(psum[0:2, b % 2, :], cond[:, k, :], w[:, k, :], start=k == 0, stop=k == KD - 1)
                mm.then_inc(*products.one())
                release()
                if b >= 1:
                    turn(pe, b - 1)
            turn(pe, 11)
            for i in range(len(gate_list)):
                pe.wait_ge(*ready_v.at(i + 1))
                bank = (i // 4) % 7
                if i // 4 >= 7 and i % 4 == 0:
                    pe.wait_ge(*read_a.at(i // 4 - 6))
                pe.matmul(psum[:, bank, 128 * (i % 4):128 * (i % 4) + 128], ones, diag[i % 4],
                          start=True, stop=True).then_inc(*products.one())

        def vector(dve):
            yield 93.0
            dve.wait_ge(*products.at(24))
            bias = columns[:, where["ada_b"][0] + 48 * l:where["ada_b"][0] + 48 * l + 48]
            chain(dve, step_v, dve.tensor_tensor(out=mods_v, in0=psum[:, 7, 0:96].rearrange("p (j s) -> p j s", s=2),
                                                 in1=bias.unsqueeze(2).broadcast_to([P, 48, 2]), op=ALU.add))
            for gain, m, name in ((gain1, 1, "norm_mix"), (gain2, 4, "norm_ffn")):
                g = columns[:, where[name][0] + 8 * l:where[name][0] + 8 * l + 8]
                chain(dve, step_v, dve.scalar_tensor_tensor(
                    out=gain, in0=mods_v[:, 8 * m:8 * m + 8, :], scalar=1.0,
                    in1=g.unsqueeze(2).broadcast_to([P, 8, 2]), op0=ALU.add, op1=ALU.mult))
            for i, (w, s, k) in enumerate(gate_list):
                if i >= 4:
                    dve.wait_ge(*products.at(24 + i - 3))
                dve.tensor_scalar(diag[i % 4], ident, mods_v[:, 8 * (2 + 3 * w) + k, s:s + 1], None, ALU.mult).then_inc(*ready_v.one())

        def scalar(act):
            for b in range(12):
                act.wait_ge(*products.at(1 if b == 0 else 2 * b))
                if b >= 1:
                    act.wait_ge(*products.at(2 * b + 1 if b < 12 else 24))
                act.copy(rows, psum[0:2, b % 2, :]).then_inc(*ready_a.one())
            for q in range(len(gate_list) // 4):
                act.wait_ge(*products.at(24 + 4 * q + 4))
                w, s, k = gate_list[4 * q]
                act.copy(gate_row(w, s)[:, P * k:P * k + 512], psum[:, q % 7, :]).then_inc(*read_a.one())

        run_stage(tensor, vector, scalar, sync)

    def first_gain(which, k, s):
        return norm_cols[:, 16 * which + 2 * k + s:16 * which + 2 * k + s + 1]

    def first_shift(which, k, s):
        j = (0 if which == 0 else 3) * 8 + k
        return mods[:, 2 * j + s:2 * j + s + 1]

    def inverse_root(dve, dst, sums, scratch, count):
        w = dst.shape[1]
        v, y, t = (scratch[:, w * i:w * i + w] for i in range(3))
        chain(dve, step_v, dve.tensor_scalar(v, sums, 1.0 / count, NORM_EPS, ALU.mult, ALU.add))
        chain(dve, step_v, dve.tensor_scalar(y.bitcast(I32), v.bitcast(I32), 1, None, ALU.logical_shift_right))
        chain(dve, step_v, dve.tensor_scalar(y.bitcast(I32), y.bitcast(I32), -1.0, float(0x5F3759DF), ALU.mult, ALU.add))
        for i in range(4):
            chain(dve, step_v, dve.tensor_tensor(out=t, in0=y, in1=y, op=ALU.mult))
            chain(dve, step_v, dve.scalar_tensor_tensor(out=t, in0=t, scalar=-0.5, in1=v, op0=ALU.mult, op1=ALU.mult))
            chain(dve, step_v, dve.scalar_tensor_tensor(out=dst if i == 3 else y, in0=t, scalar=1.5, in1=y,
                                                        op0=ALU.add, op1=ALU.mult))

    def norm_stage(tiles, gain, shift, place=None, sync=None):
        open_stage()
        n = len(tiles)

        def scalar(act):
            for i, t in enumerate(tiles):
                act.activation(mixed_v[:, t, :], stream[:, t, :], ACT.Square,
                               accum_out=stats[:, t:t + 1]).then_inc(*ready_a.one())
            for g in range(1, 2 * n, 2):
                act.wait_ge(*products.at(g + 1))
                for q in range(4):
                    k, t = 4 * (g % 2) + q, tiles[g // 2]
                    ins = act.activation(turned_s[t // 2 if place is None else place][:, k, (t % 2) * P:(t % 2) * P + P], psum[:, g % 8, q * P:q * P + P], ACT.Identity,
                                         scale=gain(k, t), bias=shift(k, t) if shift else 0.0)
                ins.then_inc(*read_a.one())

        def vector(dve):
            for i0 in range(0, n, 2):
                t = tiles[i0]
                yield 5.0
                dve.wait_ge(*ready_a.at(i0 + 2))
                inverse_root(dve, stats[:, 16 + t:18 + t], stats[:, t:t + 2], stats[:, 32:38], DM)
                for t in tiles[i0:i0 + 2]:
                    dve.tensor_scalar(mixed_v[:, t, :], stream[:, t, :], stats[:, 16 + t:17 + t], None,
                                      ALU.mult).then_inc(*ready_v.one())
            for g in range(0, 2 * n, 2):
                yield 5.0
                dve.wait_ge(*products.at(g + 1))
                for q in range(4):
                    k, t = 4 * (g % 2) + q, tiles[g // 2]
                    ins = dve.tensor_scalar(turned_s[t // 2 if place is None else place][:, k, (t % 2) * P:(t % 2) * P + P], psum[:, g % 8, q * P:q * P + P],
                                            gain(k, t), shift(k, t) if shift else 0.0, ALU.mult, ALU.add)
                ins.then_inc(*read_v.one())

        def tensor(pe):
            for g in range(2 * n):
                t = tiles[g // 2]
                pe.wait_ge(*ready_v.at(g // 2 + 1))
                for q in range(4):
                    k = 4 * (g % 2) + q
                    mm = pe.transpose(psum[:, g % 8, q * P:q * P + P], mixed_v[:, t, k * P:k * P + P], ident)
                mm.then_inc(*products.one())

        run_stage(tensor, vector, scalar, sync)

    def turn_stage(groups):
        open_stage()

        def tensor(pe):
            for g, (sources, _) in enumerate(groups):
                if g >= 8:
                    pe.wait_ge(*(read_v if g % 2 == 0 else read_a).at((g - 8) // 2 + 1))
                for q, src in enumerate(sources):
                    mm = pe.transpose(psum[:, g % 8, q * P:q * P + P], src, ident)
                mm.then_inc(*products.one())

        def vector(dve):
            for g in range(0, len(groups), 2):
                yield 3.0
                dve.wait_ge(*products.at(g + 1))
                for c0, w, dst, scale in groups[g][1]:
                    src = psum[:, g % 8, c0:c0 + w]
                    if len(dst.shape) == 3:
                        src = src.rearrange("p (a b) -> p a b", a=dst.shape[1])
                    if isinstance(scale, float):
                        ins = dve.tensor_scalar(dst, src, scale, None, ALU.mult) if scale != 1.0 else dve.tensor_copy(dst, src)
                    else:
                        ins = dve.tensor_scalar(dst, src, scale, None, ALU.mult)
                ins.then_inc(*read_v.one())

        def scalar(act):
            for g in range(1, len(groups), 2):
                act.wait_ge(*products.at(g + 1))
                for c0, w, dst, scale in groups[g][1]:
                    src = psum[:, g % 8, c0:c0 + w]
                    if len(dst.shape) == 3:
                        src = src.rearrange("p (a b) -> p a b", a=dst.shape[1])
                    ins = act.activation(dst, src, ACT.Copy, scale=scale)
                ins.then_inc(*read_a.one())

        run_stage(tensor, vector, scalar)

    def linear_stage(jobs, beside=None, sync=None):
        open_stage()
        groups = []
        for job in jobs:
            keys, kind, items, lhs, dst = job
            for it in items:
                adding = isinstance(dst, tuple)
                groups.append((job, it, "v" if adding or (len(groups) % 2 == 0 and not beside) else "a"))
        order = {"v": 0, "a": 0}
        nth = []
        for _, _, e in groups:
            order[e] += 1
            nth.append(order[e])

        def tensor(pe):
            g = 0
            for job in jobs:
                keys, kind, items, lhs, dst = job
                weights = []
                for j, key in enumerate(keys):
                    n = len(used) + j
                    assert plan[n][0] == key, (plan[n][0], key)
                    weights.append(slot_view(n))
                k_total = sum(w.shape[1] for w in weights)
                k0 = 0
                for j, w in enumerate(weights):
                    pe.wait_ge(*landing[len(used)])
                    for q, it in enumerate(items):
                        b = g + q
                        if j == 0 and b >= 8:
                            pe.wait_ge(*(read_v if groups[b - 8][2] == "v" else read_a).at(nth[b - 8]))
                        for kk in range(w.shape[1]):
                            k, cols = k0 + kk, w.shape[2]
                            if kind == "rows":
                                mm = pe.matmul(psum[:, b % 8, 0:cols], lhs(k, it), w[:, kk, :],
                                               start=k == 0, stop=k == k_total - 1)
                            else:
                                rhs = lhs(k, None)
                                mm = pe.matmul(psum[:, b % 8, 0:rhs.shape[1]], w[:, kk, it * P:it * P + P], rhs,
                                               start=k == 0, stop=k == k_total - 1)
                        if j == len(weights) - 1:
                            mm.then_inc(*products.one())
                    if j < len(weights) - 1:
                        mm.then_inc(*half_used.one())
                        release(half_used)
                    else:
                        release()
                    k0 += w.shape[1]
                g += len(items)
            if beside:
                pe.wait_ge(*read_a.at(nth[g - 7]))
                beside[2](pe, (g % 8, (g + 1) % 8))

        def vector(dve):
            if beside:
                beside[0](dve, (len(groups) % 8, (len(groups) + 1) % 8), len(groups))
                return
            for g, (job, it, e) in enumerate(groups):
                if e != "v":
                    continue
                yield 13.6 if not isinstance(job[4], tuple) else 8.0
                dve.wait_ge(*products.at(g + 1))
                dst = job[4]
                if isinstance(dst, tuple):
                    _, gate, c0 = dst
                    x = stream[:, it, c0:c0 + 512]
                    if gate is None:
                        dve.tensor_tensor(out=x, in0=psum[:, g % 8, :], in1=x, op=ALU.add).then_inc(*read_v.one())
                    else:
                        tmp = heads[:, 2048 + 512 * (g % 4):2560 + 512 * (g % 4)]
                        dve.tensor_tensor(out=tmp, in0=psum[:, g % 8, :], in1=gate(it)[:, c0:c0 + 512],
                                          op=ALU.mult).then_inc(*read_v.one())
                        dve.wait_ge(*read_v.now())
                        dve.tensor_tensor(out=x, in0=tmp, in1=x, op=ALU.add).then_inc(*step_v.one())
                else:
                    d = dst(it)
                    scale = 1.0
                    if isinstance(d, tuple):
                        d, scale = d
                    dve.tensor_scalar(d, psum[:, g % 8, 0:d.shape[1]], scale, None, ALU.mult).then_inc(*read_v.one())

        def scalar(act):
            others = beside[1](act) if beside else iter(())
            for g, (job, it, e) in enumerate(groups):
                if e != "a":
                    continue
                next(others, None)
                act.wait_ge(*products.at(g + 1))
                d = job[4](it)
                scale = 1.0
                if isinstance(d, tuple):
                    d, scale = d
                act.activation(d, psum[:, g % 8, 0:d.shape[1]], ACT.Copy, scale=scale).then_inc(*read_a.one())
            for _ in others:
                pass

        run_stage(tensor, vector, scalar, sync)

    def normed(k, t):
        return turned_s[t // 2][:, k, (t % 2) * P:(t % 2) * P + P]

    proj1 = proj[:, 0:2 * 1280].rearrange("p (t n) -> p t n", t=2)
    context_kv = proj[:, 2560:3072].rearrange("p (t n) -> p t n", t=2)
    sims_area = proj[:, 3072:7168]
    row_slots = ([lent[:, DM * u:DM * u + DM] for u in range(4)]
                 + [proj[:, 7168 + DM * u:8192 + DM * u] for u in range(2)]
                 + [turned[:, DM * u:DM * u + DM] for u in range(2)])
    proj2 = proj[:, 0:2 * W2_TOKEN_COLS].rearrange("p (t n) -> p t n", t=2)
    lifted_s = [lifted[:, 2048 * s:2048 * s + 2048].rearrange("p (c t) -> p c t", c=8) for s in range(2)]
    attention_gate = lifted_s[1].rearrange("p c t -> p (c t)").rearrange("p (t d) -> p t d", t=2)
    four_t, pool_t, attn_t = ([v[:, c0:c1, :] for v in lifted_s] for c0, c1 in ((0, 2), (2, 4), (4, 8)))
    c_len, s_len = (tables[:, 512 * i:512 * i + 512].rearrange("p (k t) -> p k t", k=2) for i in range(2))
    c_ch, s_ch = tables[:, 1024:1152], tables[:, 1152:1280]
    pools = tables[:, 1280:3328].rearrange("p (w k t) -> p w k t", w=4, k=2)

    def branch_stage(l, s):
        open_stage()
        units = range(2)
        turned_f = mixed[:, 2048 * s:2048 * s + 1024].rearrange("p (u n) -> p u n", u=2)
        pooled = mixed[:, 2048 * s + 1024:2048 * s + 1536].rearrange("p (u n) -> p u n", u=2)

        def tensor(pe):
            for u, ch in enumerate(units):
                for i, table in enumerate((c_len, s_len)):
                    for k in range(2):
                        mm = pe.matmul(psum[:, 2 * u, 256 * i:256 * i + 256], proj1[:, k, ch * P:ch * P + P],
                                       table[:, k, :], start=k == 0, stop=k == 1)
                mm.then_inc(*products.one())
                for half in range(2):
                    g = 2 * ch + half
                    for k in range(2):
                        mm = pe.matmul(psum[64 * half:64 * half + 64, 2 * u + 1, 0:256],
                                       proj1[:, k, 256 + 64 * g:320 + 64 * g], pools[:, g, k, :],
                                       start=k == 0, stop=k == 1)
                mm.then_inc(*products.one())
            for u, ch in enumerate(units):
                pe.wait_ge(*read_v.at(u + 1))
                pe.matmul(psum[:, 2 * u, 0:256], c_ch, turned_f[:, u, 0:256], start=True, stop=False)
                pe.matmul(psum[:, 2 * u, 0:256], s_ch, turned_f[:, u, 256:512], start=False, stop=True).then_inc(*products.one())
                pe.wait_ge(*read_a.at(u + 1))
                pe.matmul(psum[:, 2 * u + 1, 0:256], pool_blocks[:, (2 * l + ch) * P:(2 * l + ch + 1) * P], pooled[:, u, :],
                          start=True, stop=True).then_inc(*products.one())

        def vector(dve):
            for u in range(len(units)):
                yield 4.0
                dve.wait_ge(*products.at(2 * u + 1))
                dve.tensor_copy(turned_f[:, u, :], psum[:, 2 * u, :]).then_inc(*read_v.one())
            for u, ch in enumerate(units):
                dve.wait_ge(*products.at(2 * len(units) + 2 * u + 1))
                dve.tensor_copy(four_t[s][:, ch, :], psum[:, 2 * u, 0:256]).then_inc(*read_v.one())

        def scalar(act):
            for u in range(len(units)):
                act.wait_ge(*products.at(2 * u + 2))
                act.copy(pooled[:, u, :], psum[:, 2 * u + 1, 0:256]).then_inc(*read_a.one())
            for u, ch in enumerate(units):
                act.wait_ge(*products.at(2 * len(units) + 2 * u + 2))
                act.activation(pool_t[s][:, ch, :], psum[:, 2 * u + 1, 0:256], ACT.Copy,
                               scale=column("pool_scale", 2 * l + ch)).then_inc(*read_a.one())

        run_stage(tensor, vector, scalar)

    def rotated(t):
        return sims_area[:, 2816 + 640 * (t % 2):3456 + 640 * (t % 2)]

    def rotate_stage(*args):
        open_stage()
        run_stage(vector=rotate_work(*args))

    def rotate_work(l, tiles, base, cos, sin, axes, gains):
        f = HD // (2 * axes)
        work = ([sims_area[:, 1536 + 640 * i:2176 + 640 * i] for i in range(2)] if gains else
                [heads[:, 2048 + 640 * i:2688 + 640 * i] for i in range(2)])

        def paired(v):
            return v.rearrange("p (c h d) -> p h c d", h=2, d=HD)

        def halves(v):
            return v.rearrange("p (h c d) -> p h c d", h=2, d=HD)

        def vector(dve):
            for t in tiles:
                x = base(t)
                n = x.shape[1] // HD
                dst = rotated(t) if gains and n == 10 else mixed_v[:, t, 0:640]
                h0 = 10 - n
                xh = x.rearrange("p (h d) -> p h d", d=HD)
                yield 20.0
                if gains:
                    a = work[0].rearrange("p (h d) -> p h d", d=HD)[:, h0:10, :]
                    chain(dve, step_v, dve.tensor_tensor(out=a, in0=xh, in1=xh, op=ALU.mult))
                    chain(dve, step_v, dve.tensor_reduce(stats[:, h0:10], a, AX, ALU.add))
                    inverse_root(dve, stats[:, 10 + h0:20], stats[:, h0:10], stats[:, 24:24 + 3 * n], HD)
                    chain(dve, step_v, dve.tensor_tensor(
                        out=xh, in0=xh, in1=stats[:, 10 + h0:20].unsqueeze(2).broadcast_to([P, n, HD]), op=ALU.mult))
                    q_gain, k_gain = (head_gain[:, (2 * l + j) * HD:(2 * l + j + 1) * HD] for j in range(2))
                    if h0 == 0:
                        q = x[:, 0:512]
                        chain(dve, step_v, dve.tensor_tensor(
                            out=q.rearrange("p (h d) -> p h d", d=HD) if t < 2 else paired(dst[:, 0:512]),
                            in0=q.rearrange("p (h d) -> p h d", d=HD) if t < 2 else halves(q),
                            in1=q_gain.unsqueeze(1).broadcast_to([P, 8, HD]) if t < 2 else
                            q_gain.unsqueeze(1).unsqueeze(1).broadcast_to([P, 2, 4, HD]), op=ALU.mult))
                    yield 25.0
                    k_dst = (x if t < 2 else dst)[:, 512:640].rearrange("p (h d) -> p h d", d=HD)
                    chain(dve, step_v, dve.tensor_tensor(out=k_dst, in0=xh[:, n - 2:n, :],
                                                         in1=k_gain.unsqueeze(1).broadcast_to([P, 2, HD]), op=ALU.mult))
                if t < 2:
                    a, b = work[0], work[1]
                    c, s = cos[:, t, :], sin[:, t, :]
                    chain(dve, step_v, dve.tensor_tensor(out=a.rearrange("p (h d) -> p h d", d=HD), in0=xh,
                                                         in1=c.unsqueeze(1).broadcast_to([P, 10, HD]), op=ALU.mult))
                    xv = x.rearrange("p (h a b f) -> p h a b f", h=10, a=axes, b=2)
                    bv = b.rearrange("p (h a b f) -> p h a b f", h=10, a=axes, b=2)
                    sv = s.rearrange("p (a b f) -> p a b f", a=axes, b=2)
                    for side in range(2):
                        chain(dve, step_v, dve.tensor_tensor(
                            out=bv[:, :, :, side, :], in0=xv[:, :, :, 1 - side, :],
                            in1=sv[:, :, side, :].unsqueeze(1).broadcast_to([P, 10, axes, f]), op=ALU.mult))
                    chain(dve, step_v, dve.tensor_tensor(out=paired(dst[:, 0:512]), in0=halves(a[:, 0:512]),
                                                         in1=halves(b[:, 0:512]), op=ALU.add))
                    chain(dve, step_v, dve.tensor_tensor(out=dst[:, 512:640], in0=a[:, 512:640], in1=b[:, 512:640],
                                                         op=ALU.add))

        return vector

    def attention_stage(units, temps, wide):
        open_stage()
        n = len(units)
        s_buf, p_buf, t_buf = ([temps[:, w * i:w * i + w] for i in range(i0, i0 + m)]
                               for i0, m, w in ((0, 2, wide), (2, 3, wide), (5, 2, wide)))

        def nth_product(i, what):
            count = 0
            for r in range(n + 3):
                for w, lag in ((0, 0), (1, 2), (2, 3)):
                    if 0 <= r - lag < n:
                        count += 1
                        if (r - lag, w) == (i, what):
                            return count

        def maxima(i):
            return 1 if i == 0 else 2 * i

        def divided(i):
            return 2 * i + 3 if i < n - 1 else 2 * n

        def tensor(pe):
            for i in range(n + 3):
                if i < n:
                    u = units[i]
                    if i >= 3:
                        pe.wait_ge(*ready_a.at(i - 2))
                    for j, (a, b) in enumerate(u["scores"]):
                        mm = pe.matmul(psum[:, i % 3, 0:u["keys"]], a, b, start=j == 0, stop=j == len(u["scores"]) - 1)
                    mm.then_inc(*products.one())
                if 0 <= i - 2 < n:
                    j = i - 2
                    pe.wait_ge(*ready_v.at(divided(j)))
                    if j >= 2:
                        pe.wait_ge(*read_a.at(j - 1))
                    for k in range(units[j]["keys"] // P):
                        mm = pe.transpose(psum[:, 3 + j % 2, k * P:k * P + P], p_buf[j % 3][:, k * P:k * P + P], ident)
                    mm.then_inc(*products.one())
                if i >= 3:
                    j = i - 3
                    pe.wait_ge(*read_a.at(j + 1))
                    if j >= 2:
                        pe.wait_ge(*read_v.at(j - 1))
                    kt = units[j]["keys"] // P
                    for mk in units[j]["outputs"]:
                        o = psum[mk["p0"]:mk["p0"] + mk["np"], 5 + j % 2, mk["c0"]:mk["c0"] + mk["w"]]
                        for k in range(kt):
                            probs, v = t_buf[j % 2][:, k * P:k * P + P], mk["values"](k)
                            a, b = (v, probs) if mk["turned"] else (probs, v)
                            mm = pe.matmul(o, a, b, start=k == 0, stop=k == kt - 1)
                    mm.then_inc(*products.one())

        def vector(dve):
            for i in range(n + 4):
                if i < n:
                    u = units[i]
                    keys = u["keys"]
                    yield 7.0
                    dve.wait_ge(*products.at(nth_product(i, 0)))
                    src = psum[:, i % 3, 0:keys]
                    if u.get("mask") is not None:
                        dst = s_buf[i % 2][:, 0:keys]
                        if i >= 2:
                            dve.wait_ge(*ready_a.at(i - 1))
                        if u.get("shift") is not None:
                            chain(dve, step_v, dve.scalar_tensor_tensor(out=dst, in0=src, scalar=u["shift"], in1=u["mask"],
                                                                        op0=ALU.add, op1=ALU.add))
                        else:
                            chain(dve, step_v, dve.tensor_tensor(out=dst, in0=src, in1=u["mask"], op=ALU.add))
                        src = dst
                    neg = soft[:, 4 * (i % 3):4 * (i % 3) + 1]
                    if u.get("sink") is None:
                        dve.tensor_reduce(neg, src, AX, ALU.max, negate=True).then_inc(*ready_v.one())
                    else:
                        chain(dve, step_v, dve.tensor_reduce(neg, src, AX, ALU.max))
                        dve.tensor_scalar(neg, neg, u["sink"], -1.0, ALU.max, ALU.mult).then_inc(*ready_v.one())
                if 1 <= i <= n:
                    j = i - 1
                    keys = units[j]["keys"]
                    total, extra, inv = (soft[:, 4 * (j % 3) + q:4 * (j % 3) + q + 1] for q in (1, 2, 3))
                    dve.wait_ge(*ready_a.at(j + 1))
                    if units[j].get("sink") is not None:
                        chain(dve, step_v, dve.tensor_tensor(out=total, in0=total, in1=extra, op=ALU.add))
                    chain(dve, step_v, dve.reciprocal(inv, total))
                    dve.tensor_scalar(p_buf[j % 3][:, 0:keys], p_buf[j % 3][:, 0:keys], inv, None,
                                      ALU.mult).then_inc(*ready_v.one())
                if i >= 4:
                    j = i - 4
                    dve.wait_ge(*products.at(nth_product(j, 2)))
                    for mk in units[j]["outputs"]:
                        ins = dve.tensor_copy(mk["dst"], psum[mk["p0"]:mk["p0"] + mk["np"], 5 + j % 2,
                                                              mk["c0"]:mk["c0"] + mk["w"]])
                    ins.then_inc(*read_v.one())

        def scalar(act):
            for i in range(n + 2):
                if i < n:
                    u = units[i]
                    keys = u["keys"]
                    act.wait_ge(*ready_v.at(maxima(i)))
                    if i >= 3:
                        act.wait_ge(*products.at(nth_product(i - 3, 1)))
                    neg, total, extra = (soft[:, 4 * (i % 3) + q:4 * (i % 3) + q + 1] for q in range(3))
                    if u.get("sink") is not None:
                        act.activation(extra, u["sink"], ACT.Exp, bias=neg).then_inc(*step_a.one())
                    src = psum[:, i % 3, 0:keys] if u.get("mask") is None else s_buf[i % 2][:, 0:keys]
                    act.activation(p_buf[i % 3][:, 0:keys], src, ACT.Exp, bias=neg, accum_out=total).then_inc(*ready_a.one())
                if i >= 2:
                    j = i - 2
                    keys = units[j]["keys"]
                    act.wait_ge(*products.at(nth_product(j, 1)))
                    if j >= 2:
                        act.wait_ge(*products.at(nth_product(j - 2, 2)))
                    act.copy(t_buf[j % 2][:, 0:keys], psum[:, 3 + j % 2, 0:keys]).then_inc(*read_a.one())

        run_stage(tensor, vector, scalar)

    def merge_stage(l, s, part="all", place=None, beside=None):
        open_stage()
        tiles = [2 * s, 2 * s + 1]
        jobs = merge_jobs(part)
        place = s if place is None else place
        sources = (four_t[s], pool_t[s], attn_t[s])
        tanh = [sims_area[:, 512 * i:512 * i + 512] for i in range(2)]
        tmp = sims_area[:, 1024:1536]
        units, gate_at, branch_at = [], [], []
        count = 0
        for job in jobs:
            gates, branches = job[2:]
            units += [(job, t) for t in tiles]
            gate_at += [count + 1, count + 2]
            count += 2 if gates else 0
            branch_at += [count + 1, count + 2]
            count += 2 if branches else 0

        def tensor(pe):
            q = 0
            for cb, br, gates, branches in jobs:
                src = sources[br]
                if gates:
                    w = take(pe, ("gate", l, cb, br))
                    for i in range(2):
                        if q + i >= 4:
                            pe.wait_ge(*read_v.at(q + i - 3))
                        for k in range(KD):
                            mm = pe.matmul(psum[:, 2 * ((q + i) % 4), :], turned_s[place][:, k, i * P:i * P + P], w[:, k, :],
                                           start=k == 0, stop=k == KD - 1)
                        mm.then_inc(*products.one())
                    release()
                if branches:
                    w = take(pe, ("branch", l, cb, br))
                    for i in range(2):
                        for k in range(src.shape[1]):
                            mm = pe.matmul(psum[:, 2 * ((q + i) % 4) + 1, :], src[:, k, i * P:i * P + P],
                                           w[:, k, :], start=k == 0, stop=k == src.shape[1] - 1)
                        mm.then_inc(*products.one())
                    release()
                q += 2

        def scalar(act):
            for q, ((_, _, gates, _), _) in enumerate(units):
                if not gates:
                    continue
                act.wait_ge(*products.at(gate_at[q]))
                if q >= 2:
                    act.wait_ge(*read_v.at(q - 1))
                act.activation(tanh[q % 2], psum[:, 2 * (q % 4), :], ACT.Tanh, scale=0.5).then_inc(*read_a.one())

        def vector(dve):
            others = beside(dve) if beside else iter(())
            for q, ((cb, br, gates, branches), t) in enumerate(units):
                yield 9.5
                next(others, None)
                kept = attention_gate[:, t % 2, 512 * cb:512 * cb + 512]
                if gates:
                    dve.wait_ge(*read_a.at(q + 1))
                if not branches:
                    dve.tensor_scalar(kept, tanh[q % 2], 1.0, None, ALU.add).then_inc(*read_v.one())
                    continue
                dve.wait_ge(*products.at(branch_at[q]))
                acc = mixed_v[:, t, 512 * cb:512 * cb + 512]
                dst = acc if br == 0 else tmp
                branch = psum[:, 2 * (q % 4) + 1, :]
                if gates:
                    ins = dve.scalar_tensor_tensor(out=dst, in0=tanh[q % 2], scalar=1.0, in1=branch, op0=ALU.add, op1=ALU.mult)
                else:
                    ins = dve.tensor_tensor(out=dst, in0=kept, in1=branch, op=ALU.mult)
                ins.then_inc(*read_v.one())
                dve.wait_ge(*read_v.now())
                if br:
                    chain(dve, step_v, dve.tensor_tensor(out=acc, in0=acc, in1=tmp, op=ALU.add))
            for _ in others:
                pass

        run_stage(tensor, vector, scalar)

    def turn_mixed(s, scale):
        turn_stage([([mixed_v[:, t, (4 * g + q) * P:(4 * g + q + 1) * P] for q in range(4)],
                     [(0, 512, turned_s[s][:, 4 * g:4 * g + 4, (t % 2) * P:(t % 2) * P + P], scale)])
                    for t in (2 * s, 2 * s + 1) for g in range(2)])

    def turn_back(s):
        turn_stage([([turned_s[s][:, 4 * g + q, (t % 2) * P:(t % 2) * P + P] for q in range(4)],
                     [(0, 512, mixed_v[:, t, 512 * g:512 * g + 512], 1.0)])
                    for t in (2 * s, 2 * s + 1) for g in range(2)])

    sims = sims_area.rearrange("p (t h n) -> p t h n", t=2, h=16)
    picks_u = area("picks_u", 4 * PICKS, U32).rearrange("p (t j) -> p t j", t=4)
    probs_g = area("probs_g", 4 * PICKS).rearrange("p (t j) -> p t j", t=4)

    def keys_stage(l, s):
        open_stage()
        nt = 2
        n_tok = P * nt
        keys_t = lifted[:, 2048 * s:2048 * s + 2048]
        qt = [proj[:, n_tok * i:n_tok * (i + 1)] for i in range(4)]

        def tensor(pe):
            w = take(pe, ("keys", l))
            for g in range(4):
                for q in range(4):
                    mm = pe.transpose(psum[:, g, q * P:q * P + P], w[:, 4 * g + q, :], ident)
                mm.then_inc(*products.one())
            release()
            for h in range(16):
                if h % 4 == 0:
                    w = take(pe, ("wq", l, h // 4))
                pe.wait_ge(*read_v.at(max(4, 4 + h - 3)))
                for k in range(KD):
                    mm = pe.matmul(psum[:, h % 4, 0:n_tok], w[:, k, (h % 4) * P:(h % 4) * P + P], turned_s[s][:, k, :],
                                   start=k == 0, stop=k == KD - 1)
                mm.then_inc(*products.one())
                if h % 4 == 3:
                    release()
                if h >= 1:
                    dot(pe, h - 1)
            dot(pe, 15)

        def dot(pe, h):
            pe.wait_ge(*read_v.at(4 + h + 1))
            if h >= 4:
                pe.wait_ge(*read_a.at(h - 3))
            for i in range(nt):
                mm = pe.matmul(psum[:, 4 + h % 4, i * P:i * P + P], qt[h % 4][:, i * P:i * P + P],
                               keys_t[:, h * P:h * P + P], start=True, stop=True)
            mm.then_inc(*products.one())

        def vector(dve):
            for g in range(4):
                dve.wait_ge(*products.at(g + 1))
                dve.tensor_copy(keys_t[:, 512 * g:512 * g + 512], psum[:, g, :]).then_inc(*read_v.one())
            search, searched = search_work(dve, 2 * s), 0
            for h in range(16):
                yield 6.0
                dve.wait_ge(*products.at(4 + (1 if h == 0 else 2 * h)))
                if h >= 4:
                    dve.wait_ge(*products.at(4 + dots_at(h - 4)))
                dve.tensor_copy(qt[h % 4], psum[:, h % 4, 0:n_tok]).then_inc(*read_v.one())
                if h >= 3:
                    while searched < len(search_needs) and search_needs[searched] <= h - 2:
                        dve.wait_ge(*read_a.at(search_needs[searched] + 1))
                        next(search)
                        searched += 1
            for need in search_needs[searched:]:
                yield 7.0
                dve.wait_ge(*read_a.at(need + 1))
                next(search)
            dve.wait_ge(*step_v.now())

        def dots_at(h):
            return 2 * h + 3 if h < 15 else 32

        def scalar(act):
            for h in range(16):
                act.wait_ge(*products.at(4 + dots_at(h)))
                act.copy(sims[:, 0:nt, h, :], psum[:, 4 + h % 4, 0:n_tok].rearrange("p (t n) -> p t n", t=nt))\
                   .then_inc(*read_a.one())

        run_stage(tensor, vector, scalar)

    heads_hi = heads[:, 2048:4096]
    best = heads_hi[:, 0:256].rearrange("p (h k) -> p h k", h=16)
    best_u = heads_hi[:, 256:512].bitcast(U32).rearrange("p (h k) -> p h k", h=16)
    pos_u = heads_hi[:, 1024:1152].bitcast(U32)
    top = heads_hi[:, 1664:1792]
    search_needs = [4 * q + need for q in range(4) for need in (1, 3, 3)]

    def search_area(t):
        return lifted[:, 2048:4096] if t < 2 else lifted[:, 0:2048]

    def sixteen(dve, searches):
        last = [None] * len(searches)
        for part in range(5):
            for i, (values, indices, src) in enumerate(searches):
                if last[i]:
                    dve.wait_ge(*last[i])
                span = slice(0, 8) if part < 3 else slice(8, 16)
                if part in (0, 3):
                    ins = dve.max(values[:, span], src)
                elif part in (1, 4):
                    ins = dve.max_index(indices[:, span], values[:, span], src)
                else:
                    ins = dve.match_replace(src, values[:, span], src, -3e38)
                ins.then_inc(*step_v.one())
                last[i] = step_v.now()

    def search_work(dve, t):
        cand = [search_area(t)[:, 256 * i:256 * i + 256] for i in range(2)]
        for h in range(0, PEER_HEADS, 2):
            for g in (2 * h, 2 * h + 2):
                sixteen(dve, [(best[:, g + i, :], best_u[:, g + i, :], sims[:, t % 2, g + i, :]) for i in range(2)])
                yield
            dve.wait_ge(*step_v.now())
            for i in range(2):
                a = best[:, 2 * (h + i), :].unsqueeze(2).broadcast_to([P, 16, 16])
                b = best[:, 2 * (h + i) + 1, :].unsqueeze(1).broadcast_to([P, 16, 16])
                dve.tensor_tensor(out=cand[i].rearrange("p (a b) -> p a b", a=16), in0=a, in1=b,
                                  op=ALU.add).then_inc(*step_v.one())
            dve.wait_ge(*step_v.now())
            sixteen(dve, [(top[:, 16 * g:16 * g + 16], pos_u[:, 16 * g:16 * g + 16], cand[g - h]) for g in (h, h + 1)])
            yield

    def topk_stage(l, t):
        open_stage()
        best_i = heads_hi[:, 512:768].rearrange("p (h k) -> p h k", h=16)
        side_u = heads_hi[:, 1152:1280].bitcast(U32)
        side_f = heads_hi[:, 1280:1408]
        gathered_i = [heads_hi[:, 1408:1536], heads_hi[:, 1536:1664]]
        hot = search_area(t)
        spare = heads_hi[:, 1792:1920]

        def step(dve, ins):
            chain(dve, step_v, ins)

        def vector(dve):
            if t % 2:
                for i, _ in enumerate(search_work(dve, t)):
                    yield 18.0 if i % 3 == 2 else 9.0
                dve.wait_ge(*step_v.now())
            step(dve, dve.tensor_copy(best_i, best_u))
            for side in range(2):
                if side == 0:
                    step(dve, dve.tensor_scalar(side_u, pos_u, 4, None, ALU.logical_shift_right))
                else:
                    step(dve, dve.tensor_scalar(side_u, pos_u, 15, None, ALU.bitwise_and))
                yield 12.0
                step(dve, dve.tensor_copy(side_f, side_u))
                eq = hot.rearrange("p (j r) -> p j r", r=16)
                step(dve, dve.tensor_tensor(out=eq, in0=side_f.unsqueeze(2).broadcast_to([P, PICKS, 16]),
                                            in1=iota16.unsqueeze(1).broadcast_to([P, PICKS, 16]), op=ALU.is_equal))
                eq4 = hot.rearrange("p (h j r) -> p h j r", h=PEER_HEADS, r=16)
                keys = best_i.rearrange("p (h s) k -> p h s k", s=2)[:, :, side, :]
                step(dve, dve.tensor_tensor(out=eq4, in0=eq4, in1=keys.unsqueeze(2).broadcast_to([P, PEER_HEADS, TOPK, 16]),
                                            op=ALU.mult))
                yield 12.0
                step(dve, dve.tensor_reduce(gathered_i[side], eq, AX, ALU.add))
            step(dve, dve.scalar_tensor_tensor(out=side_f, in0=gathered_i[0], scalar=128.0, in1=gathered_i[1],
                                               op0=ALU.mult, op1=ALU.add))
            if l:
                step(dve, dve.tensor_scalar(side_f, side_f, float(l * EXPERTS), None, ALU.add))
            dve.tensor_copy(picks_u[:, t, :], side_f).then_inc(*picked.one())
            tv = top.rearrange("p (h k) -> p h k", k=TOPK)
            step(dve, dve.tensor_reduce(spare[:, 0:8], tv, AX, ALU.max))
            dve.tensor_tensor(out=tv, in0=tv, in1=spare[:, 0:8].unsqueeze(2).broadcast_to([P, 8, TOPK]),
                              op=ALU.subtract).then_inc(*ready_v.one())
            yield 12.0
            dve.wait_ge(*ready_a.at(1))
            gv = probs_g[:, t, :].rearrange("p (h k) -> p h k", k=TOPK)
            step(dve, dve.tensor_reduce(spare[:, 8:16], gv, AX, ALU.add))
            step(dve, dve.reciprocal(spare[:, 16:24], spare[:, 8:16]))
            step(dve, dve.tensor_tensor(out=gv, in0=gv, in1=spare[:, 16:24].unsqueeze(2).broadcast_to([P, 8, TOPK]),
                                        op=ALU.mult))

        def scalar(act):
            act.wait_ge(*ready_v.at(1))
            act.activation(probs_g[:, t, :], top, ACT.Exp).then_inc(*ready_a.one())

        run_stage(vector=vector, scalar=scalar)

    index_stage = area("index_stage", 16, U32)
    dots = area("dots", PICKS)
    EARLY, LATE = PICKS - 2 * ROWS, 2 * ROWS
    tables_dram = [io[n].rearrange("l n d -> (l n) d") for n in ("peer_u", "peer_v")]

    class RowWork:

        def __init__(self, block, s, scratch, row_us):
            self.block, self.s = block, s
            self.phases = [(t, which) for t in (2 * s, 2 * s + 1) for which in range(2)]
            self.base = rows_used.total
            self.row = 0
            self.owed = 0.0
            self.scratch = scratch
            self.row_us = row_us

        def advance(self, dve, us):
            self.owed += us
            while self.owed >= self.row_us and self.row < len(self.phases) * PICKS:
                self.owed -= self.row_us
                self.rows(dve, 1)

        def finish(self, dve):
            while self.row < len(self.phases) * PICKS:
                at = self.row % (2 * PICKS)
                left = min(stop - at for stop in (EARLY, PICKS, PICKS + LATE, 2 * PICKS) if stop > at)
                self.rows(dve, 1 if self.row % ROWS or PICKS <= at < PICKS + ROWS else left)

        def rows(self, dve, n):
            ph, j = divmod(self.row, PICKS)
            t, which = self.phases[ph]
            if which == 0 and j == EARLY:
                dve.wait_ge(rows_used.sem, self.base + self.row)
                self.weigh(dve, t, 0, EARLY)
            if which == 1 and j == LATE:
                self.weigh(dve, t, EARLY, PICKS)
            if n == 1:
                self.one_row(dve, t, which, self.row % ROWS, j, self.base + self.row, None)
            else:
                with dve.Fori(0, n // ROWS) as i:
                    for u in range(ROWS):
                        self.one_row(dve, t, which, u, j + u, self.base + self.row + u, i)
            self.row += n
            if self.row % PICKS == 0:
                dve.wait_ge(rows_used.sem, self.base + self.row)
                if which == 1:
                    self.store(dve, t)

        def one_row(self, dve, t, which, u, j, row, i):
            step = 0 if i is None else i
            if i is None:
                dve.wait_ge(gathered[u].sem, 16 * ((row - ROWS) // ROWS + 1))
                weight = dots[:, j:j + 1]
            else:
                dve.wait_ge(gathered[u].sem, step * 16 + 16 * ((row - ROWS) // ROWS + 1))
                weight = dots[:, bass.ds(step * ROWS + j, 1)]
            src = row_slots[u]
            if which == 0:
                dve.scalar_tensor_tensor(out=src, in0=src, scalar=1.0, in1=mixed_v[:, t, :], op0=ALU.mult, op1=ALU.mult,
                                         accum_out=weight).then_inc(rows_used.sem, 1)
            else:
                acc = heads[:, DM * (u % 2):DM * (u % 2) + DM]
                if i is None and j < 2:
                    dve.tensor_scalar(acc, src, weight, None, ALU.mult).then_inc(rows_used.sem, 1)
                    return
                dve.wait_ge(rows_used.sem, row - 1 if i is None else step * ROWS + (row - 1))
                dve.scalar_tensor_tensor(out=acc, in0=src, scalar=weight, in1=acc, op0=ALU.mult, op1=ALU.add)\
                   .then_inc(rows_used.sem, 1)

        def weigh(self, dve, t, c0, c1):
            cube, arg, n, f, poly, power, dots_, probs = (v[:, c0:c1] for v in self.scratch + [dots, probs_g[:, t, :]])
            c = -2.0 * float(np.sqrt(2.0 / np.pi))
            shift = 1.5 * 2.0 ** 23
            chain(dve, step_v, dve.tensor_tensor(out=cube, in0=dots_, in1=dots_, op=ALU.mult))
            chain(dve, step_v, dve.tensor_scalar(cube, cube, 0.044715 * c, c, ALU.mult, ALU.add))
            chain(dve, step_v, dve.tensor_tensor(out=arg, in0=cube, in1=dots_, op=ALU.mult))
            chain(dve, step_v, dve.tensor_scalar(arg, arg, 80.0, -80.0, ALU.min, ALU.max))
            chain(dve, step_v, dve.tensor_scalar(n, arg, 1.0 / float(np.log(2.0)), shift, ALU.mult, ALU.add))
            chain(dve, step_v, dve.tensor_scalar(n, n, -shift, None, ALU.add))
            chain(dve, step_v, dve.scalar_tensor_tensor(out=f, in0=n, scalar=-LN2_HIGH, in1=arg, op0=ALU.mult, op1=ALU.add))
            dve.tensor_scalar(power, n, 2.0 ** 23, 127 * 2.0 ** 23, ALU.mult, ALU.add).then_inc(*step_v.one())
            chain(dve, step_v, dve.scalar_tensor_tensor(out=f, in0=n, scalar=-LN2_LOW, in1=f, op0=ALU.mult, op1=ALU.add))
            dve.tensor_copy(n.bitcast(U32), power).then_inc(*step_v.one())
            chain(dve, step_v, dve.tensor_scalar(poly, f, 1.0 / 5040, None, ALU.mult))
            for factorial in (720, 120, 24, 6, 2, 1):
                chain(dve, step_v, dve.scalar_tensor_tensor(out=poly, in0=poly, scalar=1.0 / factorial, in1=f,
                                                            op0=ALU.add, op1=ALU.mult))
            chain(dve, step_v, dve.scalar_tensor_tensor(out=arg, in0=poly, scalar=1.0, in1=n, op0=ALU.add, op1=ALU.mult))
            chain(dve, step_v, dve.tensor_scalar(cube, arg, 1.0, None, ALU.add))
            chain(dve, step_v, dve.reciprocal(arg, cube))
            chain(dve, step_v, dve.tensor_tensor(out=cube, in0=arg, in1=dots_, op=ALU.mult))
            chain(dve, step_v, dve.tensor_tensor(out=dots_, in0=cube, in1=probs, op=ALU.mult))

        def store(self, dve, t):
            acc, other = heads[:, 0:DM], heads[:, DM:2 * DM]
            chain(dve, step_v, dve.tensor_tensor(out=acc, in0=acc, in1=other, op=ALU.add))
            chain(dve, step_v, dve.tensor_tensor(out=acc, in0=acc, in1=gate_row(1, t // 2), op=ALU.mult))
            chain(dve, step_v, dve.tensor_tensor(out=stream[:, t, :], in0=stream[:, t, :], in1=acc, op=ALU.add))

    def experts_stage(s, gelu_row, guests, row_us, sync=None):
        base, stage0, picked0 = rows_used.total, staged.total, 2 * gather_count[0]
        gather_count[0] += 1

        def turn_of_ring(pool, t, which, half, row0, turn, i):
            reg = i is not None
            pool.wait_ge(rows_used.sem, i * 16 + (row0 - ROWS + 1) if reg else row0 - ROWS + 1)
            src = picks_u[:, t, bass.ds(i * 16 + 8 * half, 8)] if reg else picks_u[:, t, 8 * half:8 * half + 8]
            pool.tensor_copy(index_stage[:, 8 * half:8 * half + 8], src).then_inc(staged.sem, 1)
            for u in range(ROWS):
                if u == 0:
                    pool.wait_ge(staged.sem, i * 2 + (turn + 1) if reg else turn + 1)
                pool.wait_ge(rows_used.sem, i * 16 + (row0 + u - ROWS + 1) if reg else row0 + u - ROWS + 1)
                pool.sem_inc(*admitted.one())
                pool.indirect_dma_start(
                    out=row_slots[u], out_offset=None, in_=tables_dram[which],
                    in_offset=bass.IndirectOffsetOnAxis(ap=index_stage[:, 8 * half + u:8 * half + u + 1], axis=0),
                ).then_inc(gathered[u].sem, 16)

        def gpsimd(pool):
            for ph in range(4):
                t, which = 2 * s + ph // 2, ph % 2
                row0, turn0 = base + ph * PICKS, stage0 + ph * PICKS // ROWS
                if which == 0:
                    pool.wait_ge(picked.sem, picked0 + t % 2 + 1)
                for half in range(2):
                    turn_of_ring(pool, t, which, half, row0 + 8 * half, turn0 + half, None)
                with pool.Fori(1, PICKS // 16) as i:
                    for half in range(2):
                        turn_of_ring(pool, t, which, half, row0 + 8 * half, turn0 + half, i)

        with nc.Block() as block:
            work = RowWork(block, s, [gelu_row[:, PICKS * i:PICKS * i + PICKS] for i in range(6)], row_us)
            block.gpsimd(gpsimd)
            if sync:
                block.sync(sync)
            host[0] = work
            for guest in guests:
                guest()
            host[0] = None

            @block.vector
            def _(dve):
                work.finish(dve)

            @block.sync
            def _(sp):
                issue_loads(sp)
                if stored.total:
                    sp.wait_ge(*stored.now())
        rows_used.total += PICKS * 4
        gathers_done[0] += 1
        staged.total += PICKS * 4 // ROWS

    def turn_heads(s, tiles):
        q_t, k_t = heads[:, 2048:3072].rearrange("p (c t) -> p c t", c=4), heads[:, 3072:3584]
        groups = []
        for t in tiles:
            j = t - 2 * s
            src = rotated(t) if j < 2 else mixed_v[:, t, 0:640]
            if j < 2:
                groups.append(([src[:, c * P:c * P + P] for c in range(4)],
                               [(0, 512, q_t[:, :, j * P:j * P + P], HD ** -0.5)]))
            groups.append(([src[:, 512:640]], [(0, 128, k_t[:, j * P:j * P + P], 1.0)]))
        turn_stage(groups)

    def first_attention(s):
        q_t, k_t = heads[:, 2048:3072].rearrange("p (c t) -> p c t", c=4), heads[:, 3072:3584]
        tiles = (2 * s, 2 * s + 1)
        key_tiles = [0, 1, 2, 3] if s == 0 else [2, 3]

        def values(k, half):
            if k < 2:
                return proj1[:, k, 1152 + 64 * half:1216 + 64 * half]
            return context_kv[:, k - 2, 128 + 64 * half:192 + 64 * half]

        units = []
        for t in tiles:
            for half in range(2):
                for c in range(4):
                    rows = slice(64 * half, 64 * half + 64)
                    span = slice((t % 2) * P, (t % 2) * P + P)
                    units.append(dict(
                        keys=P * len(key_tiles), scores=[(q_t[rows, c, span], k_t[rows, 0:P * len(key_tiles)])],
                        outputs=[dict(values=lambda k, half=half: values(k, half), p0=64 * half, np=64, c0=0, w=128,
                                      turned=True, dst=attn_t[s][rows, c, span])]))
        wide = P * len(key_tiles)
        attention_stage(units, sims_area[:, 0:7 * wide], wide)

    cos1 = tables[:, 3328:3456].rearrange("p (t d) -> p t d", t=2)
    sin1 = tables[:, 3456:3584].rearrange("p (t d) -> p t d", t=2)

    def attention_base(s):
        def base(t):
            if s == 0 and t >= 2:
                return context_kv[:, t - 2, 0:128]
            return proj1[:, t % 2, 512:1152]
        return base

    def input_norm(l, tiles, place=None):
        norm_stage(tiles, lambda k, t: first_gain(0, k, t // 2), lambda k, t: first_shift(0, k, t // 2), place)

    def project(l, s, with_context, place):
        tiles = [2 * s, 2 * s + 1]

        def lhs(k, t):
            return normed(k, t) if place is None else turned_s[place][:, k, (t % 2) * P:(t % 2) * P + P]

        def store(t, b):
            if s == 0 and t >= 2:
                return context_kv[:, t - 2, :]
            return proj1[:, t % 2, 512 * b:min(512 * b + 512, 1280)]

        linear_stage([([("w_in", l, b)], "rows", tiles + [2, 3] if b == 2 and with_context else tiles, lhs,
                       lambda t, b=b: store(t, b)) for b in range(3)])

    def mix_latents(l):
        tiles = [0, 1, 2, 3]
        return [lambda: project(l, 0, True, None), lambda: branch_stage(l, 0),
                lambda: merge_stage(l, 0, "early", beside=rotate_work(l, tiles, attention_base(0), cos1, sin1, 2, True)),
                lambda: turn_heads(0, tiles), lambda: first_attention(0), lambda: merge_stage(l, 0, "late")]

    def mix_context(l):
        tiles = [2, 3]
        return [lambda: project(l, 1, False, None), lambda: branch_stage(l, 1),
                lambda: rotate_stage(l, tiles, attention_base(1), cos1, sin1, 2, True),
                lambda: turn_heads(1, tiles), lambda: first_attention(1), lambda: merge_stage(l, 1)]

    def mix_early(l):
        return [lambda: input_norm(l, [0, 1], 1), lambda: project(l, 0, False, 1), lambda: branch_stage(l, 0),
                lambda: rotate_stage(l, [0, 1], attention_base(0), cos1, sin1, 2, True),
                lambda: turn_heads(0, [0, 1]), lambda: merge_stage(l, 0, "early", 1)]

    def mix_late(l):
        return [lambda: input_norm(l, [2, 3]),
                lambda: linear_stage([([("w_in_kv", l)], "rows", [2, 3], normed, lambda t: context_kv[:, t - 2, :])]),
                lambda: rotate_stage(l, [2, 3], attention_base(0), cos1, sin1, 2, True),
                lambda: turn_heads(0, [2, 3]), lambda: first_attention(0), lambda: merge_stage(l, 0, "late")]

    def to_keys(l, s):
        tiles = [2 * s, 2 * s + 1]
        return [lambda: turn_mixed(s, HALVED),
                lambda: linear_stage([([("w_out", l, b)], "rows", tiles, normed, ("add", lambda t: gate_row(0, s), 512 * b))
                                      for b in range(2)]),
                lambda: norm_stage(tiles, lambda k, t: first_gain(1, k, s), lambda k, t: first_shift(1, k, s)),
                lambda: turn_back(s), lambda: keys_stage(l, s)]

    def first_block():
        ada_stage(0, lambda sp: sp.wait_ge(*loaded.now()))
        input_norm(0, [0, 1, 2, 3])
        for stage in mix_latents(0) + to_keys(0, 0) + [lambda: topk_stage(0, 0)]:
            stage()
        experts_stage(0, gate_row(0, 0), [lambda: topk_stage(0, 1)] + mix_context(0) + to_keys(0, 1)
                      + [lambda: topk_stage(0, 2)], 1.62)
        experts_stage(1, gate_row(0, 1), [lambda: topk_stage(0, 3), lambda: ada_stage(1)] + mix_early(1), 1.5)
        for stage in mix_late(1) + to_keys(1, 0) + [lambda: topk_stage(1, 0)]:
            stage()
        experts_stage(0, gate_row(0, 1), [lambda: topk_stage(1, 1), await_memory]
                      + [lambda l=l: memory_stages(l) for l in range(DEPTH)], 1.2, load_second)

    upper = tables[:, 0:512].rearrange("p (k t) -> p k t", k=2)
    band = tables[:, 512:1024].rearrange("p (t k) -> p t k", t=2)
    causal = tables[:, 1024:1536].rearrange("p (t k) -> p t k", t=2)
    causal_t = tables[:, 1536:2048].rearrange("p (t k) -> p t k", t=2)
    cos2 = tables[:, 2048:2176].rearrange("p (t d) -> p t d", t=2)
    sin2 = tables[:, 2176:2304].rearrange("p (t d) -> p t d", t=2)
    sinks = [small_rows[:, 8 * l:8 * l + 8] for l in range(2)]
    forget_bias = [small_rows[:, 16 + 8 * l:24 + 8 * l] for l in range(2)]
    dt_bias = [small_rows[:, 32 + 16 * l:48 + 16 * l] for l in range(2)]
    a_log = [small_rows[:, 64 + 16 * l:80 + 16 * l] for l in range(2)]
    d_skip = [small_rows[:, 96 + 16 * l:112 + 16 * l] for l in range(2)]
    raw_conv = gate_rows[:, 0:12 * 259].rearrange("p (c t) -> p c t", c=12)
    conv = lifted[:, 0:3072].rearrange("p (c t) -> p c t", c=12)
    dt_raw = soft[:, 16:48].rearrange("p (t h) -> p t h", t=2)
    softened = soft[:, 48:96].rearrange("p (t h) -> p t h", t=2)
    cum_f = soft[:, 96:112].rearrange("p (t h) -> p t h", t=2)
    decays = soft[:, 112:144].rearrange("p (t h) -> p t h", t=2)
    neg_acs = soft[:, 144:176].rearrange("p (t h) -> p t h", t=2)
    fallen_rows = tables[:, 2304:2560]
    acs_rows = tables[:, 2560:2816]
    silu_gates = gate_rows.rearrange("p (t d) -> p t d", t=2)
    y_v = mixed.rearrange("p (t d) -> p t d", t=2)

    def load_second(sp):
        sp.dma_start(tables[:, 0:2304], io["second"]).then_inc(*loaded.one(16))
        for t in range(2):
            sp.dma_start(stream[:, 2 + t, :], io["mem_2"][0, t * P:t * P + P, :]).then_inc(*loaded.one(16))

    def await_memory():
        open_stage()
        run_stage(scalar=lambda act: act.wait_ge(*loaded.now()))

    def memory_stages(l):
        kept = (lifted if l == 0 else sims_area).rearrange("p (j n) -> p j n", j=2)
        k_t = kept[:, 0, :].rearrange("p (c t) -> p c t", c=8)
        v_m = kept[:, 1, :].rearrange("p (t n) -> p t n", t=2)
        norm_stage([2, 3], lambda k, t: column("norm_mem_w_2", 8 * l + k), None)
        linear_stage(
            [([("w_mk_2", l, b)], "cols", [0, 1, 2, 3], lambda k, _: turned_s[1][:, k, :],
              lambda c, b=b: k_t[:, 4 * b + c, :]) for b in range(2)]
            + [([("w_mv_2", l, b)], "rows", [2, 3], normed, lambda t, b=b: v_m[:, t - 2, 512 * b:512 * b + 512])
               for b in range(2)])

        @host[0].block.sync
        def _(sp):
            sp.wait_ge(*meeting.now())
            sp.dma_start(memory_kv[l], kept).then_inc(*stored.one(16))

    def small_work(l):
        z = soft[:, 176:224].rearrange("p (t h) -> p t h", t=2)
        e, r, s, acc = (soft[:, 224 + 48 * i:272 + 48 * i].rearrange("p (t h) -> p t h", t=2) for i in range(4))
        a_row = soft[:, 416:432]
        cw, cb = where["conv_w_2"][0] + 48 * l, where["conv_b_2"][0] + 12 * l
        tanh = [heads[:, 256 * i:256 * i + 256] for i in range(4)]
        rotate = rotate_work(l, [0, 1], lambda t: proj2[:, t, 0:640], cos2, sin2, 1, False)

        def bc(v, n):
            return v.unsqueeze(1).broadcast_to([P, 2, n])

        def vector(dve, banks, products_before):
            def step(ins):
                chain(dve, step_v, ins)
            dve.wait_ge(*ready_a.at(1))
            step(dve.tensor_scalar(a_row, a_row, -1.0, None, ALU.mult))
            step(dve.tensor_tensor(out=z[:, :, 0:8], in0=proj2[:, :, 2816:2824], in1=bc(forget_bias[l], 8), op=ALU.add))
            step(dve.tensor_scalar(z[:, :, 0:8], z[:, :, 0:8], -1.0, None, ALU.mult))
            step(dve.tensor_tensor(out=z[:, :, 8:24], in0=dt_raw, in1=bc(dt_bias[l], 16), op=ALU.add))
            step(dve.tensor_scalar(r, z, -1.0, None, ALU.mult))
            dve.tensor_tensor(out=e, in0=z, in1=r, op=ALU.min).then_inc(*ready_v.one())
            dve.wait_ge(*ready_a.at(2))
            step(dve.tensor_scalar(r, e, 2.0, None, ALU.add))
            step(dve.reciprocal(s, r))
            step(dve.tensor_tensor(out=r, in0=e, in1=s, op=ALU.mult))
            step(dve.tensor_tensor(out=s, in0=r, in1=r, op=ALU.mult))
            step(dve.tensor_scalar(acc, s, 1.0 / 19, None, ALU.mult))
            for odd in (17, 15, 13, 11, 9, 7, 5, 3):
                step(dve.scalar_tensor_tensor(out=acc, in0=acc, scalar=1.0 / odd, in1=s, op0=ALU.add, op1=ALU.mult))
            step(dve.scalar_tensor_tensor(out=acc, in0=acc, scalar=1.0, in1=r, op0=ALU.add, op1=ALU.mult))
            step(dve.tensor_scalar(acc, acc, 2.0, None, ALU.mult))
            step(dve.scalar_tensor_tensor(out=softened, in0=z, scalar=0.0, in1=acc, op0=ALU.max, op1=ALU.add))
            step(dve.tensor_scalar(z[:, :, 0:8], softened[:, :, 0:8], -1.0, None, ALU.mult))
            dve.tensor_tensor(out=decays, in0=softened[:, :, 8:24], in1=bc(a_row, 16), op=ALU.mult).then_inc(*ready_v.one())
            step(dve.memset(tables[:, 2304:2816], 0.0))
            step(dve.memset(raw_conv[:, :, 0:3], 0.0))
            for c in range(12):
                dst = conv[:, c, :]
                step(dve.tensor_scalar(dst, raw_conv[:, c, 0:256], columns[:, cw + c:cw + c + 1],
                                       columns[:, cb + c:cb + c + 1], ALU.mult, ALU.add))
                for k in range(1, 4):
                    ins = dve.scalar_tensor_tensor(out=dst, in0=raw_conv[:, c, k:k + 256],
                                                   scalar=columns[:, cw + 12 * k + c:cw + 12 * k + c + 1],
                                                   in1=dst, op0=ALU.mult, op1=ALU.add)
                    if k < 3:
                        step(ins)
                ins.then_inc(*ready_v.one())
                if c >= 2:
                    finish(dve, c - 2)
            finish(dve, 10)
            finish(dve, 11)
            for _ in rotate(dve):
                pass
            dve.wait_ge(*products.at(products_before + 1))
            step(dve.tensor_copy(cum_f, psum[:, banks[0], 0:16].rearrange("p (t h) -> p t h", t=2)))
            step(dve.tensor_scalar(neg_acs, psum[:, banks[1], 0:32].rearrange("p (t h) -> p t h", t=2), -1.0, None, ALU.mult))
            dve.tensor_copy(fallen_rows[0:8, :], psum[0:8, banks[0], 256:512]).then_inc(*step_v.one())
            dve.tensor_copy(acs_rows[0:16, :], psum[0:16, banks[1], 256:512]).then_inc(*step_v.one())

        def finish(dve, c):
            dve.wait_ge(*ready_a.at(2 + c + 1))
            dve.wait_ge(*ready_v.at(2 + c + 1))
            dve.scalar_tensor_tensor(out=conv[:, c, :], in0=tanh[c % 4], scalar=1.0, in1=conv[:, c, :],
                                     op0=ALU.add, op1=ALU.mult).then_inc(*read_v.one())

        def scalar(act):
            act.activation(a_row, a_log[l], ACT.Exp).then_inc(*ready_a.one())
            act.wait_ge(*ready_v.at(1))
            act.activation(e, e, ACT.Exp).then_inc(*ready_a.one())
            yield
            for c in range(12):
                act.wait_ge(*ready_v.at(2 + c + 1))
                if c >= 4:
                    act.wait_ge(*read_v.at(c - 3))
                act.activation(tanh[c % 4], conv[:, c, :], ACT.Tanh).then_inc(*ready_a.one())
                yield

        def tensor(pe, banks):
            pe.wait_ge(*ready_v.at(2))
            for bank, src, n in ((banks[0], z[:, :, 0:8], 8), (banks[1], decays, 16)):
                for t in range(2):
                    for k in range(2):
                        pe.matmul(psum[:, bank, n * t:n * t + n], upper[:, k, t * P:t * P + P], src[:, k, :],
                                  start=k == 0, stop=k == 1)
            for bank, src, n in ((banks[0], softened[:, :, 0:8], 8), (banks[1], decays, 16)):
                for k in range(2):
                    mm = pe.matmul(psum[0:n, bank, 256:512], src[:, k, :], upper[:, k, :], start=k == 0, stop=k == 1)
            mm.then_inc(*products.one())

        return vector, scalar, tensor

    def second_attention(l):
        qa_t = heads[:, 0:1024].rearrange("p (c t) -> p c t", c=4)
        ka_t = heads[:, 1024:1280]
        qb_t = heads[:, 1280:2304].rearrange("p (c t) -> p c t", c=4)
        kb_t = heads[:, 2304:3328].rearrange("p (c t) -> p c t", c=4)
        groups = []
        for t in range(2):
            span = slice(t * P, t * P + P)
            groups.append(([mixed_v[:, t, c * P:c * P + P] for c in range(4)], [(0, 512, qa_t[:, :, span], HD ** -0.5)]))
            groups.append(([mixed_v[:, t, 512:640]], [(0, 128, ka_t[:, span], 1.0)]))
            groups.append(([proj2[:, t, 1280 + c * P:1408 + c * P] for c in range(4)], [(0, 512, qb_t[:, :, span], HD ** -0.5)]))
            groups.append(([proj2[:, t, 1792 + c * P:1920 + c * P] for c in range(4)], [(0, 512, kb_t[:, :, span], 1.0)]))
        turn_stage(groups)
        units = []
        for t in range(2):
            seen = P * (t + 1)
            for half in range(2):
                for c in range(4):
                    rows = slice(64 * half, 64 * half + 64)
                    h = 4 * half + c
                    units.append(dict(
                        keys=seen, scores=[(qa_t[rows, c, t * P:t * P + P], ka_t[rows, 0:seen])], mask=band[:, t, 0:seen],
                        sink=sinks[l][:, h:h + 1],
                        outputs=[dict(values=lambda k, half=half: proj2[:, k, 640 + 64 * half:704 + 64 * half],
                                      p0=0, np=128, c0=0, w=64, turned=False, dst=y_v[:, t, h * 64:h * 64 + 64])]))
        for t in range(2):
            seen = P * (t + 1)
            for h in range(8):
                rows = slice(64 * (h % 2), 64 * (h % 2) + 64)
                scores = [(qb_t[rows, h // 2, t * P:t * P + P], kb_t[rows, h // 2, 0:seen])]
                scores.append((ident[:, h:h + 1].broadcast_to([P, P]), fallen_rows[:, 0:seen]))
                units.append(dict(
                    keys=seen, scores=scores, mask=causal[:, t, 0:seen], shift=cum_f[:, t, h:h + 1],
                    outputs=[dict(values=lambda k, h=h: proj2[:, k, 2304 + 64 * h:2368 + 64 * h],
                                  p0=0, np=128, c0=0, w=64, turned=False, dst=y_v[:, t, 512 + h * 64:576 + h * 64])]))
        attention_stage(units, turned[:, 0:1792], 256)

    x_rows = turned[:, 0:2048].rearrange("p (t d) -> p t d", t=2)
    x_dt = turned[:, 2048:4096].rearrange("p (t d) -> p t d", t=2)

    def ssm_stage(l):
        open_stage()
        cb = heads[:, 0:768].rearrange("p (g n) -> p g n", g=2)
        decay = [heads[:, 768 + 384 * i:1152 + 384 * i] for i in range(2)]
        kernel_ = [heads[:, 1536 + 384 * i:1920 + 384 * i] for i in range(2)]

        def tensor(pe):
            for g in range(2):
                pe.matmul(psum[:, g, 0:256], conv[:, 8 + g, 0:128], conv[:, 10 + g, :], start=True, stop=True)
                pe.matmul(psum[:, g, 256:384], conv[:, 8 + g, 128:256], conv[:, 10 + g, 128:256],
                          start=True, stop=True).then_inc(*products.one())
            for h in range(17):
                if h < 16:
                    bank = 2 + h % 2
                    if h >= 2:
                        pe.wait_ge(*ready_a.at(h - 1))
                    head_row = ident[:, h:h + 1].broadcast_to([P, P])
                    for o, l0, n, s in ((0, 0, 128, 0), (128, 128, 128, None), (256, 128, 128, 1)):
                        mm = pe.matmul(psum[:, bank, o:o + n], head_row, acs_rows[:, l0:l0 + n], start=True, stop=s is None)
                        if s is not None:
                            mm = pe.matmul(psum[:, bank, o:o + n], ident, causal_t[:, s, l0:l0 + n], start=False, stop=True)
                    mm.then_inc(*products.one())
                if h >= 1:
                    j = h - 1
                    m = kernel_[j % 2]
                    pe.wait_ge(*ready_v.at(j + 1))
                    if j >= 2:
                        pe.wait_ge(*read_v.at(2 + j - 1))
                    xs = [x_dt[:, t, j * 64:j * 64 + 64] for t in range(2)]
                    bank = 4 + j % 2
                    pe.matmul(psum[:, bank, 0:64], m[:, 0:128], xs[0], start=True, stop=True)
                    pe.matmul(psum[:, bank, 64:128], m[:, 128:256], xs[0], start=True, stop=False)
                    pe.matmul(psum[:, bank, 64:128], m[:, 256:384], xs[1], start=False, stop=True).then_inc(*products.one())

        def vector(dve):
            chain(dve, step_v, dve.tensor_tensor(
                out=x_dt.rearrange("p t (h d) -> p t h d", d=64), in0=x_rows.rearrange("p t (h d) -> p t h d", d=64),
                in1=softened[:, :, 8:24].unsqueeze(3).broadcast_to([P, 2, 16, 64]), op=ALU.mult))
            for g in range(2):
                dve.wait_ge(*products.at(g + 1))
                dve.tensor_copy(cb[:, g, :], psum[:, g, 0:384]).then_inc(*read_v.one())
            dve.wait_ge(*read_v.now())
            for h in range(17):
                if h < 16:
                    dve.wait_ge(*ready_a.at(h + 1))
                    if h >= 2:
                        dve.wait_ge(*products.at(2 + 2 * (h - 2) + 3))
                    dve.tensor_tensor(out=kernel_[h % 2], in0=decay[h % 2], in1=cb[:, h // 8, :], op=ALU.mult)\
                       .then_inc(*ready_v.one())
                if h >= 1:
                    j = h - 1
                    dve.wait_ge(*products.at(2 + (2 * j + 3 if j < 15 else 32)))
                    for t in range(2):
                        ins = dve.scalar_tensor_tensor(
                            out=y_v[:, t, 1024 + j * 64:1088 + j * 64], in0=x_rows[:, t, j * 64:j * 64 + 64],
                            scalar=d_skip[l][:, j:j + 1], in1=psum[:, 4 + j % 2, 64 * t:64 * t + 64],
                            op0=ALU.mult, op1=ALU.add)
                    ins.then_inc(*read_v.one())
                if 2 <= h < 10:
                    gate(dve, h - 2)

        def gate_piece(j):
            t, i = divmod(j, 4)
            g0 = 768 if i == 0 else 2312 + 512 * i
            return t, i, y_v[:, t, 512 * i:512 * i + 512], proj2[:, t, g0:g0 + 512], silu_gates[:, t, 512 * i:512 * i + 512]

        def gate(dve, j):
            t, i, y, g, th = gate_piece(j)
            dve.wait_ge(*step_a.at(j + 1))
            chain(dve, step_v, dve.scalar_tensor_tensor(out=th, in0=th, scalar=1.0, in1=g, op0=ALU.add, op1=ALU.mult))
            if i < 2:
                dve.scalar_tensor_tensor(out=y, in0=th, scalar=HALVED, in1=y, op0=ALU.mult, op1=ALU.mult)\
                   .then_inc(*step_v.one())

        def scalar(act):
            for h in range(16):
                if h < 8:
                    _, _, _, g, th = gate_piece(h)
                    act.activation(th, g, ACT.Tanh, scale=0.5).then_inc(*step_a.one())
                act.wait_ge(*products.at(2 + (1 if h == 0 else 2 * h)))
                if h >= 2:
                    act.wait_ge(*ready_v.at(h - 1))
                for o, n, s in ((0, 256, 0), (256, 128, 1)):
                    ins = act.activation(decay[h % 2][:, o:o + n], psum[:, 2 + h % 2, o:o + n], ACT.Exp,
                                         bias=neg_acs[:, s, h:h + 1])
                ins.then_inc(*ready_a.one())

        run_stage(tensor, vector, scalar)

    def gating_stage():
        open_stage()
        squares = turned.rearrange("p (t d) -> p t d", t=2)

        def scalar(act):
            for t in range(2):
                act.wait_ge(*ready_v.at(t + 1))
                act.activation(squares[:, t, 0:1024], y_v[:, t, 1024:2048], ACT.Square,
                               accum_out=stats[:, t:t + 1]).then_inc(*ready_a.one())

        def vector(dve):
            for t in range(2):
                y = y_v[:, t, 1024:2048]
                dve.scalar_tensor_tensor(out=y, in0=silu_gates[:, t, 1024:2048], scalar=HALVED, in1=y,
                                         op0=ALU.mult, op1=ALU.mult).then_inc(*ready_v.one())
            dve.wait_ge(*ready_a.at(2))
            inverse_root(dve, stats[:, 16:18], stats[:, 0:2], stats[:, 32:38], DM)
            for t in range(2):
                dve.tensor_scalar(y_v[:, t, 1024:2048], y_v[:, t, 1024:2048], stats[:, 16 + t:17 + t], None,
                                  ALU.mult).then_inc(*step_v.one())

        run_stage(vector=vector, scalar=scalar)

    def second_layer(l):
        norm_stage([0, 1], lambda k, t: column("norm_mix_w_2", 8 * l + k), None)
        def token_jobs(blocks):
            return [([("w_in2", l, b)], "rows", [0, 1], normed,
                     lambda t, b=b: proj2[:, t, 512 * b:min(512 * b + 512, W2_TOKEN_COLS)]) for b in blocks]

        linear_stage([([("conv", l, b)], "cols", [0, 1, 2, 3], lambda k, _: turned_s[0][:, k, :],
                       lambda c, b=b: raw_conv[:, 4 * b + c, 3:259]) for b in range(3)]
                     + [([("dt", l)], "rows", [0, 1], normed, lambda t: dt_raw[:, t, :])] + token_jobs(W2_FIRST))
        linear_stage(token_jobs(W2_REST), small_work(l))
        second_attention(l)
        turn_stage([([conv[:, 4 * g + q, t * P:t * P + P] for q in range(4)],
                     [(0, 512, x_rows[:, t, 512 * g:512 * g + 512], 1.0)]) for t in range(2) for g in range(2)])
        ssm_stage(l)
        gating_stage()
        y_t = lifted.rearrange("p (k t) -> p k t", k=16)
        groups = []
        for t in range(2):
            for g in range(4):
                srcs = [y_v[:, t, (4 * g + q) * P:(4 * g + q + 1) * P] for q in range(4)]
                if g < 2:
                    outs = [(0, 512, y_t[:, 4 * g:4 * g + 4, t * P:t * P + P], 1.0)]
                else:
                    outs = [(q * P, P, y_t[:, 4 * g + q, t * P:t * P + P], column("ssm_norm_w_2", 8 * l + 4 * (g - 2) + q))
                            for q in range(4)]
                groups.append((srcs, outs))
        turn_stage(groups)
        linear_stage([([("w_out2", l, b, 0), ("w_out2", l, b, 1)], "rows", [0, 1],
                       lambda k, t: y_t[:, k, t * P:t * P + P], ("add", None, 512 * b)) for b in range(2)])
        q_t = lifted[:, 2048:4096].rearrange("p (c t) -> p c t", c=8)
        kept = heads.rearrange("p (j n) -> p j n", j=2)
        k_t = kept[:, 0, :].rearrange("p (c t) -> p c t", c=8)
        v_m = kept[:, 1, :].rearrange("p (t n) -> p t n", t=2)
        o_t = lifted[:, 0:2048].rearrange("p (c t) -> p c t", c=8)
        norm_stage([0, 1], lambda k, t: column("norm_xq_w_2", 8 * l + k), None,
                   sync=lambda sp: sp.dma_start(kept, memory_kv[l]).then_inc(*loaded.one(16)))
        linear_stage([([("w_mq_2", l, b)], "cols", [0, 1, 2, 3], lambda k, _: turned_s[0][:, k, :],
                       lambda c, b=b: (q_t[:, 4 * b + c, :], 256 ** -0.5)) for b in range(2)],
                     sync=lambda sp: sp.wait_ge(*loaded.now()))
        units = []
        for t in range(2):
            for h in range(4):
                units.append(dict(
                    keys=256, scores=[(q_t[:, 2 * h + j, t * P:t * P + P], k_t[:, 2 * h + j, :]) for j in range(2)],
                    outputs=[dict(values=lambda k, c=2 * h + j: v_m[:, k, c * P:c * P + P],
                                  p0=0, np=128, c0=128 * j, w=128, turned=True, dst=o_t[:, 2 * h + j, t * P:t * P + P])
                             for j in range(2)]))
        attention_stage(units, turned[:, 0:1792], 256)
        linear_stage([([("w_mo_2", l, b)], "rows", [0, 1], lambda k, t: o_t[:, k, t * P:t * P + P],
                       ("add", None, 512 * b)) for b in range(2)])

    def final_stage():
        open_stage()
        gain = lifted[:, 0:DM]

        def sync(sp):
            sp.dma_start(gain, io["final_norm_w_2"].rearrange("(a d) -> a d", a=1).broadcast_to([P, DM]))\
              .then_inc(*loaded.one(16))
            for t in range(2):
                sp.wait_ge(*ready_v.at(t + 1))
                sp.dma_start(out[0, t * P:t * P + P, :], mixed_v[:, t, :]).then_inc(*stored.one(16))
            sp.wait_ge(*stored.now())

        def scalar(act):
            for t in range(2):
                act.activation(mixed_v[:, t, :], stream[:, t, :], ACT.Square,
                               accum_out=stats[:, t:t + 1]).then_inc(*ready_a.one())

        def vector(dve):
            dve.wait_ge(*ready_a.at(2))
            inverse_root(dve, stats[:, 16:18], stats[:, 0:2], stats[:, 32:38], DM)
            dve.wait_ge(*loaded.at(16))
            for t in range(2):
                dve.scalar_tensor_tensor(out=mixed_v[:, t, :], in0=stream[:, t, :], scalar=stats[:, 16 + t:17 + t],
                                         in1=gain, op0=ALU.mult, op1=ALU.mult).then_inc(*ready_v.one())

        run_stage(vector=vector, scalar=scalar, sync=sync)

    first_block()
    for l in range(DEPTH):
        second_layer(l)
    final_stage()


_INS = ['x', 'c', 'ctx', 'c_ctx', 'ada_w', 'ada_b', 'norm_mix', 'w_in', 'fourier_w', 'pool_w', 'pool_scale',
        'pool_proj', 'q_norm', 'k_norm', 'attn_proj', 'w_out', 'norm_ffn', 'peer_wq', 'peer_keys', 'peer_u', 'peer_v',
        'mem_2', 'norm_mix_w_2', 'w_in_2', 'b_forget_2', 'swa_sinks_2', 'conv_w_2', 'conv_b_2', 'dt_bias_2',
        'a_log_2', 'd_skip_2', 'ssm_norm_w_2', 'w_out_2', 'norm_xq_w_2', 'norm_mem_w_2', 'w_mq_2', 'w_mk_2',
        'w_mv_2', 'w_mo_2', 'final_norm_w_2']
_OUTS = [((1, 256, 1024), 'float32')]


def kernel(**inputs):
    import numpy as _np
    import concourse.bacc as _bacc
    from concourse import mybir as _mybir
    from concourse.bass_utils import run_bass_kernel_spmd as _run

    nc = _bacc.Bacc("TRN2", target_bir_lowering=False, num_devices=1)
    arrays, io = {}, {}
    named = {name: inputs[name] for name in _INS}
    named.update(zip(("common", "first", "second"), shape_constants()))
    for name, a in named.items():
        a = _np.ascontiguousarray(a)
        arrays[f"in_{name}_dram"] = a
        io[name] = nc.dram_tensor(f"in_{name}_dram", a.shape, _mybir.dt.from_np(a.dtype), kind="ExternalInput").ap()
    outs = [nc.dram_tensor(f"out_{i}_dram", shape, _mybir.dt.from_np(_np.dtype(dtype)), kind="ExternalOutput").ap()
            for i, (shape, dtype) in enumerate(_OUTS)]
    build_kernel(nc, io, outs[0])
    r = _run(nc, [arrays], core_ids=[0])
    return r.results[0]["out_0_dram"]
```
